# Optimizing a Trainium2 kernel written in Bass

```python
import jax, jax.numpy as jnp
from jax import lax
import numpy as np

D_MODEL = 1024
BATCH = 1
SEQ = 1024
DEPTH = 1
DEC_BATCH = 1
DEC_SEQ = 256
PAST_LEN = 128

D_MIX = D_MODEL
HEAD_DIM = 64
D_ATTN = D_MIX // 2
N_HEADS = D_ATTN // HEAD_DIM
N_KV_HEADS = 2
Q_PER_KV = N_HEADS // N_KV_HEADS
D_KV = N_KV_HEADS * HEAD_DIM
D_CONV = D_MIX - D_ATTN
CONV_WIDTH = 31
CONV_PAD = CONV_WIDTH // 2
D_IN = D_ATTN + 2 * D_KV + 2 * D_CONV
N_EXPERTS = 16
CAPACITY_FACTOR = 2
D_EXPERT = D_MODEL
GRID_W = 64
ROPE_THETA = 10000.0
ROPE_AXIS_DIM = HEAD_DIM // 2
Q_BLOCK = 128
EPS = 1e-6

kernel_name = "hybrid_conformer_axialgqa_ec_moe_encoder"

def rms_norm(x, g):
    xf = x.astype(jnp.float32)
    y = xf * lax.rsqrt(jnp.mean(xf * xf, axis=-1, keepdims=True) + EPS)
    return (y * g.astype(jnp.float32)).astype(x.dtype)

def layer_norm(x, g, b):
    xf = x.astype(jnp.float32)
    mu = jnp.mean(xf, axis=-1, keepdims=True)
    xc = xf - mu
    y = xc * lax.rsqrt(jnp.mean(xc * xc, axis=-1, keepdims=True) + EPS)
    return (y * g.astype(jnp.float32) + b.astype(jnp.float32)).astype(x.dtype)

def axial_rope_tables(s):
    n_rows = s // GRID_W
    rr, cc = jnp.meshgrid(jnp.arange(n_rows), jnp.arange(GRID_W), indexing='ij')
    row = rr.reshape(-1).astype(jnp.float32)
    col = cc.reshape(-1).astype(jnp.float32)
    inv = ROPE_THETA ** (-jnp.arange(0, ROPE_AXIS_DIM, 2, dtype=jnp.float32) / ROPE_AXIS_DIM)
    ang = jnp.concatenate([row[:, None] * inv, col[:, None] * inv], axis=-1)
    return jnp.cos(ang), jnp.sin(ang)

def apply_rope(x, cos, sin):
    xf = x.astype(jnp.float32)
    x1, x2 = xf[..., 0::2], xf[..., 1::2]
    c, s_ = cos[None, :, None, :], sin[None, :, None, :]
    out = jnp.stack([x1 * c - x2 * s_, x1 * s_ + x2 * c], axis=-1)
    return out.reshape(x.shape).astype(x.dtype)

def blocked_gqa_attention(q, k, v):
    b, s, _, d = q.shape
    nb = s // Q_BLOCK
    qb = q.reshape(b, nb, Q_BLOCK, N_KV_HEADS, Q_PER_KV, d).transpose(1, 0, 2, 3, 4, 5)
    scale = HEAD_DIM ** -0.5

    def one_block(qblk):
        sc = jnp.einsum('bqkgd,bskd->bkgqs', qblk, k).astype(jnp.float32) * scale
        p = jax.nn.softmax(sc, axis=-1)
        return jnp.einsum('bkgqs,bskd->bqkgd', p.astype(v.dtype), v)

    o = lax.map(one_block, qb)
    return o.transpose(1, 0, 2, 3, 4, 5).reshape(b, s, N_HEADS * d)

def conformer_conv(u, conv_w, conv_b, ln_g, ln_b):
    val, gate = jnp.split(u, 2, axis=-1)
    a = val * jax.nn.sigmoid(gate)
    y = lax.conv_general_dilated(a, conv_w, window_strides=(1,), padding=((CONV_PAD, CONV_PAD),),
                                 dimension_numbers=('NWC', 'WIO', 'NWC'), feature_group_count=D_CONV)
    y = layer_norm(y + conv_b, ln_g, ln_b)
    return jax.nn.silu(y)

def expert_choice_ffn(h, w_router, w_gate, w_up, w_down):
    b, s, d = h.shape
    t = h.reshape(-1, d)
    n = t.shape[0]
    cap = CAPACITY_FACTOR * n // N_EXPERTS
    aff = jax.nn.softmax((t @ w_router).astype(jnp.float32), axis=-1)
    g, idx = lax.top_k(aff.T, cap)
    xe = t[idx]
    hid = jax.nn.silu(jnp.einsum('ecd,edf->ecf', xe, w_gate)) * jnp.einsum('ecd,edf->ecf', xe, w_up)
    ye = jnp.einsum('ecf,efd->ecd', hid, w_down) * g[..., None].astype(t.dtype)
    out = jnp.zeros_like(t).at[idx.reshape(-1)].add(ye.reshape(-1, d))
    return out.reshape(b, s, d)

def encoder_layer(x, c, ada_w, ada_b, norm_mix, w_in, q_norm, k_norm, conv_w, conv_b,
                  conv_ln_g, conv_ln_b, w_out, norm_ffn, w_router, w_gate, w_up, w_down):
    b, s, _ = x.shape
    mod = jax.nn.silu(c) @ ada_w + ada_b
    shift1, scale1, gate1, shift2, scale2, gate2 = [m[:, None, :] for m in jnp.split(mod, 6, axis=-1)]

    h = rms_norm(x, norm_mix) * (1 + scale1) + shift1
    z = h @ w_in
    q, k, v, u = jnp.split(z, [D_ATTN, D_ATTN + D_KV, D_ATTN + 2 * D_KV], axis=-1)
    cos, sin = axial_rope_tables(s)
    q = apply_rope(rms_norm(q.reshape(b, s, N_HEADS, HEAD_DIM), q_norm), cos, sin)
    k = apply_rope(rms_norm(k.reshape(b, s, N_KV_HEADS, HEAD_DIM), k_norm), cos, sin)
    v = v.reshape(b, s, N_KV_HEADS, HEAD_DIM)
    attn_out = blocked_gqa_attention(q, k, v)
    conv_out = conformer_conv(u, conv_w, conv_b, conv_ln_g, conv_ln_b)
    mix = jnp.concatenate([attn_out, conv_out], axis=-1) @ w_out
    x = x + gate1 * mix

    h2 = rms_norm(x, norm_ffn) * (1 + scale2) + shift2
    x = x + gate2 * expert_choice_ffn(h2, w_router, w_gate, w_up, w_down)
    return x

def setup_inputs(seed: int = 0) -> dict:
    key = jax.random.key(seed)
    ks = jax.random.split(key, 24)
    f32 = jnp.float32
    nrm = lambda k, shape, sc: jax.random.normal(k, shape, f32) * sc
    D = D_MODEL
    return {
        "x_prompt": nrm(ks[0], (BATCH, SEQ, D), 1.0),
        "x_sample": nrm(ks[1], (DEC_BATCH, DEC_SEQ, D), 1.0),
        "c_prompt": nrm(ks[2], (BATCH, D), 1.0),
        "c_sample": nrm(ks[3], (DEC_BATCH, D), 1.0),
        "ada_w": nrm(ks[4], (DEPTH, D, 6 * D), 0.5 * D ** -0.5),
        "ada_b": nrm(ks[5], (DEPTH, 6 * D), 0.02),
        "norm_mix": 1.0 + nrm(ks[6], (DEPTH, D), 0.05),
        "w_in": nrm(ks[7], (DEPTH, D, D_IN), D ** -0.5),
        "q_norm": 1.0 + nrm(ks[8], (DEPTH, HEAD_DIM), 0.05),
        "k_norm": 1.0 + nrm(ks[9], (DEPTH, HEAD_DIM), 0.05),
        "conv_w": nrm(ks[10], (DEPTH, CONV_WIDTH, 1, D_CONV), CONV_WIDTH ** -0.5),
        "conv_b": nrm(ks[11], (DEPTH, D_CONV), 0.02),
        "conv_ln_g": 1.0 + nrm(ks[12], (DEPTH, D_CONV), 0.05),
        "conv_ln_b": nrm(ks[13], (DEPTH, D_CONV), 0.02),
        "w_out": nrm(ks[14], (DEPTH, D_MIX, D), D_MIX ** -0.5),
        "norm_ffn": 1.0 + nrm(ks[15], (DEPTH, D), 0.05),
        "w_router": nrm(ks[16], (DEPTH, D, N_EXPERTS), D ** -0.5),
        "w_gate": nrm(ks[17], (DEPTH, N_EXPERTS, D, D_EXPERT), D ** -0.5),
        "w_up": nrm(ks[18], (DEPTH, N_EXPERTS, D, D_EXPERT), D ** -0.5),
        "w_down": nrm(ks[19], (DEPTH, N_EXPERTS, D_EXPERT, D), D_EXPERT ** -0.5),
    }

def reference(x_prompt, x_sample, c_prompt, c_sample, ada_w, ada_b, norm_mix, w_in, q_norm, k_norm,
              conv_w, conv_b, conv_ln_g, conv_ln_b, w_out, norm_ffn, w_router, w_gate, w_up, w_down):
    y_prompt = x_prompt
    y_sample = x_sample
    for l in range(DEPTH):
        p = (ada_w[l], ada_b[l], norm_mix[l], w_in[l], q_norm[l], k_norm[l], conv_w[l], conv_b[l],
             conv_ln_g[l], conv_ln_b[l], w_out[l], norm_ffn[l], w_router[l], w_gate[l], w_up[l], w_down[l])
        y_prompt = encoder_layer(y_prompt, c_prompt, *p)
        y_sample = encoder_layer(y_sample, c_sample, *p)
    return (y_prompt, y_sample)


_drawn_inputs = setup_inputs


def setup_inputs(seed=0):
    import zlib

    import numpy as np

    out = dict(_drawn_inputs(seed))
    spreads = {}
    factors = {'ada_b': 3.94,
     'norm_mix': 6.786,
     'q_norm': 8.0,
     'k_norm': 8.0,
     'conv_b': 8.0,
     'conv_ln_g': 7.046,
     'conv_ln_b': 8.0,
     'norm_ffn': 5.212}
    for name, (base, spread) in spreads.items():
        noise = np.random.default_rng([zlib.crc32(name.encode()), seed]).standard_normal(out[name].shape)
        drawn = base * np.exp(spread * noise) if base else spread * noise
        out[name] = __import__('jax').numpy.asarray(drawn.astype(out[name].dtype))
    for name, factor in factors.items():
        out[name] = (out[name] * factor).astype(out[name].dtype)
    return out
```

```python
from contextlib import ExitStack

import numpy as np

import concourse.bass as bass
from concourse import mybir

F32 = mybir.dt.float32
F32R = mybir.dt.float32r
U32 = mybir.dt.uint32
ACT = mybir.ActivationFunctionType
ALU = mybir.AluOpType
AX = mybir.AxisListType

P = 128
D = 1024
KC = D // P
SP_TOK, SS_TOK = 1024, 256
TOK = SP_TOK + SS_TOK
NT = TOK // P
NPAIR = NT // 2
HD = 64
NH = 8
NKV = 2
QPK = NH // NKV
DA = NH * HD
DKV = NKV * HD
DC = D - DA
CC = DC // P
TAPS = 31
PAD = TAPS // 2
D_IN = DA + 2 * DKV + 2 * DC
NQKV = DA + 2 * DKV
NE = 16
CAP_P = 2 * SP_TOK // NE
CAP_S = 2 * SS_TOK // NE
CAP = CAP_P + CAP_S
EPS = 1e-6
LOWEST = -1.0

A_PROMPT = PAD
A_SAMPLE = PAD + SP_TOK + 2 * PAD
A_LEN = A_SAMPLE + SS_TOK + PAD
A_ROW = A_LEN + 4
C_SAMPLE = SP_TOK + 2 * PAD
C_LEN = C_SAMPLE + SS_TOK
TAPS_FIRST = 7
TAPS_STEP = (TAPS - TAPS_FIRST) // (SP_TOK // P)

SHIFT1, SCALE1, GATE1, SHIFT2, SCALE2, GATE2 = (i * KC for i in range(6))
ADA_BLOCK = 512
ADA_FIRST = 2 * D // ADA_BLOCK
ADA_BLOCKS = 6 * D // ADA_BLOCK

ROW_C, ROW_NMIX, ROW_NFFN, ROW_CB, ROW_LG, ROW_LB, ROW_AB = 0, 16, 24, 32, 36, 40, 44
ROWS = ROW_AB + 48


def encoder_layer(nc, x_p, x_s, c_p, c_s, ada_w, ada_b, norm_mix, w_in, q_norm, k_norm, conv_w, conv_b,
                  ln_g, ln_b, w_out, norm_ffn, w_router, w_gate, w_up, w_down, rope_cos, rope_sin,
                  y_p, y_s):
    xn_p = nc.dram_tensor("xn_prompt", (SP_TOK, D), F32).ap()
    xn_s = nc.dram_tensor("xn_sample", (SS_TOK, D), F32).ap()

    base = 16512
    small = base
    Z1 = small + 16384
    Z2 = Z1 + 81920
    Z3 = Z2 + 93184
    at = {"small": small}

    def put(name, shape, dt, offset):
        return nc.alloc_sbuf_tensor_at(name, shape, dt, offset=offset)

    def keep(name, shape, dt=F32):
        n = int(np.prod(shape[1:])) * 4
        t = put(name, shape, dt, at["small"])
        at["small"] += (n + 31) // 32 * 32
        assert at["small"] <= Z1
        return t

    ident = keep("ident", [P, P])
    ones = keep("ones", [P, P])
    cols = keep("cols", [P, ROWS])
    taps = keep("taps", [P, CC, TAPS])
    silu_c = keep("silu_c", [P, 2 * KC])
    mod = keep("mod", [P, 6 * KC, 2])
    a1 = keep("a1", [P, KC, 2])
    a2 = keep("a2", [P, KC, 2])
    ss_x = keep("ss_x", [P, 2])
    rt_x = keep("rt_x", [P, 2])
    rs_x = keep("rs_x", [P, 2])
    ss_q = keep("ss_q", [P, 2, 10])
    rt_q = keep("rt_q", [P, 2, 10])
    rs_q = keep("rs_q", [P, 2, 10])
    negmax = keep("negmax", [P, 4])
    router = keep("router", [P, KC, NE])
    eps_col = keep("eps_col", [P, 1])
    g_top_p = keep("g_top_p", [P, NE + 1])
    g_top_s = keep("g_top_s", [P, NE + 1])
    i_top_p = keep("i_top_p", [P, NE + 1], U32)
    i_top_s = keep("i_top_s", [P, NE + 1], U32)
    i_now = keep("i_now", [P, 4], U32)
    smx = keep("smx", [P, 3, NT])
    mod_rows = keep("mod_rows", [2, 2, ADA_BLOCK])
    rope_c = put("rope_c", [P, 8, 2, HD], F32, at["small"])
    rope_s = put("rope_s", [P, 8, 2, HD], F32, at["small"] + 4096)
    gate1_row = put("gate1_row", [P, 2, D], F32, at["small"])
    assert at["small"] + 8192 <= Z1, at["small"] + 8192 - Z1

    x_in = put("x_in", [P, 2, D], F32, Z1)
    h_t = put("h_t", [P, 2, KC, 2 * P], F32, Z1 + 8192)
    w_in_sb = put("w_in_sb", [P, KC, D_IN], F32, Z1 + 24576)
    ada = [put(f"ada{i}", [P, KC, ADA_BLOCK], F32, Z2 + 16384 * i) for i in range(3)]
    rows = put("rows", [ROWS, P], F32, Z3)
    taps_row = put("taps_row", [TAPS, DC], F32, Z3 + 512)
    gains = put("gains", [P, 2, HD], F32, Z3 + 2560)
    ngains = put("ngains", [P, 2, HD], F32, Z3 + 3072)
    cos_sb = put("cos_sb", [P, 8, HD // 2], F32, Z1 + 16384)
    sin_sb = put("sin_sb", [P, 8, HD // 2], F32, Z1 + 17408)
    q_st = put("q_st", [P, NT, NH, P], F32R, Z2)
    k_hi = put("k_hi", [P, NKV, TOK], F32R, Z2 + 40960)
    k_lo = put("k_lo", [P, NKV, TOK], F32R, Z2 + 51200)
    v_one = put("v_one", [P, NT, NKV, P], F32, Z2 + 61440)
    a_t = put("a_t", [P, CC, A_ROW], F32, Z2 + 71680)
    junk = put("junk", [P, D], F32, Z3 + 4096)
    qk = [put(f"qk{i}", [P, 10, HD], F32, Z3 + 8192 + 2560 * i) for i in range(2)]
    sq = put("sq", [P, 10, HD], F32, Z3 + 13312)
    rot1 = sq
    rot2 = put("rot2", [P, 10, HD], F32, Z3 + 15872)
    sig = put("sig", [P, 2, 2 * P], F32, Z3 + 18432)
    ada2 = [put(f"ada2_{i}", [P, KC, ADA_BLOCK], F32, Z1 + 32768 + 16384 * i) for i in range(3)]
    diag = put("diag", [P, 2, 4, P], F32, Z1 + 32768)
    c_t = put("c_t", [P, CC, C_LEN], F32, Z3)
    w_out_sb = put("w_out_sb", [P, KC, D], F32, Z1)
    probs = put("probs", [P, 2, SP_TOK], F32, Z1 + 32768)
    probs_t = put("probs_t", [P, KC, QPK, P], F32, Z1 + 40960)
    mix_t = put("mix_t", [P, CC, TOK], F32, Z1 + 57344)
    q_now = put("q_now", [P, 2, P], F32R, Z1 + 77824)
    rsum = put("rsum", [HD, QPK, P], F32, Z1 + 78848)
    sq_c = put("sq_c", [P, CC, 512], F32, Z1 + 32768)
    rt_c = put("rt_c", [P, 512], F32, Z1 + 40960)
    rs_c = put("rs_c", [P, 512], F32, Z1 + 43008)
    x_again = put("x_again", [P, 2, D], F32, Z1 + 32768)
    x1 = put("x1", [P, 2, D], F32, Z1 + 40960)
    xn2 = put("xn2", [P, 2, D], F32, Z1 + 49152)
    h2_t = put("h2_t", [P, 2, KC, 2 * P], F32, Z2 + 65536)
    logits_t = put("logits_t", [NE, TOK], F32, Z2 + 81920)
    aff = put("aff", [P, NT, NE], F32, Z3)
    aff_p = put("aff_p", [NE, SP_TOK], F32, Z3 + 1024)
    aff_s = put("aff_s", [NE, SS_TOK], F32, Z3 + 5120)
    top_p = put("top_p", [NE, 2, CAP_P], F32, Z3 + 6144)
    top_s = put("top_s", [NE, 2, CAP_S], F32, Z3 + 7168)
    idx_p = put("idx_p", [NE, CAP_P], U32, Z3 + 7680)
    idx_s = put("idx_s", [NE, CAP_S], U32, Z3 + 8192)
    MC = 256
    NS = D // MC
    gate_w_sb = put("gate_w_sb", [P, NS, KC, MC], F32, Z2)
    up_w_sb = put("up_w_sb", [P, NS, KC, MC], F32, Z2 + 32768)
    down_w_sb = put("down_w_sb", [P, NS, KC, MC], F32, Z1)
    xg_p = put("xg_p", [CAP_P, D], F32, Z1 + 32768)
    xg_s = put("xg_s", [CAP_S, D], F32, Z1 + 36864)
    ye_p = put("ye_p", [CAP_P, D], F32, Z1 + 40960)
    ye_s = put("ye_s", [CAP_S, D], F32, Z1 + 45056)
    xe_t = put("xe_t", [P, KC, CAP], F32, Z1 + 49152)
    hid = put("hid", [P, KC, CAP], F32, Z1 + 54272)
    y_t = put("y_t", [P, KC, CAP], F32, Z1 + 59392)
    sil = put("sil", [P, 2, CAP], F32, Z1 + 64512)

    with ExitStack() as ctx:
        two = [ctx.enter_context(nc.psum_tensor(f"banks{2 * i}", [P, 2, 512], F32)) for i in range(4)]

        def bank(k):
            return two[k // 2][:, k % 2, :]

        def sem(name):
            return ctx.enter_context(nc.semaphore(name))

        rows_loaded = sem("rows_loaded")
        gains_loaded = sem("gains_loaded")
        router_loaded = sem("router_loaded")
        ada_loaded = [sem(f"ada_loaded{i}") for i in range(3)]
        wu_loaded = sem("wu_loaded")
        wqkv_loaded = sem("wqkv_loaded")
        w_out_loaded = sem("w_out_loaded")
        x_loaded = sem("x_loaded")
        ident_made = sem("ident_made")
        fills_made = sem("fills_made")
        cols_turned = sem("cols_turned")
        cols_ready = sem("cols_ready")
        silu_ready = sem("silu_ready")
        rows_ready = sem("rows_ready")
        rows_copied = sem("rows_copied")
        rows_turned = sem("rows_turned")
        mod_turned = sem("mod_turned")
        mod_ready = sem("mod_ready")
        scale_ready = sem("scale_ready")
        gains_scaled = sem("gains_scaled")
        tables_ready = sem("tables_ready")
        x_squared = sem("x_squared")
        x_root = sem("x_root")
        x_recip = sem("x_recip")
        x_normed = sem("x_normed")
        t_ready = [sem(f"t_ready{i}") for i in range(2)]
        t_free = [sem(f"t_free{i}") for i in range(2)]
        u_ready = sem("u_ready")
        sig_ready = sem("sig_ready")
        u_gated = sem("u_gated")
        qkv_ready = sem("qkv_ready")
        qkv_copied = sem("qkv_copied")
        sq_ready = sem("sq_ready")
        sq_summed = sem("sq_summed")
        q_root = sem("q_root")
        q_recip = sem("q_recip")
        q_normed = sem("q_normed")
        rot1_ready = sem("rot1_ready")
        rot2_ready = sem("rot2_ready")
        rotated = sem("rotated")
        high_ready = sem("high_ready")
        diag_ready = sem("diag_ready")
        gate_rows_ready = sem("gate_rows_ready")
        gate_rows_copied = sem("gate_rows_copied")
        conv_done = [sem(f"conv_done{c}") for c in range(CC)]
        q_copied = sem("q_copied")
        scores_ready = sem("scores_ready")
        max_ready = sem("max_ready")
        probs_ready = sem("probs_ready")
        turned = sem("turned")
        turn_bank_free = sem("turn_bank_free")
        pv_ready = sem("pv_ready")
        sums_inverted = sem("sums_inverted")
        out_bank_free = sem("out_bank_free")
        mean_ready = sem("mean_ready")
        centred = sem("centred")
        squared = sem("squared")
        var_ready = sem("var_ready")
        root_ready = sem("root_ready")
        inv_ready = sem("inv_ready")
        scaled = sem("scaled")
        conv_out = sem("conv_out")
        x_reloaded = sem("x_reloaded")
        mix_ready = sem("mix_ready")
        mix_gated = sem("mix_gated")
        x1_ready = sem("x1_ready")
        x1_squared = sem("x1_squared")
        x1_root = sem("x1_root")
        x1_recip = sem("x1_recip")
        xn2_ready = sem("xn2_ready")
        y_stored = [sem(f"y_stored{a}") for a in range(2)]
        xn_stored = [sem(f"xn_stored{a}") for a in range(2)]
        t2_ready = [sem(f"t2_ready{i}") for i in range(2)]
        t2_free = [sem(f"t2_free{i}") for i in range(2)]
        logits_ready = sem("logits_ready")
        logits_copied = sem("logits_copied")
        logits_turned = sem("logits_turned")
        router_max = sem("router_max")
        router_shifted = sem("router_shifted")
        router_exp = sem("router_exp")
        router_sum = sem("router_sum")
        router_inv = sem("router_inv")
        aff_ready = sem("aff_ready")
        aff_turned = sem("aff_turned")
        aff_copied = sem("aff_copied")
        top_p_step = sem("top_p_step")
        top_s_step = sem("top_s_step")
        top_float = sem("top_float")
        top_turned = sem("top_turned")
        top_ready = sem("top_ready")
        gate_w_loaded = [sem(f"gate_w_loaded{i}") for i in range(NS)]
        up_w_loaded = [sem(f"up_w_loaded{i}") for i in range(NS)]
        down_w_loaded = [sem(f"down_w_loaded{i}") for i in range(NS)]
        idx_copied = sem("idx_copied")
        gathered = sem("gathered")
        gate_ready = sem("gate_ready")
        up_ready = sem("up_ready")
        silu_done = sem("silu_done")
        hid_ready = sem("hid_ready")
        d_ready = sem("d_ready")
        d_free = sem("d_free")
        y_turned = sem("y_turned")
        ye_ready = sem("ye_ready")
        scattered = sem("scattered")
        ye_free = sem("ye_free")
        act_steps = sem("act_steps")
        pool_steps = sem("pool_steps")

        turn_at = {}
        n_turns = [0]

        def order(key, uses):
            turn_at[key] = n_turns[0]
            n_turns[0] += uses

        order(("x", 0), 4)
        for p in range(NPAIR):
            if p:
                order(("q", p - 1, 1), 3)
            if p + 1 < NPAIR:
                order(("x", p + 1), 4)
            order(("q", p, 0), 3)
        order(("q", NPAIR - 1, 1), 3)

        def group(p):
            return 1 if p == NPAIR - 1 else 0

        def x_rows(p):
            src = x_s[0] if group(p) else x_p[0, 2 * P * p:2 * P * (p + 1), :]
            return src.rearrange("(a q) d -> q a d", q=P)

        def a_cols(p):
            return A_SAMPLE if group(p) else A_PROMPT + 2 * P * p

        def attention_phases():
            n = 0
            for j in range(NKV):
                for t0, nt in ((0, SP_TOK // P), (SP_TOK // P, SS_TOK // P)):
                    yield j, t0, nt, n
                    n += nt

        phases = list(attention_phases())
        STEPS = sum(ph[2] for ph in phases)
        HEADS_ALL = STEPS * QPK

        def conv_slices(c, k):
            return a_t[:, c, k:k + C_LEN]

        block = ctx.enter_context(nc.Block())

        @block.sync
        def _(sp):
            for r, src, n in ((ROW_C, c_p[0], KC), (ROW_C + KC, c_s[0], KC), (ROW_NMIX, norm_mix[0], KC),
                              (ROW_NFFN, norm_ffn[0], KC), (ROW_CB, conv_b[0], CC), (ROW_LG, ln_g[0], CC),
                              (ROW_LB, ln_b[0], CC), (ROW_AB, ada_b[0], 6 * KC)):
                sp.dma_start(rows[r:r + n, :], src.rearrange("(k q) -> k q", q=P)).then_inc(rows_loaded, 16)
            sp.dma_start(taps_row[:, :], conv_w[0, :, 0, :]).then_inc(rows_loaded, 16)
            sp.dma_start(x_in[:, :, :], x_rows(0)).then_inc(x_loaded, 16)
            ada_view = ada_w[0].rearrange("(k q) (b n) -> b q k n", q=P, n=ADA_BLOCK)
            for b in range(ADA_FIRST):
                if b >= 3:
                    sp.wait_ge(rows_ready, b - 2)
                sp.dma_start(ada[b % 3][:, :, :], ada_view[b]).then_inc(ada_loaded[b % 3], 16)
                if b == 0:
                    sp.dma_start(gains[:, 0, :], q_norm[0].partition_broadcast(P)).then_inc(gains_loaded, 16)
                    sp.dma_start(gains[:, 1, :], k_norm[0].partition_broadcast(P)).then_inc(gains_loaded, 16)
                    sp.dma_start(cos_sb[:, :, :], rope_cos.rearrange("(t q) i -> q t i", q=P)).then_inc(gains_loaded, 16)
                    sp.dma_start(sin_sb[:, :, :], rope_sin.rearrange("(t q) i -> q t i", q=P)).then_inc(gains_loaded, 16)
            w_view = w_in[0].rearrange("(k q) n -> q k n", q=P)
            sp.dma_start(w_in_sb[:, :, NQKV:], w_view[:, :, NQKV:]).then_inc(wu_loaded, 16)
            sp.dma_start(w_in_sb[:, :, 0:NQKV], w_view[:, :, 0:NQKV]).then_inc(wqkv_loaded, 16)
            sp.dma_start(router[:, :, :], w_router[0].rearrange("(k q) e -> q k e", q=P)).then_inc(router_loaded, 16)
            for p in range(1, NPAIR):
                n = turn_at["x", p - 1] + 3
                sp.wait_ge(t_ready[n % 2], n // 2 + 1)
                sp.dma_start(x_in[:, :, :], x_rows(p)).then_inc(x_loaded, 16)
            sp.wait_ge(qkv_ready, 2 * NT)
            for b in range(ADA_FIRST, ADA_BLOCKS):
                i = b - ADA_FIRST
                if i >= 3:
                    sp.wait_ge(rows_ready, b - 2)
                sp.dma_start(ada2[i % 3][:, :, :], ada_view[b]).then_inc(ada_loaded[i % 3], 16)
            sp.dma_start(w_out_sb[:, :, :], w_out[0].rearrange("(k q) n -> q k n", q=P)).then_inc(w_out_loaded, 16)
            gate_view = w_gate[0].rearrange("e (k q) (s n) -> e s q k n", q=P, n=MC)
            up_view = w_up[0].rearrange("e (k q) (s n) -> e s q k n", q=P, n=MC)
            down_view = w_down[0].rearrange("e (k q) (s n) -> e s q k n", q=P, n=MC)
            for p in range(NPAIR):
                if p == 0:
                    sp.wait_ge(conv_out, 3 * CC)
                    sp.wait_ge(out_bank_free, STEPS + 1)
                else:
                    sp.wait_ge(x1_ready, 2 * p)
                sp.dma_start(x_again[:, :, :], x_rows(p)).then_inc(x_reloaded, 16)
                if p == 0:
                    for s in range(NS):
                        sp.dma_start(gate_w_sb[:, s], gate_view[0, s]).then_inc(gate_w_loaded[s], 16)
                        sp.dma_start(up_w_sb[:, s], up_view[0, s]).then_inc(up_w_loaded[s], 16)
                for a in range(2):
                    q = 2 * p + a
                    dst_y = y_s[0] if group(p) else y_p[0, 2 * P * p:2 * P * (p + 1)]
                    dst_n = xn_s if group(p) else xn_p[2 * P * p:2 * P * (p + 1)]
                    sp.wait_ge(x1_ready, q + 1)
                    sp.dma_start(dst_y[P * a:P * (a + 1), :], x1[:, a, :]).then_inc(y_stored[a], 16)
                    sp.wait_ge(xn2_ready, q + 1)
                    sp.dma_start(dst_n[P * a:P * (a + 1), :], xn2[:, a, :]).then_inc(xn_stored[a], 16)
            sp.wait_ge(mix_ready, NT)
            for s in range(NS):
                sp.dma_start(down_w_sb[:, s], down_view[0, s]).then_inc(down_w_loaded[s], 16)
            with sp.Fori(1, NE) as e:
                for s in range(NS):
                    m = 2 * s + 1
                    sp.wait_ge(gate_ready, (e - 1) * KC + m + 1)
                    sp.dma_start(gate_w_sb[:, s], gate_view[e, s]).then_inc(gate_w_loaded[s], 16)
                    sp.wait_ge(up_ready, (e - 1) * KC + m + 1)
                    sp.dma_start(up_w_sb[:, s], up_view[e, s]).then_inc(up_w_loaded[s], 16)
                for s in range(NS):
                    m = 2 * s + 1
                    sp.wait_ge(d_ready, KC + (e - 1) * 2 * KC + m + 1)
                    sp.dma_start(down_w_sb[:, s], down_view[e, s]).then_inc(down_w_loaded[s], 16)

        @block.gpsimd
        def _(pool):
            pool.memset(ident[:, :], 0.0).then_inc(ident_made, 1)
            pool.memset(ones[:, :], 1.0).then_inc(fills_made, 1)
            pool.memset(eps_col[:, :], EPS).then_inc(fills_made, 1)
            pool.wait_ge(ident_made, 1)
            pool.affine_select(out=ident[:, :], in_=ident[:, :], compare_op=ALU.not_equal, fill=1.0,
                               base=0, pattern=[[-1, P]], channel_multiplier=1).then_inc(ident_made, 1)
            pool.memset(a_t[:, :, 0:A_PROMPT], 0.0).then_inc(fills_made, 1)
            pool.memset(a_t[:, :, A_PROMPT + SP_TOK:A_SAMPLE], 0.0).then_inc(fills_made, 1)
            pool.memset(a_t[:, :, A_SAMPLE + SS_TOK:A_ROW], 0.0).then_inc(fills_made, 1)
            pool.memset(v_one[:, :, :, HD:P], 1.0).then_inc(fills_made, 1)
            pool.memset(i_top_p[:, NE:NE + 1], 0).then_inc(fills_made, 1)
            pool.memset(i_top_s[:, NE:NE + 1], 0).then_inc(fills_made, 1)

            for q in range(NT):
                a = q % 2
                pool.wait_ge(qkv_copied, 2 * q + 2)
                if q:
                    pool.wait_ge(rotated, q)
                pool.tensor_tensor(sq[:, :, :], qk[a][:, :, :], qk[a][:, :, :], ALU.mult).then_inc(sq_ready, 1)
                pool.wait_ge(q_normed, q + 1)
                even = qk[a][:, :, :].rearrange("p h (i b) -> p h i b", b=2)
                out = rot2[:, :, :].rearrange("p h (i b) -> p h i b", b=2)
                tab = rope_s[:, q % 8, :, :].rearrange("p g (i b) -> p g i b", b=2)
                for b in range(2):
                    for g, h0, nh in ((0, 0, NH), (1, NH, NKV)):
                        t = tab[:, g:g + 1, :, b].to_broadcast([P, nh, HD // 2])
                        last = pool.tensor_tensor(out[:, h0:h0 + nh, :, b], even[:, h0:h0 + nh, :, 1 - b], t, ALU.mult)
                last.then_inc(rot2_ready, 1)

            for n in (n_turns[0] - 2, n_turns[0] - 1):
                pool.wait_ge(t_free[n % 2], n // 2 + 1)
            pool.wait_ge(rows_ready, ADA_BLOCKS)

            def copy_q(n, h, t, head):
                if n is not None:
                    pool.wait_ge(scores_ready, n - 1)
                pool.tensor_copy(q_now[:, h % 2, :], q_st[:, t, head, :]).then_inc(q_copied, 1)

            j0, t0, _, _ = phases[0]
            copy_q(None, 0, t0, j0 * QPK)
            copy_q(None, 1, t0, j0 * QPK + 1)
            for i, (j, t0, nt, s0) in enumerate(phases):
                def ahead(step, t, nxt):
                    n = step * QPK
                    copy_q(n + 2, 2, t, j * QPK + 2)
                    copy_q(n + 3, 3, t, j * QPK + 3)
                    if nxt is not None:
                        nj, ntile = nxt
                        copy_q(n + 4, 0, ntile, nj * QPK)
                        copy_q(n + 5, 1, ntile, nj * QPK + 1)
                with pool.Fori(0, nt - 1) as r:
                    ahead(r + s0, r + t0, (j, r + t0 + 1))
                follow = (phases[i + 1][0], phases[i + 1][1]) if i + 1 < len(phases) else None
                ahead(s0 + nt - 1, t0 + nt - 1, follow)

            for q in range(NT):
                p, a = q // 2, q % 2
                pool.wait_ge(x_reloaded, 16 * (p + 1))
                pool.wait_ge(mix_gated, q + 1)
                pool.tensor_tensor(x1[:, a, :], x1[:, a, :], x_again[:, a, :], ALU.add).then_inc(x1_ready, 1)

            def fetch(e, n):
                pool.tensor_copy(i_now[:, 0:1], i_top_p[:, bass.ds(e, 1)]).then_inc(idx_copied, 1)
                pool.tensor_copy(i_now[0:CAP_S, 1:2], i_top_s[0:CAP_S, bass.ds(e, 1)]).then_inc(idx_copied, 1)
                pool.wait_ge(idx_copied, n)
                pool.sem_inc(pool_steps, 1)
                pool.indirect_dma_start(xg_p[:, :], None, xn_p, bass.IndirectOffsetOnAxis(i_now[:, 0:1], axis=0)).then_inc(gathered, 16)
                pool.indirect_dma_start(xg_s[:, :], None, xn_s, bass.IndirectOffsetOnAxis(i_now[0:CAP_S, 1:2], axis=0)).then_inc(gathered, 16)

            pool.wait_ge(top_ready, 4)
            pool.wait_ge(fills_made, 8)
            for a in range(2):
                pool.wait_ge(xn_stored[a], 16 * NPAIR)
                pool.wait_ge(y_stored[a], 16 * NPAIR)
            pool.sem_inc(ye_free, 1)
            fetch(0, 2)
            with pool.Fori(0, NE) as e:
                pool.wait_ge(d_ready, e * 2 * KC + KC)
                fetch(e + 1, 4 * e + 4)
                pool.tensor_copy(i_now[:, 2:3], i_top_p[:, bass.ds(e, 1)]).then_inc(idx_copied, 1)
                pool.tensor_copy(i_now[0:CAP_S, 3:4], i_top_s[0:CAP_S, bass.ds(e, 1)]).then_inc(idx_copied, 1)
                pool.wait_ge(idx_copied, 4 * e + 6)
                pool.wait_ge(ye_ready, 4 * e + 5)
                pool.sem_inc(pool_steps, 1)
                pool.indirect_dma_start(y_p[0], bass.IndirectOffsetOnAxis(i_now[:, 2:3], axis=0), ye_p[:, :], None,
                                        compute_op=ALU.add).then_inc(scattered, 16)
                pool.indirect_dma_start(y_s[0], bass.IndirectOffsetOnAxis(i_now[0:CAP_S, 3:4], axis=0), ye_s[:, :], None,
                                        compute_op=ALU.add).then_inc(scattered, 16)
                pool.wait_ge(scattered, 32 * e + 32)
                pool.sem_inc(ye_free, 1)
            pool.wait_ge(gathered, 32 * (NE + 1))

        @block.scalar
        def _(act):
            act.wait_ge(cols_ready, 1)
            act.activation(silu_c[:, :], cols[:, ROW_C:ROW_C + 2 * KC], ACT.Silu).then_inc(silu_ready, 1)

            def copy_rows(b):
                act.wait_ge(rows_ready, b + 1)
                if b >= 2:
                    act.wait_ge(rows_turned, b - 1)
                act.activation(mod_rows[:, b % 2, :], bank(2 + b % 2)[0:2, :], ACT.Copy).then_inc(rows_copied, 1)

            for b in range(ADA_FIRST):
                copy_rows(b)

            def square_x(p):
                act.wait_ge(x_loaded, 16 * (p + 1))
                if p:
                    act.wait_ge(x_recip, p)
                for a in range(2):
                    if p or a:
                        act.wait_ge(x_squared, 2 * p + a)
                    act.activation(junk[:, :], x_in[:, a, :], ACT.Square, accum_out=ss_x[:, a:a + 1]).then_inc(x_squared, 1)
                act.wait_ge(x_squared, 2 * p + 2)
                act.activation(rt_x[:, :], ss_x[:, :], ACT.Sqrt, scale=1.0 / D, bias=eps_col[:, :]).then_inc(x_root, 1)

            def x_out(p):
                for i in range(0, 4, 2):
                    n = turn_at["x", p] + i
                    act.wait_ge(t_ready[n % 2], n // 2 + 1)
                    for c in range(2):
                        k = 2 * i + c
                        last = act.activation(h_t[:, p % 2, k, :], bank(n % 2)[:, 256 * c:256 * (c + 1)], ACT.Identity,
                                              scale=a1[:, k, group(p):group(p) + 1],
                                              bias=mod[:, SHIFT1 + k, group(p):group(p) + 1])
                    last.then_inc(t_free[n % 2], 1)

            def high_out(p, a):
                t = 2 * p + a
                for i in range(3):
                    n = turn_at["q", p, a] + i
                    act.wait_ge(t_ready[n % 2], n // 2 + 1)
                    if i < 2:
                        src = bank(n % 2)[0:HD, :].rearrange("d (h q) -> d h q", h=4)
                        last = act.activation(q_st[0:HD, t, 4 * i:4 * i + 4, :], src, ACT.Copy)
                    else:
                        src = bank(n % 2)[0:HD, 0:NKV * P].rearrange("d (j q) -> d j q", j=NKV)
                        act.activation(k_hi[0:HD, :, P * t:P * (t + 1)], src, ACT.Copy)
                        last = act.activation(k_hi[HD:P, :, P * t:P * (t + 1)], src, ACT.Copy)
                    last.then_inc(high_ready, 1)

            def copies(p, a):
                q = 2 * p + a
                if q >= 2:
                    n = turn_at["q", p - 1, a] + 2
                    act.wait_ge(t_ready[n % 2], n // 2 + 1)
                act.wait_ge(qkv_ready, 2 * q + 1)
                act.activation(qk[a][:, 0:NH, :], bank(4 + a).rearrange("p (h d) -> p h d", h=NH), ACT.Copy).then_inc(qkv_copied, 1)
                act.wait_ge(qkv_ready, 2 * q + 2)
                act.activation(qk[a][:, NH:NH + NKV, :], bank(6 + a)[:, 0:DKV].rearrange("p (h d) -> p h d", h=NKV), ACT.Copy)
                act.activation(v_one[:, q, :, 0:HD], bank(6 + a)[:, DKV:2 * DKV].rearrange("p (h d) -> p h d", h=NKV),
                               ACT.Copy).then_inc(qkv_copied, 1)
                act.wait_ge(sq_summed, q + 1)
                act.activation(rt_q[:, a, :], ss_q[:, a, :], ACT.Sqrt, scale=1.0 / HD, bias=eps_col[:, :]).then_inc(q_root, 1)

            act.wait_ge(fills_made, 8)
            square_x(0)
            act.wait_ge(scale_ready, 1)
            x_out(0)
            for p in range(NPAIR):
                if p + 1 < NPAIR:
                    square_x(p + 1)
                for i in range(CC):
                    n = CC * p + i
                    act.wait_ge(u_ready, n + 1)
                    if n >= 2:
                        act.wait_ge(u_gated, n - 1)
                    act.activation(sig[:, n % 2, :], bank(2 + n % 2)[:, 256:512], ACT.Sigmoid).then_inc(sig_ready, 1)
                if p:
                    high_out(p - 1, 1)
                copies(p, 0)
                if p + 1 < NPAIR:
                    x_out(p + 1)
                copies(p, 1)
                high_out(p, 0)
            high_out(NPAIR - 1, 1)

            for b in range(ADA_FIRST, ADA_BLOCKS):
                copy_rows(b)
            for n in range(4):
                act.wait_ge(gate_rows_ready, n + 1)
                act.activation(gate1_row[:, n // 2, 512 * (n % 2):512 * (n % 2) + 512], bank(2 + n % 2), ACT.Copy).then_inc(gate_rows_copied, 1)

            act.sem_inc(turn_bank_free, 2)
            act.sem_inc(out_bank_free, 1)

            def exponent(n, h, nk):
                act.wait_ge(max_ready, n + 1)
                act.activation(probs[:, h % 2, 0:P * nk], two[h % 2][:, :, :].rearrange("p b n -> p (b n)")[:, 0:P * nk], ACT.Exp,
                               bias=negmax[:, h:h + 1]).then_inc(probs_ready, 1)

            def probs_out(n, h, nk):
                for half in range(2):
                    act.wait_ge(turned, 2 * n + half + 1)
                    kk = nk // 2
                    act.activation(probs_t[:, kk * half:kk * half + kk, h, :],
                                   bank(4 + half)[:, 0:kk * P].rearrange("p (k q) -> p k q", k=kk), ACT.Copy).then_inc(turn_bank_free, 1)

            exponent(0, 0, phases[0][2])
            for i, (j, t0, nt, s0) in enumerate(phases):
                def soft(step, nxt_nk):
                    n = step * QPK
                    for h in range(QPK):
                        if h + 1 < QPK:
                            exponent(n + h + 1, h + 1, nt)
                        elif nxt_nk is not None:
                            exponent(n + QPK, 0, nxt_nk)
                        probs_out(n + h, h, nt)
                with act.Fori(0, nt - 1) as r:
                    soft(r + s0, nt)
                soft(s0 + nt - 1, phases[i + 1][2] if i + 1 < len(phases) else None)

            for s, (o, n) in enumerate(((0, 512), (512, 512), (C_SAMPLE, SS_TOK))):
                for c in range(CC):
                    act.wait_ge(centred, CC * s + c + 1)
                    if s and c == 0:
                        act.wait_ge(var_ready, s)
                    act.activation(sq_c[:, c, 0:n], c_t[:, c, o:o + n], ACT.Square).then_inc(squared, 1)
                act.wait_ge(var_ready, s + 1)
                act.activation(rt_c[:, 0:n], bank(1)[:, 0:n], ACT.Sqrt, scale=1.0 / DC, bias=eps_col[:, :]).then_inc(root_ready, 1)
            for s, (o, n) in enumerate(((0, 512), (512, 512), (C_SAMPLE, SS_TOK))):
                for c in range(CC):
                    act.wait_ge(scaled, CC * s + c + 1)
                    act.activation(c_t[:, c, o:o + n], c_t[:, c, o:o + n], ACT.Silu, scale=cols[:, ROW_LG + c:ROW_LG + c + 1],
                                   bias=cols[:, ROW_LB + c:ROW_LB + c + 1]).then_inc(conv_out, 1)

            def norm2(q):
                a = q % 2
                act.wait_ge(x1_ready, q + 1)
                if q >= 2:
                    act.wait_ge(xn_stored[a], 16 * (q // 2))
                    act.wait_ge(t2_ready[1], 2 * ((q - 2) // 2) + 2)
                if q:
                    act.wait_ge(x1_recip, q)
                act.activation(xn2[:, a, :], x1[:, a, :], ACT.Square, accum_out=ss_x[:, 0:1]).then_inc(x1_squared, 1)
                act.wait_ge(x1_squared, q + 1)
                act.activation(rt_x[:, 0:1], ss_x[:, 0:1], ACT.Sqrt, scale=1.0 / D, bias=eps_col[:, :]).then_inc(x1_root, 1)

            def h2_out(p):
                for i in range(0, 4, 2):
                    n = 4 * p + i
                    act.wait_ge(t2_ready[n % 2], n // 2 + 1)
                    for c in range(2):
                        k = 2 * i + c
                        last = act.activation(h2_t[:, p % 2, k, :], bank(4 + n % 2)[:, 256 * c:256 * (c + 1)], ACT.Identity,
                                              scale=a2[:, k, group(p):group(p) + 1],
                                              bias=mod[:, SHIFT2 + k, group(p):group(p) + 1])
                    last.then_inc(t2_free[n % 2], 1)

            def logits_out(p):
                act.wait_ge(logits_ready, p + 1)
                act.activation(logits_t[:, 2 * P * p:2 * P * (p + 1)], bank(6)[0:NE, 0:2 * P], ACT.Copy).then_inc(logits_copied, 1)

            for p in range(NPAIR):
                norm2(2 * p)
                norm2(2 * p + 1)
                h2_out(p)
                logits_out(p)

            act.wait_ge(router_shifted, 1)
            act.activation(aff[:, :, :], aff[:, :, :], ACT.Exp).then_inc(router_exp, 1)

            def y_out(e, half):
                act.wait_ge(y_turned, 2 * e + half + 1)
                act.sem_inc(act_steps, 1)
                act.activation(ye_p[:, 512 * half:512 * half + 512], bank(6), ACT.Copy,
                               scale=g_top_p[:, bass.ds(e, 1)]).then_inc(ye_ready, 1)
                act.activation(ye_s[:, 512 * half:512 * half + 512], bank(7)[0:CAP_S, :], ACT.Copy,
                               scale=g_top_s[0:CAP_S, bass.ds(e, 1)]).then_inc(ye_ready, 1)

            act.wait_ge(top_ready, 4)
            act.sem_inc(ye_ready, 1)
            with act.Fori(0, NE) as e:
                for m in range(KC):
                    act.wait_ge(gate_ready, e * KC + m + 1)
                    act.activation(sil[:, m % 2, :], bank(m % 2)[:, 0:CAP], ACT.Silu).then_inc(silu_done, 1)
                act.wait_ge(ye_free, e + 1)
                y_out(e, 0)
                y_out(e, 1)

        @block.tensor
        def _(pe):
            pe.wait_ge(ident_made, 2)
            pe.wait_ge(rows_loaded, 16 * 9)
            pe.transpose(bank(0)[:, 0:ROWS], rows[:, :], ident[0:ROWS, 0:ROWS])
            for c in range(CC):
                last = pe.transpose(bank(0)[:, 128 + TAPS * c:128 + TAPS * (c + 1)], taps_row[:, P * c:P * (c + 1)],
                                    ident[0:TAPS, 0:TAPS])
            last.then_inc(cols_turned, 1)

            silu_pair = silu_c[:, :].rearrange("p (g k) -> p k g", g=2)

            def mod_block(b, w, loads):
                if b == 0:
                    pe.wait_ge(silu_ready, 1)
                if b >= 2:
                    pe.wait_ge(rows_copied, b - 1)
                pe.wait_ge(ada_loaded[loads[0]], 16 * loads[1])
                for k in range(KC):
                    last = pe.matmul(bank(2 + b % 2)[0:2, :], silu_pair[:, k, :], w[:, k, :], start=(k == 0), stop=(k == KC - 1))
                last.then_inc(rows_ready, 1)

            def mod_turn(b):
                pe.wait_ge(rows_copied, b + 1)
                for j in range(4):
                    last = pe.transpose(bank(7)[:, 2 * (4 * b + j):2 * (4 * b + j) + 2], mod_rows[:, b % 2, P * j:P * (j + 1)],
                                        ident[0:2, 0:2])
                last.then_inc(rows_turned, 1)

            for b in range(ADA_FIRST):
                mod_block(b, ada[b % 3], (b % 3, b // 3 + 1))
                if b:
                    mod_turn(b - 1)
            mod_turn(ADA_FIRST - 1)

            def turn_x(p):
                pe.wait_ge(x_normed, 2 * p + 2)
                for i in range(4):
                    n = turn_at["x", p] + i
                    if n >= 2:
                        pe.wait_ge(t_free[n % 2], n // 2)
                    for c in range(2):
                        for a in range(2):
                            last = pe.transpose(bank(n % 2)[:, 256 * c + P * a:256 * c + P * (a + 1)],
                                                x_in[:, a, P * (2 * i + c):P * (2 * i + c + 1)], ident[:, :])
                    last.then_inc(t_ready[n % 2], 1)

            def turn_q(p, a):
                pe.wait_ge(rotated, 2 * p + a + 1)
                for i in range(3):
                    n = turn_at["q", p, a] + i
                    pe.wait_ge(t_free[n % 2], n // 2)
                    for h in range(4 if i < 2 else NKV):
                        last = pe.transpose(bank(n % 2)[0:HD, P * h:P * (h + 1)], qk[a][:, 4 * i + h, :], ident[:, :])
                    last.then_inc(t_ready[n % 2], 1)

            def project_u(p):
                for b in range(2):
                    n = turn_at["x", p] + 2 + b
                    pe.wait_ge(t_free[n % 2], n // 2 + 1)
                for i in range(CC):
                    n = CC * p + i
                    if n >= 2:
                        pe.wait_ge(u_gated, n - 1)
                    for part in range(2):
                        col = NQKV + DC * part + P * i
                        for k in range(KC):
                            last = pe.matmul(bank(2 + n % 2)[:, 256 * part:256 * part + 256], w_in_sb[:, k, col:col + P],
                                             h_t[:, p % 2, k, :], start=(k == 0), stop=(k == KC - 1))
                    last.then_inc(u_ready, 1)

            def project_qkv(p, a):
                q = 2 * p + a
                if q >= 2:
                    pe.wait_ge(qkv_copied, 2 * q - 2)
                for b, c0, n in ((4 + a, 0, DA), (6 + a, DA, 2 * DKV)):
                    for k in range(KC):
                        last = pe.matmul(bank(b)[:, 0:n], h_t[:, p % 2, k, P * a:P * (a + 1)], w_in_sb[:, k, c0:c0 + n],
                                         start=(k == 0), stop=(k == KC - 1))
                    last.then_inc(qkv_ready, 1)

            turn_x(0)
            pe.wait_ge(wu_loaded, 16)
            pe.wait_ge(rows_copied, ADA_FIRST)
            for p in range(NPAIR):
                project_u(p)
                if p:
                    turn_q(p - 1, 1)
                if p == 0:
                    pe.wait_ge(wqkv_loaded, 16)
                    pe.wait_ge(mod_ready, 1)
                project_qkv(p, 0)
                if p + 1 < NPAIR:
                    turn_x(p + 1)
                project_qkv(p, 1)
                turn_q(p, 0)
            turn_q(NPAIR - 1, 1)

            pe.wait_ge(u_gated, CC * NPAIR)
            pe.wait_ge(qkv_copied, 2 * NT)
            for b in range(ADA_FIRST, ADA_BLOCKS):
                i = b - ADA_FIRST
                prior = 2 if i % 3 == 0 else 1
                mod_block(b, ada2[i % 3], (i % 3, prior + i // 3 + 1))
                if i:
                    mod_turn(b - 1)
            mod_turn(ADA_BLOCKS - 1)
            pe.wait_ge(rows_copied, ADA_BLOCKS)
            for n in range(4):
                pe.wait_ge(diag_ready, 4 * n + 4)
                if n >= 2:
                    pe.wait_ge(gate_rows_copied, n - 1)
                for i in range(4):
                    last = pe.matmul(bank(2 + n % 2)[:, P * i:P * (i + 1)], ones[:, :], diag[:, n % 2, i, :], start=True, stop=True)
                last.then_inc(gate_rows_ready, 1)

            pe.wait_ge(gate_rows_copied, 4)
            last_turn = n_turns[0] - 1
            for n in (last_turn - 1, last_turn):
                pe.wait_ge(t_free[n % 2], n // 2 + 1)

            def scores(n, h, j, t0, nk, first=False):
                pe.wait_ge(q_copied, n + 1)
                if not first:
                    pe.wait_ge(probs_ready, n - 1)
                k0 = P * t0
                for c in range(0, P * nk, 512):
                    w = min(512, P * nk - c)
                    for part, ks in enumerate((k_hi, k_lo)):
                        last = pe.matmul(two[h % 2][:, c // 512, 0:w], q_now[:, h % 2, :], ks[:, j, k0 + c:k0 + c + w],
                                         start=(part == 0), stop=(part == 1))
                last.then_inc(scores_ready, 1)

            def turn_probs(n, h, nk):
                pe.wait_ge(probs_ready, n + 1)
                kk = nk // 2
                for half in range(2):
                    pe.wait_ge(turn_bank_free, 2 * n + half + 1)
                    for k in range(kk):
                        last = pe.transpose(bank(4 + half)[:, P * k:P * (k + 1)],
                                            probs[:, h % 2, P * (kk * half + k):P * (kk * half + k + 1)], ident[:, :])
                    last.then_inc(turned, 1)

            def weigh(step, j, t0, nk):
                pe.wait_ge(turn_bank_free, step * 8 + 10)
                pe.wait_ge(out_bank_free, step + 1)
                for k in range(nk):
                    last = pe.matmul(bank(6), v_one[:, t0 + k, j, :], probs_t[:, k, :, :].rearrange("p h q -> p (h q)"),
                                     start=(k == 0), stop=(k == nk - 1))
                last.then_inc(pv_ready, 1)

            j0, t00, nt0, _ = phases[0]
            scores(0, 0, j0, t00, nt0, first=True)
            scores(1, 1, j0, t00, nt0, first=True)
            for i, (j, t0, nt, s0) in enumerate(phases):
                def attend(step, nxt):
                    n = step * QPK
                    turn_probs(n, 0, nt)
                    scores(n + 2, 2, j, t0, nt)
                    turn_probs(n + 1, 1, nt)
                    scores(n + 3, 3, j, t0, nt)
                    turn_probs(n + 2, 2, nt)
                    if nxt is not None:
                        scores(n + 4, 0, *nxt)
                    turn_probs(n + 3, 3, nt)
                    if nxt is not None:
                        scores(n + 5, 1, *nxt)
                    weigh(step, j, t0, nt)
                with pe.Fori(0, nt - 1) as r:
                    attend(r + s0, (j, t0, nt))
                attend(s0 + nt - 1, (phases[i + 1][0], phases[i + 1][1], phases[i + 1][2]) if i + 1 < len(phases) else None)

            pe.wait_ge(probs_ready, HEADS_ALL)
            for c in range(CC):
                pe.wait_ge(conv_done[c], TAPS)
            for s, (o, n) in enumerate(((0, 512), (512, 512), (C_SAMPLE, SS_TOK))):
                if s:
                    pe.wait_ge(centred, CC * s)
                for c in range(CC):
                    last = pe.matmul(bank(0)[:, 0:n], ones[:, :], c_t[:, c, o:o + n], start=(c == 0), stop=(c == CC - 1))
                last.then_inc(mean_ready, 1)
                pe.wait_ge(squared, CC * (s + 1))
                if s:
                    pe.wait_ge(root_ready, s)
                for c in range(CC):
                    last = pe.matmul(bank(1)[:, 0:n], ones[:, :], sq_c[:, c, 0:n], start=(c == 0), stop=(c == CC - 1))
                last.then_inc(var_ready, 1)

            def project_out(q):
                if q >= 2:
                    pe.wait_ge(mix_gated, q - 1)
                p = q // 2
                o = C_SAMPLE + P * (q % 2) if group(p) else P * q
                for half in range(2):
                    for k in range(KC):
                        lhs = mix_t[:, k, P * q:P * (q + 1)] if k < CC else c_t[:, k - CC, o:o + P]
                        last = pe.matmul(two[q % 2][:, half, :], lhs, w_out_sb[:, k, 512 * half:512 * half + 512],
                                         start=(k == 0), stop=(k == KC - 1))
                last.then_inc(mix_ready, 1)

            def turn_x1(p):
                pe.wait_ge(xn2_ready, 2 * p + 2)
                for i in range(4):
                    n = 4 * p + i
                    if n >= 2:
                        pe.wait_ge(t2_free[n % 2], n // 2)
                    for c in range(2):
                        for a in range(2):
                            last = pe.transpose(bank(4 + n % 2)[:, 256 * c + P * a:256 * c + P * (a + 1)],
                                                xn2[:, a, P * (2 * i + c):P * (2 * i + c + 1)], ident[:, :])
                    last.then_inc(t2_ready[n % 2], 1)

            def route(p):
                for b in range(2):
                    pe.wait_ge(t2_free[b], 2 * p + 2)
                if p:
                    pe.wait_ge(logits_copied, p)
                for k in range(KC):
                    last = pe.matmul(bank(6)[0:NE, 0:2 * P], router[:, k, :], h2_t[:, p % 2, k, :], start=(k == 0), stop=(k == KC - 1))
                last.then_inc(logits_ready, 1)

            pe.wait_ge(w_out_loaded, 16)
            pe.wait_ge(root_ready, 3)
            pe.wait_ge(conv_out, 3 * CC)
            pe.wait_ge(out_bank_free, STEPS + 1)
            pe.wait_ge(router_loaded, 16)
            for p in range(NPAIR):
                project_out(2 * p)
                if p:
                    turn_x1(p - 1)
                project_out(2 * p + 1)
                if p:
                    route(p - 1)
            turn_x1(NPAIR - 1)
            route(NPAIR - 1)

            pe.wait_ge(logits_copied, NPAIR)
            pe.wait_ge(mix_gated, NT)
            for t in range(NT):
                last = pe.transpose(bank(0)[:, NE * t:NE * (t + 1)], logits_t[:, P * t:P * (t + 1)], ident[0:NE, 0:NE])
            last.then_inc(logits_turned, 1)
            pe.wait_ge(aff_ready, 1)
            for t in range(NT):
                b, o = (1 + t // 4, P * (t % 4))
                last = pe.transpose(bank(b)[0:NE, o:o + P], aff[:, t, :], ident[:, :])
                if t in (3, 7, 9):
                    last.then_inc(aff_turned, 1)
            pe.wait_ge(top_float, 4)
            for i in range(2):
                pe.transpose(bank(0)[:, NE * i:NE * (i + 1)], top_p[:, i, :], ident[0:NE, 0:NE])
            for i in range(2):
                last = pe.transpose(bank(0)[0:CAP_S, NE * (2 + i):NE * (3 + i)], top_s[:, i, :], ident[0:NE, 0:NE])
            last.then_inc(top_turned, 1)

            def turn_tokens(e, n0):
                pe.wait_ge(gathered, 32 * e + 32)
                for k in range(KC):
                    pe.wait_ge(d_free, n0 + k + 1)
                    b = bank(4 + k % 2)
                    pe.transpose(b[:, 0:CAP_P], xg_p[:, P * k:P * (k + 1)], ident[:, :])
                    pe.transpose(b[:, CAP_P:CAP], xg_s[:, P * k:P * (k + 1)], ident[0:CAP_S, 0:CAP_S]).then_inc(d_ready, 1)

            def turn_y(e, m):
                pe.wait_ge(d_free, 2 * KC * e + KC + m + 3)
                if m % 4 == 0:
                    pe.wait_ge(ye_ready, 4 * e + 1 + m // 2)
                o = P * (m % 4)
                pe.transpose(bank(6)[:, o:o + P], y_t[:, m, 0:CAP_P], ident[:, :])
                last = pe.transpose(bank(7)[0:CAP_S, o:o + P], y_t[:, m, CAP_P:CAP], ident[:, :])
                if m % 4 == 3:
                    last.then_inc(y_turned, 1)

            turn_tokens(0, 0)
            with pe.Fori(0, NE) as e:
                pe.wait_ge(d_free, 2 + KC + 2 * KC * e)
                for m in range(KC):
                    s, o = m // 2, P * (m % 2)
                    pe.wait_ge(hid_ready, e * KC + m + 1)
                    if m % 2 == 0:
                        pe.wait_ge(gate_w_loaded[s], 16 * e + 16)
                    for k in range(KC):
                        last = pe.matmul(bank(m % 2)[:, 0:CAP], gate_w_sb[:, s, k, o:o + P], xe_t[:, k, :], start=(k == 0), stop=(k == KC - 1))
                    last.then_inc(gate_ready, 1)
                    if m % 2 == 0:
                        pe.wait_ge(up_w_loaded[s], 16 * e + 16)
                    for k in range(KC):
                        last = pe.matmul(bank(2 + m % 2)[:, 0:CAP], up_w_sb[:, s, k, o:o + P], xe_t[:, k, :], start=(k == 0), stop=(k == KC - 1))
                    last.then_inc(up_ready, 1)
                pe.wait_ge(hid_ready, 2 + e * KC + KC)
                for m in range(KC):
                    s, o = m // 2, P * (m % 2)
                    pe.wait_ge(d_free, 2 * KC * e + KC + m + 1)
                    if m % 2 == 0:
                        pe.wait_ge(down_w_loaded[s], 16 * e + 16)
                    for k in range(KC):
                        last = pe.matmul(bank(4 + m % 2)[:, 0:CAP], down_w_sb[:, s, k, o:o + P], hid[:, k, :], start=(k == 0), stop=(k == KC - 1))
                    last.then_inc(d_ready, 1)
                    if m:
                        turn_y(e, m - 1)
                turn_tokens(e + 1, 2 * KC * (e + 1))
                turn_y(e, KC - 1)

        @block.vector
        def _(dve):
            dve.wait_ge(cols_turned, 1)
            dve.tensor_copy(cols[:, :], bank(0)[:, 0:ROWS]).then_inc(cols_ready, 1)
            dve.tensor_copy(taps[:, :, :], bank(0)[:, 128:128 + CC * TAPS].rearrange("p (c t) -> p c t", c=CC)).then_inc(cols_ready, 1)
            dve.wait_ge(gains_loaded, 64)
            dve.tensor_scalar(gains[:, 0, :], gains[:, 0, :], HD ** -0.5, None, ALU.mult).then_inc(gains_scaled, 1)
            dve.wait_ge(gains_scaled, 1)
            dve.tensor_scalar(ngains[:, :, :], gains[:, :, :], -1.0, None, ALU.mult).then_inc(gains_scaled, 1)
            dve.wait_ge(gains_scaled, 2)
            for g in range(2):
                gain = gains[:, g, :].rearrange("p (i b) -> p i b", b=2)
                ngain = ngains[:, g, :].rearrange("p (i b) -> p i b", b=2)
                out_c = rope_c[:, :, g, :].rearrange("p t (i b) -> p t i b", b=2)
                out_s = rope_s[:, :, g, :].rearrange("p t (i b) -> p t i b", b=2)

                def over_tiles(v):
                    return v.unsqueeze(1).to_broadcast([P, 8, HD // 2])
                for b in range(2):
                    dve.tensor_tensor(out_c[:, :, :, b], cos_sb[:, :, :], over_tiles(gain[:, :, b]), ALU.mult).then_inc(tables_ready, 1)
                dve.tensor_tensor(out_s[:, :, :, 0], sin_sb[:, :, :], over_tiles(ngain[:, :, 1]), ALU.mult).then_inc(tables_ready, 1)
                dve.tensor_tensor(out_s[:, :, :, 1], sin_sb[:, :, :], over_tiles(gain[:, :, 0]), ALU.mult).then_inc(tables_ready, 1)

            def norm_x(p):
                dve.wait_ge(x_root, p + 1)
                dve.reciprocal(rs_x[:, :], rt_x[:, :]).then_inc(x_recip, 1)
                dve.wait_ge(x_recip, p + 1)
                for a in range(2):
                    dve.tensor_scalar(x_in[:, a, :], x_in[:, a, :], rs_x[:, a:a + 1], None, ALU.mult).then_inc(x_normed, 1)

            norm_x(0)
            dve.wait_ge(rows_turned, ADA_FIRST)
            dve.wait_ge(cols_ready, 2)

            def mod_cols(c0, c1):
                bias = cols[:, ROW_AB + c0:ROW_AB + c1].unsqueeze(2).to_broadcast([P, c1 - c0, 2])
                dve.tensor_tensor(mod[:, c0:c1, :], bank(7)[:, 2 * c0:2 * c1].rearrange("p (c g) -> p c g", g=2), bias,
                                  ALU.add).then_inc(mod_ready, 1)

            mod_cols(0, GATE1)
            dve.wait_ge(mod_ready, 1)

            def scale_of(out, norm_row, scale_col):
                gain = cols[:, norm_row:norm_row + KC].unsqueeze(2).to_broadcast([P, KC, 2])
                dve.scalar_tensor_tensor(out=out[:, :, :], in0=mod[:, scale_col:scale_col + KC, :], scalar=1.0, in1=gain,
                                         op0=ALU.add, op1=ALU.mult).then_inc(scale_ready, 1)

            scale_of(a1, ROW_NMIX, SCALE1)
            dve.wait_ge(scale_ready, 1)

            def x_out(p):
                g = group(p)
                for i in range(1, 4, 2):
                    n = turn_at["x", p] + i
                    dve.wait_ge(t_ready[n % 2], n // 2 + 1)
                    for c in range(2):
                        k = 2 * i + c
                        last = dve.tensor_scalar(h_t[:, p % 2, k, :], bank(n % 2)[:, 256 * c:256 * (c + 1)], a1[:, k, g:g + 1],
                                                 mod[:, SHIFT1 + k, g:g + 1], ALU.mult, ALU.add)
                    last.then_inc(t_free[n % 2], 1)

            def low_out(p, a):
                t = 2 * p + a
                for i in range(3):
                    n = turn_at["q", p, a] + i
                    dve.wait_ge(high_ready, 3 * t + i + 1)
                    if i < 2:
                        src = bank(n % 2)[0:HD, :].rearrange("d (h q) -> d h q", h=4)
                        last = dve.tensor_tensor(q_st[HD:P, t, 4 * i:4 * i + 4, :], src,
                                                 q_st[0:HD, t, 4 * i:4 * i + 4, :].bitcast(F32), ALU.subtract)
                    else:
                        src = bank(n % 2)[0:HD, 0:NKV * P].rearrange("d (j q) -> d j q", j=NKV)
                        for lo in (0, HD):
                            last = dve.tensor_tensor(k_lo[lo:lo + HD, :, P * t:P * (t + 1)], src,
                                                     k_hi[0:HD, :, P * t:P * (t + 1)].bitcast(F32), ALU.subtract)
                    last.then_inc(t_free[n % 2], 1)

            def qk_norm(q):
                a = q % 2
                dve.wait_ge(sq_ready, q + 1)
                dve.tensor_reduce(ss_q[:, a, :], sq[:, :, :], AX.X, ALU.add).then_inc(sq_summed, 1)
                dve.wait_ge(q_root, q + 1)
                dve.reciprocal(rs_q[:, a, :], rt_q[:, a, :]).then_inc(q_recip, 1)
                dve.wait_ge(q_recip, q + 1)
                dve.tensor_tensor(qk[a][:, :, :], qk[a][:, :, :], rs_q[:, a, :].unsqueeze(2).to_broadcast([P, 10, HD]),
                                  ALU.mult).then_inc(q_normed, 1)
                dve.wait_ge(q_normed, q + 1)
                for g, h0, nh in ((0, 0, NH), (1, NH, NKV)):
                    tab = rope_c[:, q % 8, g:g + 1, :].to_broadcast([P, nh, HD])
                    dve.tensor_tensor(rot1[:, h0:h0 + nh, :], qk[a][:, h0:h0 + nh, :], tab, ALU.mult).then_inc(rot1_ready, 1)
                dve.wait_ge(rot1_ready, 2 * q + 2)
                dve.wait_ge(rot2_ready, q + 1)
                dve.tensor_tensor(qk[a][:, :, :], rot1[:, :, :], rot2[:, :, :], ALU.add).then_inc(rotated, 1)

            x_out(0)
            for p in range(NPAIR):
                if p + 1 < NPAIR:
                    norm_x(p + 1)
                for i in range(CC):
                    n = CC * p + i
                    dve.wait_ge(sig_ready, n + 1)
                    dve.tensor_tensor(a_t[:, i, a_cols(p):a_cols(p) + 2 * P], bank(2 + n % 2)[:, 0:256], sig[:, n % 2, :],
                                      ALU.mult).then_inc(u_gated, 1)
                if p:
                    low_out(p - 1, 1)
                qk_norm(2 * p)
                if p + 1 < NPAIR:
                    x_out(p + 1)
                qk_norm(2 * p + 1)
                low_out(p, 0)
            low_out(NPAIR - 1, 1)

            dve.wait_ge(u_gated, CC * NPAIR)
            dve.wait_ge(fills_made, 8)

            def tap(c, k, n):
                dve.wait_ge(conv_done[c], n)
                dve.scalar_tensor_tensor(out=c_t[:, c, :], in0=a_t[:, c, bass.ds(k, C_LEN)], scalar=taps[:, c, bass.ds(k, 1)],
                                         in1=c_t[:, c, :], op0=ALU.mult, op1=ALU.add).then_inc(conv_done[c], 1)

            dve.wait_ge(rotated, NT)
            n = n_turns[0] - 1
            dve.wait_ge(t_ready[n % 2], n // 2 + 1)
            for c in range(CC):
                dve.tensor_scalar(c_t[:, c, :], conv_slices(c, 0), taps[:, c, 0:1], cols[:, ROW_CB + c:ROW_CB + c + 1],
                                  ALU.mult, ALU.add).then_inc(conv_done[c], 1)
            for k in range(1, TAPS_FIRST):
                for c in range(CC):
                    tap(c, k, k)
            dve.wait_ge(rows_turned, ADA_BLOCKS)
            mod_cols(GATE1, 6 * KC)
            dve.wait_ge(mod_ready, 2)
            scale_of(a2, ROW_NFFN, SCALE2)
            for n in range(4):
                if n >= 2:
                    dve.wait_ge(gate_rows_ready, n - 1)
                for i in range(4):
                    k = GATE1 + 4 * (n % 2) + i
                    dve.tensor_scalar(diag[:, n % 2, i, :], ident[:, :], mod[:, k, n // 2:n // 2 + 1], None, ALU.mult).then_inc(diag_ready, 1)

            def maximum(n, h, nk):
                dve.wait_ge(scores_ready, n + 1)
                dve.tensor_reduce(negmax[:, h:h + 1], two[h % 2][:, :, :].rearrange("p b n -> p (b n)")[:, 0:P * nk], AX.X,
                                  ALU.max, negate=True).then_inc(max_ready, 1)

            def divide(step, t, j):
                dve.wait_ge(pv_ready, step + 1)
                dve.reciprocal(rsum[:, :, :].rearrange("d h q -> d (h q)"), bank(6)[HD:P, :]).then_inc(sums_inverted, 1)
                dve.wait_ge(sums_inverted, step + 1)
                o = bank(6)[0:HD, :].rearrange("d (c b q) -> d c b q", c=2, b=2)
                r = rsum[:, :, :].rearrange("d (c b) q -> d c b q", b=2)
                for b in range(2):
                    last = dve.tensor_tensor(mix_t[HD * b:HD * (b + 1), 2 * j:2 * j + 2, bass.ds(t * P, P)], o[:, :, b, :], r[:, :, b, :], ALU.mult)
                last.then_inc(out_bank_free, 1)

            maximum(0, 0, phases[0][2])
            maximum(1, 1, phases[0][2])
            for i, (j, t0, nt, s0) in enumerate(phases):
                chunks = (2 * j, 2 * j + 1) if t0 == 0 else ()

                def between(step, t, r, nxt_nk):
                    n = step * QPK

                    def some(i):
                        for c in chunks:
                            tap(c, r * TAPS_STEP + (TAPS_FIRST + i), r * TAPS_STEP + (TAPS_FIRST + i))
                    maximum(n + 2, 2, nt)
                    some(0)
                    maximum(n + 3, 3, nt)
                    some(1)
                    if nxt_nk is not None:
                        maximum(n + 4, 0, nxt_nk)
                        maximum(n + 5, 1, nxt_nk)
                    some(2)
                    divide(step, t, j)
                with dve.Fori(0, nt - 1) as r:
                    between(r + s0, r + t0, r, nt)
                between(s0 + nt - 1, t0 + nt - 1, nt - 1, phases[i + 1][2] if i + 1 < len(phases) else None)

            for s, (o, n) in enumerate(((0, 512), (512, 512), (C_SAMPLE, SS_TOK))):
                dve.wait_ge(mean_ready, s + 1)
                for c in range(CC):
                    dve.scalar_tensor_tensor(out=c_t[:, c, o:o + n], in0=bank(0)[:, 0:n], scalar=-1.0 / DC, in1=c_t[:, c, o:o + n],
                                             op0=ALU.mult, op1=ALU.add).then_inc(centred, 1)
                dve.wait_ge(root_ready, s + 1)
                dve.reciprocal(rs_c[:, 0:n], rt_c[:, 0:n]).then_inc(inv_ready, 1)
                dve.wait_ge(inv_ready, s + 1)
                dve.wait_ge(squared, CC * (s + 1))
                for c in range(CC):
                    dve.tensor_tensor(c_t[:, c, o:o + n], c_t[:, c, o:o + n], rs_c[:, 0:n], ALU.mult).then_inc(scaled, 1)

            def gate_mix(q):
                a = q % 2
                dve.wait_ge(mix_ready, q + 1)
                if q >= 2:
                    dve.wait_ge(y_stored[a], 16 * (q // 2))
                    dve.wait_ge(xn2_ready, q - 1)
                g = group(q // 2)
                dve.tensor_tensor(x1[:, a, :], two[a][:, :, :].rearrange("p b n -> p (b n)"), gate1_row[:, g, :], ALU.mult).then_inc(mix_gated, 1)

            def norm_x1(q):
                a = q % 2
                dve.wait_ge(x1_root, q + 1)
                dve.reciprocal(rs_x[:, 0:1], rt_x[:, 0:1]).then_inc(x1_recip, 1)
                dve.wait_ge(x1_recip, q + 1)
                dve.tensor_scalar(xn2[:, a, :], x1[:, a, :], rs_x[:, 0:1], None, ALU.mult).then_inc(xn2_ready, 1)

            def h2_out(p):
                g = group(p)
                for i in range(1, 4, 2):
                    n = 4 * p + i
                    dve.wait_ge(t2_ready[n % 2], n // 2 + 1)
                    for c in range(2):
                        k = 2 * i + c
                        last = dve.tensor_scalar(h2_t[:, p % 2, k, :], bank(4 + n % 2)[:, 256 * c:256 * (c + 1)], a2[:, k, g:g + 1],
                                                 mod[:, SHIFT2 + k, g:g + 1], ALU.mult, ALU.add)
                    last.then_inc(t2_free[n % 2], 1)

            dve.wait_ge(gate_rows_copied, 4)
            dve.wait_ge(scale_ready, 2)
            gate_mix(0)
            norm_x1(0)
            gate_mix(1)
            norm_x1(1)
            for p in range(1, NPAIR):
                gate_mix(2 * p)
                h2_out(p - 1)
                norm_x1(2 * p)
                gate_mix(2 * p + 1)
                norm_x1(2 * p + 1)
            h2_out(NPAIR - 1)

            dve.wait_ge(logits_turned, 1)
            lg = bank(0)[:, 0:NT * NE].rearrange("p (t e) -> p t e", e=NE)
            dve.tensor_reduce(smx[:, 0, :], lg, AX.X, ALU.max).then_inc(router_max, 1)
            dve.wait_ge(router_max, 1)
            dve.tensor_tensor(aff[:, :, :], lg, smx[:, 0, :].unsqueeze(2).to_broadcast([P, NT, NE]), ALU.subtract).then_inc(router_shifted, 1)
            dve.wait_ge(router_exp, 1)
            dve.tensor_reduce(smx[:, 1, :], aff[:, :, :], AX.X, ALU.add).then_inc(router_sum, 1)
            dve.wait_ge(router_sum, 1)
            dve.reciprocal(smx[:, 2, :], smx[:, 1, :]).then_inc(router_inv, 1)
            dve.wait_ge(router_inv, 1)
            dve.tensor_tensor(aff[:, :, :], aff[:, :, :], smx[:, 2, :].unsqueeze(2).to_broadcast([P, NT, NE]), ALU.mult).then_inc(aff_ready, 1)
            for i in range(2):
                dve.wait_ge(aff_turned, i + 1)
                dve.tensor_copy(aff_p[:, 512 * i:512 * i + 512], bank(1 + i)[0:NE, :]).then_inc(aff_copied, 1)
            dve.wait_ge(aff_turned, 3)
            dve.tensor_copy(aff_s[:, :], bank(3)[0:NE, 0:SS_TOK]).then_inc(aff_copied, 1)
            dve.wait_ge(aff_copied, 3)

            def top_eight(vals, top, idx, r, step):
                if r:
                    dve.wait_ge(step, 3 * r)
                dve.max(top[:, 0, 8 * r:8 * r + 8], vals[:, :]).then_inc(step, 1)
                dve.wait_ge(step, 3 * r + 1)
                dve.max_index(idx[:, 8 * r:8 * r + 8], top[:, 0, 8 * r:8 * r + 8], vals[:, :]).then_inc(step, 1)
                dve.wait_ge(step, 3 * r + 2)
                dve.match_replace(vals[:, :], top[:, 0, 8 * r:8 * r + 8], vals[:, :], LOWEST).then_inc(step, 1)

            for r in range(CAP_P // 8):
                top_eight(aff_p, top_p, idx_p, r, top_p_step)
                if r < CAP_S // 8:
                    top_eight(aff_s, top_s, idx_s, r, top_s_step)
            dve.wait_ge(top_p_step, 3 * CAP_P // 8)
            dve.wait_ge(top_s_step, 3 * CAP_S // 8)
            dve.tensor_copy(top_p[:, 1, :], idx_p[:, :]).then_inc(top_float, 2)
            dve.tensor_copy(top_s[:, 1, :], idx_s[:, :]).then_inc(top_float, 2)
            dve.wait_ge(top_turned, 1)
            dve.tensor_copy(g_top_p[:, 0:NE], bank(0)[:, 0:NE]).then_inc(top_ready, 1)
            dve.tensor_copy(i_top_p[:, 0:NE], bank(0)[:, NE:2 * NE]).then_inc(top_ready, 1)
            dve.tensor_copy(g_top_s[0:CAP_S, 0:NE], bank(0)[0:CAP_S, 2 * NE:3 * NE]).then_inc(top_ready, 1)
            dve.tensor_copy(i_top_s[0:CAP_S, 0:NE], bank(0)[0:CAP_S, 3 * NE:4 * NE]).then_inc(top_ready, 1)

            def tokens_out(e, n0):
                for k in range(KC):
                    dve.wait_ge(d_ready, n0 + k + 1)
                    b = bank(4 + k % 2)
                    dve.tensor_scalar(xe_t[:, k, 0:CAP_P], b[:, 0:CAP_P], a2[:, k, 0:1], mod[:, SHIFT2 + k, 0:1], ALU.mult, ALU.add)
                    dve.tensor_scalar(xe_t[:, k, CAP_P:CAP], b[:, CAP_P:CAP], a2[:, k, 1:2], mod[:, SHIFT2 + k, 1:2],
                                      ALU.mult, ALU.add).then_inc(d_free, 1)

            dve.sem_inc(hid_ready, 2)
            dve.sem_inc(d_free, 2)
            tokens_out(0, 0)
            with dve.Fori(0, NE) as e:
                for m in range(KC):
                    dve.wait_ge(silu_done, e * KC + m + 1)
                    dve.wait_ge(up_ready, e * KC + m + 1)
                    dve.tensor_tensor(hid[:, m, :], sil[:, m % 2, :], bank(2 + m % 2)[:, 0:CAP], ALU.mult).then_inc(hid_ready, 1)
                for m in range(KC):
                    dve.wait_ge(d_ready, 2 * KC * e + KC + m + 1)
                    b = bank(4 + m % 2)
                    dve.tensor_scalar(y_t[:, m, 0:CAP_P], b[:, 0:CAP_P], mod[:, GATE2 + m, 0:1], None, ALU.mult)
                    dve.tensor_scalar(y_t[:, m, CAP_P:CAP], b[:, CAP_P:CAP], mod[:, GATE2 + m, 1:2], None, ALU.mult).then_inc(d_free, 1)
                tokens_out(e + 1, 2 * KC * (e + 1))


def rope_tables():
    pos = np.arange(SP_TOK)
    inv = (10000.0 ** (-np.arange(0, HD // 2, 2, dtype=np.float32) / np.float32(HD // 2))).astype(np.float32)
    row = (pos // 64).astype(np.float32)
    col = (pos % 64).astype(np.float32)
    ang = np.concatenate([row[:, None] * inv, col[:, None] * inv], axis=-1)
    return np.cos(ang).astype(np.float32), np.sin(ang).astype(np.float32)


_INS = ["x_prompt", "x_sample", "c_prompt", "c_sample", "ada_w", "ada_b", "norm_mix", "w_in", "q_norm", "k_norm",
        "conv_w", "conv_b", "conv_ln_g", "conv_ln_b", "w_out", "norm_ffn", "w_router", "w_gate", "w_up", "w_down"]


def kernel(**inputs):
    import concourse.bacc as bacc
    from concourse.bass_utils import run_bass_kernel_spmd

    nc = bacc.Bacc("TRN2", target_bir_lowering=False, num_devices=1)
    arrays, args = {}, []
    for name in _INS:
        arrays[f"in_{name}"] = np.ascontiguousarray(inputs[name])
    arrays["in_rope_cos"], arrays["in_rope_sin"] = rope_tables()
    for name, a in arrays.items():
        args.append(nc.dram_tensor(name, a.shape, mybir.dt.from_np(a.dtype), kind="ExternalInput").ap())
    for name, shape in (("out_prompt", (1, SP_TOK, D)), ("out_sample", (1, SS_TOK, D))):
        args.append(nc.dram_tensor(name, shape, F32, kind="ExternalOutput").ap())
    encoder_layer(nc, *args)
    r = run_bass_kernel_spmd(nc, [arrays], core_ids=[0])
    return r.results[0]["out_prompt"], r.results[0]["out_sample"]
```

```python
from contextlib import ExitStack

import numpy as np

import concourse.bass as bass
from concourse import mybir

F32 = mybir.dt.float32
F32R = mybir.dt.float32r
U32 = mybir.dt.uint32
ACT = mybir.ActivationFunctionType
ALU = mybir.AluOpType
AX = mybir.AxisListType

P = 128
D = 1024
KC = D // P
SP_TOK, SS_TOK = 1024, 256
TOK = SP_TOK + SS_TOK
NT = TOK // P
NPAIR = NT // 2
HD = 64
NH = 8
NKV = 2
QPK = NH // NKV
DA = NH * HD
DKV = NKV * HD
DC = D - DA
CC = DC // P
TAPS = 31
PAD = TAPS // 2
D_IN = DA + 2 * DKV + 2 * DC
NQKV = DA + 2 * DKV
NE = 16
CAP_P = 2 * SP_TOK // NE
CAP_S = 2 * SS_TOK // NE
CAP = CAP_P + CAP_S
EPS = 1e-6
LOWEST = -1.0

A_PROMPT = PAD
A_SAMPLE = PAD + SP_TOK + 2 * PAD
A_LEN = A_SAMPLE + SS_TOK + PAD
A_ROW = A_LEN + 4
C_SAMPLE = SP_TOK + 2 * PAD
C_LEN = C_SAMPLE + SS_TOK
TAPS_FIRST = 7
TAPS_STEP = (TAPS - TAPS_FIRST) // (SP_TOK // P)

SHIFT1, SCALE1, GATE1, SHIFT2, SCALE2, GATE2 = (i * KC for i in range(6))
ADA_BLOCK = 512
ADA_FIRST = 2 * D // ADA_BLOCK
ADA_BLOCKS = 6 * D // ADA_BLOCK

ROW_C, ROW_NMIX, ROW_NFFN, ROW_CB, ROW_LG, ROW_LB, ROW_AB = 0, 16, 24, 32, 36, 40, 44
ROWS = ROW_AB + 48


def encoder_layer(nc, x_p, x_s, c_p, c_s, ada_w, ada_b, norm_mix, w_in, q_norm, k_norm, conv_w, conv_b,
                  ln_g, ln_b, w_out, norm_ffn, w_router, w_gate, w_up, w_down, rope_cos, rope_sin,
                  y_p, y_s):
    xn_p = nc.dram_tensor("xn_prompt", (SP_TOK, D), F32).ap()
    xn_s = nc.dram_tensor("xn_sample", (SS_TOK, D), F32).ap()

    base = 16512
    small = base
    Z1 = small + 16384
    Z2 = Z1 + 81920
    Z3 = Z2 + 93184
    at = {"small": small}

    def put(name, shape, dt, offset):
        return nc.alloc_sbuf_tensor_at(name, shape, dt, offset=offset)

    def keep(name, shape, dt=F32):
        n = int(np.prod(shape[1:])) * 4
        t = put(name, shape, dt, at["small"])
        at["small"] += (n + 31) // 32 * 32
        assert at["small"] <= Z1
        return t

    ident = keep("ident", [P, P])
    ones = keep("ones", [P, P])
    cols = keep("cols", [P, ROWS])
    taps = keep("taps", [P, CC, TAPS])
    silu_c = keep("silu_c", [P, 2 * KC])
    mod = keep("mod", [P, 6 * KC, 2])
    a1 = keep("a1", [P, KC, 2])
    a2 = keep("a2", [P, KC, 2])
    ss_x = keep("ss_x", [P, 2])
    rt_x = keep("rt_x", [P, 2])
    rs_x = keep("rs_x", [P, 2])
    ss_q = keep("ss_q", [P, 2, 10])
    rt_q = keep("rt_q", [P, 2, 10])
    rs_q = keep("rs_q", [P, 2, 10])
    negmax = keep("negmax", [P, 4])
    router = keep("router", [P, KC, NE])
    eps_col = keep("eps_col", [P, 1])
    g_top_p = keep("g_top_p", [P, NE])
    g_top_s = keep("g_top_s", [P, NE])
    i_top_p = keep("i_top_p", [P, NE], U32)
    i_top_s = keep("i_top_s", [P, NE], U32)
    i_now = keep("i_now", [P, 4], U32)
    smx = keep("smx", [P, 3, NT])
    mod_rows = keep("mod_rows", [2, 2, ADA_BLOCK])
    rope_c = put("rope_c", [P, 8, 2, HD], F32, at["small"])
    rope_s = put("rope_s", [P, 8, 2, HD], F32, at["small"] + 4096)
    gate1_row = put("gate1_row", [P, 2, D], F32, at["small"])
    assert at["small"] + 8192 <= Z1, at["small"] + 8192 - Z1

    x_in = put("x_in", [P, 2, D], F32, Z1)
    h_t = put("h_t", [P, 2, KC, 2 * P], F32, Z1 + 8192)
    w_in_sb = put("w_in_sb", [P, KC, D_IN], F32, Z1 + 24576)
    ada = [put(f"ada{i}", [P, KC, ADA_BLOCK], F32, Z2 + 16384 * i) for i in range(3)]
    rows = put("rows", [ROWS, P], F32, Z3)
    taps_row = put("taps_row", [TAPS, DC], F32, Z3 + 512)
    gains = put("gains", [P, 2, HD], F32, Z3 + 2560)
    ngains = put("ngains", [P, 2, HD], F32, Z3 + 3072)
    cos_sb = put("cos_sb", [P, 8, HD // 2], F32, Z1 + 16384)
    sin_sb = put("sin_sb", [P, 8, HD // 2], F32, Z1 + 17408)
    q_st = put("q_st", [P, NT, NH, P], F32R, Z2)
    k_hi = put("k_hi", [P, NKV, TOK], F32R, Z2 + 40960)
    k_lo = put("k_lo", [P, NKV, TOK], F32R, Z2 + 51200)
    v_one = put("v_one", [P, NT, NKV, HD + 1], F32, Z2 + 61440)
    a_t = put("a_t", [P, CC, A_ROW], F32, Z2 + 71680)
    junk = put("junk", [P, D], F32, Z3 + 4096)
    qk = [put(f"qk{i}", [P, 10, HD], F32, Z3 + 8192 + 2560 * i) for i in range(2)]
    sq = put("sq", [P, 10, HD], F32, Z3 + 13312)
    rot1 = sq
    rot2 = put("rot2", [P, 10, HD], F32, Z3 + 15872)
    sig = put("sig", [P, 2, 2 * P], F32, Z3 + 18432)
    ada2 = [put(f"ada2_{i}", [P, KC, ADA_BLOCK], F32, Z1 + 32768 + 16384 * i) for i in range(3)]
    diag = put("diag", [P, 2, 4, P], F32, Z1 + 32768)
    c_t = put("c_t", [P, CC, C_LEN], F32, Z3)
    w_out_sb = put("w_out_sb", [P, KC, D], F32, Z1)
    probs = put("probs", [P, 2, SP_TOK], F32, Z1 + 32768)
    probs_t = put("probs_t", [P, KC, QPK, P], F32, Z1 + 40960)
    mix_t = put("mix_t", [P, CC, TOK], F32, Z1 + 57344)
    q_now = put("q_now", [P, 2, P], F32R, Z1 + 77824)
    out_rows = put("out_rows", [P, QPK, HD], F32, Z1 + 78848)
    rsum = put("rsum", [P, QPK, 1], F32, Z1 + 79872)
    sq_c = put("sq_c", [P, CC, 512], F32, Z1 + 32768)
    rt_c = put("rt_c", [P, 512], F32, Z1 + 40960)
    rs_c = put("rs_c", [P, 512], F32, Z1 + 43008)
    x_again = put("x_again", [P, 2, D], F32, Z1 + 32768)
    x1 = put("x1", [P, 2, D], F32, Z1 + 40960)
    xn2 = put("xn2", [P, 2, D], F32, Z1 + 49152)
    h2_t = put("h2_t", [P, 2, KC, 2 * P], F32, Z2 + 65536)
    logits_t = put("logits_t", [NE, TOK], F32, Z2 + 81920)
    aff = put("aff", [P, NT, NE], F32, Z3)
    aff_p = put("aff_p", [NE, SP_TOK], F32, Z3 + 1024)
    aff_s = put("aff_s", [NE, SS_TOK], F32, Z3 + 5120)
    top_p = put("top_p", [NE, 2, CAP_P], F32, Z3 + 6144)
    top_s = put("top_s", [NE, 2, CAP_S], F32, Z3 + 7168)
    idx_p = put("idx_p", [NE, CAP_P], U32, Z3 + 7680)
    idx_s = put("idx_s", [NE, CAP_S], U32, Z3 + 8192)
    MC = 256
    NS = D // MC
    gate_w_sb = put("gate_w_sb", [P, NS, KC, MC], F32, Z2)
    up_w_sb = put("up_w_sb", [P, NS, KC, MC], F32, Z2 + 32768)
    down_w_sb = put("down_w_sb", [P, NS, KC, MC], F32, Z1)
    xg_p = put("xg_p", [CAP_P, D], F32, Z1 + 32768)
    xg_s = put("xg_s", [CAP_S, D], F32, Z1 + 36864)
    ye_p = put("ye_p", [CAP_P, D], F32, Z1 + 40960)
    ye_s = put("ye_s", [CAP_S, D], F32, Z1 + 45056)
    xe_t = put("xe_t", [P, KC, CAP], F32, Z1 + 49152)
    hid = put("hid", [P, KC, CAP], F32, Z1 + 54272)
    y_t = put("y_t", [P, KC, CAP], F32, Z1 + 59392)
    sil = put("sil", [P, 2, CAP], F32, Z1 + 64512)

    with ExitStack() as ctx:
        two = [ctx.enter_context(nc.psum_tensor(f"banks{2 * i}", [P, 2, 512], F32)) for i in range(4)]

        def bank(k):
            return two[k // 2][:, k % 2, :]

        def sem(name):
            return ctx.enter_context(nc.semaphore(name))

        rows_loaded = sem("rows_loaded")
        gains_loaded = sem("gains_loaded")
        router_loaded = sem("router_loaded")
        ada_loaded = [sem(f"ada_loaded{i}") for i in range(3)]
        wu_loaded = sem("wu_loaded")
        wqkv_loaded = sem("wqkv_loaded")
        w_out_loaded = sem("w_out_loaded")
        x_loaded = sem("x_loaded")
        ident_made = sem("ident_made")
        fills_made = sem("fills_made")
        cols_turned = sem("cols_turned")
        cols_ready = sem("cols_ready")
        silu_ready = sem("silu_ready")
        rows_ready = sem("rows_ready")
        rows_copied = sem("rows_copied")
        rows_turned = sem("rows_turned")
        mod_turned = sem("mod_turned")
        mod_ready = sem("mod_ready")
        scale_ready = sem("scale_ready")
        gains_scaled = sem("gains_scaled")
        tables_ready = sem("tables_ready")
        x_squared = sem("x_squared")
        x_root = sem("x_root")
        x_recip = sem("x_recip")
        x_normed = sem("x_normed")
        t_ready = [sem(f"t_ready{i}") for i in range(2)]
        t_free = [sem(f"t_free{i}") for i in range(2)]
        u_ready = sem("u_ready")
        sig_ready = sem("sig_ready")
        u_gated = sem("u_gated")
        qkv_ready = sem("qkv_ready")
        qkv_copied = sem("qkv_copied")
        sq_ready = sem("sq_ready")
        sq_summed = sem("sq_summed")
        q_root = sem("q_root")
        q_recip = sem("q_recip")
        q_normed = sem("q_normed")
        rot1_ready = sem("rot1_ready")
        rot2_ready = sem("rot2_ready")
        rotated = sem("rotated")
        high_ready = sem("high_ready")
        diag_ready = sem("diag_ready")
        gate_rows_ready = sem("gate_rows_ready")
        gate_rows_copied = sem("gate_rows_copied")
        conv_done = [sem(f"conv_done{c}") for c in range(CC)]
        q_copied = sem("q_copied")
        scores_ready = sem("scores_ready")
        max_ready = sem("max_ready")
        probs_ready = sem("probs_ready")
        turned = sem("turned")
        turn_bank_free = sem("turn_bank_free")
        weighed = sem("weighed")
        sums_inverted = sem("sums_inverted")
        out_divided = sem("out_divided")
        out_turned = sem("out_turned")
        out_copied = sem("out_copied")
        mean_ready = sem("mean_ready")
        centred = sem("centred")
        squared = sem("squared")
        var_ready = sem("var_ready")
        root_ready = sem("root_ready")
        inv_ready = sem("inv_ready")
        scaled = sem("scaled")
        conv_out = sem("conv_out")
        x_reloaded = sem("x_reloaded")
        mix_ready = sem("mix_ready")
        mix_gated = sem("mix_gated")
        x1_ready = sem("x1_ready")
        x1_squared = sem("x1_squared")
        x1_root = sem("x1_root")
        x1_recip = sem("x1_recip")
        xn2_ready = sem("xn2_ready")
        y_stored = [sem(f"y_stored{a}") for a in range(2)]
        xn_stored = [sem(f"xn_stored{a}") for a in range(2)]
        t2_ready = [sem(f"t2_ready{i}") for i in range(2)]
        t2_free = [sem(f"t2_free{i}") for i in range(2)]
        logits_ready = sem("logits_ready")
        logits_copied = sem("logits_copied")
        logits_turned = sem("logits_turned")
        router_max = sem("router_max")
        router_shifted = sem("router_shifted")
        router_exp = sem("router_exp")
        router_sum = sem("router_sum")
        router_inv = sem("router_inv")
        aff_ready = sem("aff_ready")
        aff_turned = sem("aff_turned")
        aff_copied = sem("aff_copied")
        top_p_step = sem("top_p_step")
        top_s_step = sem("top_s_step")
        top_float = sem("top_float")
        top_turned = sem("top_turned")
        top_ready = sem("top_ready")
        gate_w_loaded = [sem(f"gate_w_loaded{i}") for i in range(NS)]
        up_w_loaded = [sem(f"up_w_loaded{i}") for i in range(NS)]
        down_w_loaded = [sem(f"down_w_loaded{i}") for i in range(NS)]
        idx_copied = sem("idx_copied")
        gathered = sem("gathered")
        gate_ready = sem("gate_ready")
        up_ready = sem("up_ready")
        silu_done = sem("silu_done")
        hid_ready = sem("hid_ready")
        x_turned = sem("x_turned")
        x_scaled = sem("x_scaled")
        down_ready = sem("down_ready")
        y_scaled = sem("y_scaled")
        y_turned = sem("y_turned")
        ye_ready = sem("ye_ready")
        scattered = sem("scattered")
        ye_free = sem("ye_free")
        act_steps = sem("act_steps")
        pool_steps = sem("pool_steps")

        turn_at = {}
        n_turns = [0]

        def order(key, uses):
            turn_at[key] = n_turns[0]
            n_turns[0] += uses

        order(("x", 0), 4)
        for p in range(NPAIR):
            if p:
                order(("q", p - 1, 1), 3)
            if p + 1 < NPAIR:
                order(("x", p + 1), 4)
            order(("q", p, 0), 3)
        order(("q", NPAIR - 1, 1), 3)

        def group(p):
            return 1 if p == NPAIR - 1 else 0

        def x_rows(p):
            src = x_s[0] if group(p) else x_p[0, 2 * P * p:2 * P * (p + 1), :]
            return src.rearrange("(a q) d -> q a d", q=P)

        def a_cols(p):
            return A_SAMPLE if group(p) else A_PROMPT + 2 * P * p

        def attention_phases():
            n = 0
            for j in range(NKV):
                for t0, nt in ((0, SP_TOK // P), (SP_TOK // P, SS_TOK // P)):
                    yield j, t0, nt, n
                    n += nt

        phases = list(attention_phases())
        STEPS = sum(ph[2] for ph in phases)
        HEADS_ALL = STEPS * QPK

        def steps_of(eng, nt, step):
            step(0, True, False)
            if nt > 2:
                with eng.Fori(1, nt - 1) as r:
                    step(r, False, False)
            step(nt - 1, False, True)

        def last_tile(i, l, first):
            j, t0, _, s0 = phases[i]
            if first:
                pj, pt0, pnt, _ = phases[i - 1]
                return s0 - 1, pt0 + pnt - 1, pj
            return l + (s0 - 1), l + (t0 - 1), j

        def conv_slices(c, k):
            return a_t[:, c, k:k + C_LEN]

        block = ctx.enter_context(nc.Block())

        @block.sync
        def _(sp):
            for r, src, n in ((ROW_C, c_p[0], KC), (ROW_C + KC, c_s[0], KC), (ROW_NMIX, norm_mix[0], KC),
                              (ROW_NFFN, norm_ffn[0], KC), (ROW_CB, conv_b[0], CC), (ROW_LG, ln_g[0], CC),
                              (ROW_LB, ln_b[0], CC), (ROW_AB, ada_b[0], 6 * KC)):
                sp.dma_start(rows[r:r + n, :], src.rearrange("(k q) -> k q", q=P)).then_inc(rows_loaded, 16)
            sp.dma_start(taps_row[:, :], conv_w[0, :, 0, :]).then_inc(rows_loaded, 16)
            sp.dma_start(x_in[:, :, :], x_rows(0)).then_inc(x_loaded, 16)
            ada_view = ada_w[0].rearrange("(k q) (b n) -> b q k n", q=P, n=ADA_BLOCK)
            for b in range(ADA_FIRST):
                if b >= 3:
                    sp.wait_ge(rows_ready, b - 2)
                sp.dma_start(ada[b % 3][:, :, :], ada_view[b]).then_inc(ada_loaded[b % 3], 16)
                if b == 0:
                    sp.dma_start(gains[:, 0, :], q_norm[0].partition_broadcast(P)).then_inc(gains_loaded, 16)
                    sp.dma_start(gains[:, 1, :], k_norm[0].partition_broadcast(P)).then_inc(gains_loaded, 16)
                    sp.dma_start(cos_sb[:, :, :], rope_cos.rearrange("(t q) i -> q t i", q=P)).then_inc(gains_loaded, 16)
                    sp.dma_start(sin_sb[:, :, :], rope_sin.rearrange("(t q) i -> q t i", q=P)).then_inc(gains_loaded, 16)
            w_view = w_in[0].rearrange("(k q) n -> q k n", q=P)
            sp.dma_start(w_in_sb[:, :, NQKV:], w_view[:, :, NQKV:]).then_inc(wu_loaded, 16)
            sp.dma_start(w_in_sb[:, :, 0:NQKV], w_view[:, :, 0:NQKV]).then_inc(wqkv_loaded, 16)
            sp.dma_start(router[:, :, :], w_router[0].rearrange("(k q) e -> q k e", q=P)).then_inc(router_loaded, 16)
            for p in range(1, NPAIR):
                n = turn_at["x", p - 1] + 3
                sp.wait_ge(t_ready[n % 2], n // 2 + 1)
                sp.dma_start(x_in[:, :, :], x_rows(p)).then_inc(x_loaded, 16)
            sp.wait_ge(qkv_ready, 2 * NT)
            for b in range(ADA_FIRST, ADA_BLOCKS):
                i = b - ADA_FIRST
                if i >= 3:
                    sp.wait_ge(rows_ready, b - 2)
                sp.dma_start(ada2[i % 3][:, :, :], ada_view[b]).then_inc(ada_loaded[i % 3], 16)
            sp.dma_start(w_out_sb[:, :, :], w_out[0].rearrange("(k q) n -> q k n", q=P)).then_inc(w_out_loaded, 16)
            gate_view = w_gate[0].rearrange("e (k q) (s n) -> e s q k n", q=P, n=MC)
            up_view = w_up[0].rearrange("e (k q) (s n) -> e s q k n", q=P, n=MC)
            down_view = w_down[0].rearrange("e (k q) (s n) -> e s q k n", q=P, n=MC)
            for p in range(NPAIR):
                if p == 0:
                    sp.wait_ge(conv_out, 3 * CC)
                    sp.wait_ge(out_copied, STEPS + 1)
                else:
                    sp.wait_ge(x1_ready, 2 * p)
                sp.dma_start(x_again[:, :, :], x_rows(p)).then_inc(x_reloaded, 16)
                if p == 0:
                    for s in range(NS):
                        sp.dma_start(gate_w_sb[:, s], gate_view[0, s]).then_inc(gate_w_loaded[s], 16)
                        sp.dma_start(up_w_sb[:, s], up_view[0, s]).then_inc(up_w_loaded[s], 16)
                for a in range(2):
                    q = 2 * p + a
                    dst_y = y_s[0] if group(p) else y_p[0, 2 * P * p:2 * P * (p + 1)]
                    dst_n = xn_s if group(p) else xn_p[2 * P * p:2 * P * (p + 1)]
                    sp.wait_ge(x1_ready, q + 1)
                    sp.dma_start(dst_y[P * a:P * (a + 1), :], x1[:, a, :]).then_inc(y_stored[a], 16)
                    sp.wait_ge(xn2_ready, q + 1)
                    sp.dma_start(dst_n[P * a:P * (a + 1), :], xn2[:, a, :]).then_inc(xn_stored[a], 16)
            sp.wait_ge(mix_ready, NT)
            for s in range(NS):
                sp.dma_start(down_w_sb[:, s], down_view[0, s]).then_inc(down_w_loaded[s], 16)
            with sp.Fori(1, NE) as e:
                for s in range(NS):
                    m = 2 * s + 1
                    sp.wait_ge(gate_ready, (e - 1) * KC + m + 1)
                    sp.dma_start(gate_w_sb[:, s], gate_view[e, s]).then_inc(gate_w_loaded[s], 16)
                    sp.wait_ge(up_ready, (e - 1) * KC + m + 1)
                    sp.dma_start(up_w_sb[:, s], up_view[e, s]).then_inc(up_w_loaded[s], 16)
                for s in range(NS):
                    m = 2 * s + 1
                    sp.wait_ge(down_ready, (e - 1) * KC + m + 1)
                    sp.dma_start(down_w_sb[:, s], down_view[e, s]).then_inc(down_w_loaded[s], 16)

        @block.gpsimd
        def _(pool):
            pool.memset(ident[:, :], 0.0).then_inc(ident_made, 1)
            pool.memset(ones[:, :], 1.0).then_inc(fills_made, 1)
            pool.memset(eps_col[:, :], EPS).then_inc(fills_made, 1)
            pool.wait_ge(ident_made, 1)
            pool.affine_select(out=ident[:, :], in_=ident[:, :], compare_op=ALU.not_equal, fill=1.0,
                               base=0, pattern=[[-1, P]], channel_multiplier=1).then_inc(ident_made, 1)
            pool.memset(a_t[:, :, 0:A_PROMPT], 0.0).then_inc(fills_made, 1)
            pool.memset(a_t[:, :, A_PROMPT + SP_TOK:A_SAMPLE], 0.0).then_inc(fills_made, 1)
            pool.memset(a_t[:, :, A_SAMPLE + SS_TOK:A_ROW], 0.0).then_inc(fills_made, 1)
            pool.memset(v_one[:, :, :, HD:HD + 1], 1.0).then_inc(fills_made, 1)

            for q in range(NT):
                a = q % 2
                pool.wait_ge(qkv_copied, 2 * q + 2)
                if q:
                    pool.wait_ge(rotated, q)
                pool.tensor_tensor(sq[:, :, :], qk[a][:, :, :], qk[a][:, :, :], ALU.mult).then_inc(sq_ready, 1)
                pool.wait_ge(q_normed, q + 1)
                even = qk[a][:, :, :].rearrange("p h (i b) -> p h i b", b=2)
                out = rot2[:, :, :].rearrange("p h (i b) -> p h i b", b=2)
                tab = rope_s[:, q % 8, :, :].rearrange("p g (i b) -> p g i b", b=2)
                for b in range(2):
                    for g, h0, nh in ((0, 0, NH), (1, NH, NKV)):
                        t = tab[:, g:g + 1, :, b].to_broadcast([P, nh, HD // 2])
                        last = pool.tensor_tensor(out[:, h0:h0 + nh, :, b], even[:, h0:h0 + nh, :, 1 - b], t, ALU.mult)
                last.then_inc(rot2_ready, 1)

            for n in (n_turns[0] - 2, n_turns[0] - 1):
                pool.wait_ge(t_free[n % 2], n // 2 + 1)
            pool.wait_ge(rows_ready, ADA_BLOCKS)

            def copy_q(n, h, t, head):
                if n is not None:
                    pool.wait_ge(scores_ready, n - 1)
                pool.tensor_copy(q_now[:, h % 2, :], q_st[:, t, head, :]).then_inc(q_copied, 1)

            j0, t0, _, _ = phases[0]
            copy_q(None, 0, t0, j0 * QPK)
            copy_q(None, 1, t0, j0 * QPK + 1)
            for i, (j, t0, nt, s0) in enumerate(phases):
                follow = (phases[i + 1][0], phases[i + 1][1]) if i + 1 < len(phases) else None

                def ahead(l, first, last):
                    n = (l + s0) * QPK
                    copy_q(n + 2, 2, l + t0, j * QPK + 2)
                    copy_q(n + 3, 3, l + t0, j * QPK + 3)
                    nxt = follow if last else (j, l + (t0 + 1))
                    if nxt is not None:
                        nj, tile = nxt
                        copy_q(n + 4, 0, tile, nj * QPK)
                        copy_q(n + 5, 1, tile, nj * QPK + 1)
                steps_of(pool, nt, ahead)

            for q in range(NT):
                p, a = q // 2, q % 2
                pool.wait_ge(x_reloaded, 16 * (p + 1))
                pool.wait_ge(mix_gated, q + 1)
                pool.tensor_tensor(x1[:, a, :], x1[:, a, :], x_again[:, a, :], ALU.add).then_inc(x1_ready, 1)

            def fetch(e, n):
                pool.tensor_copy(i_now[:, 0:1], i_top_p[:, bass.ds(e, 1)]).then_inc(idx_copied, 1)
                pool.tensor_copy(i_now[0:CAP_S, 1:2], i_top_s[0:CAP_S, bass.ds(e, 1)]).then_inc(idx_copied, 1)
                pool.wait_ge(idx_copied, n)
                pool.sem_inc(pool_steps, 1)
                pool.indirect_dma_start(xg_p[:, :], None, xn_p, bass.IndirectOffsetOnAxis(i_now[:, 0:1], axis=0)).then_inc(gathered, 16)
                pool.indirect_dma_start(xg_s[:, :], None, xn_s, bass.IndirectOffsetOnAxis(i_now[0:CAP_S, 1:2], axis=0)).then_inc(gathered, 16)

            pool.wait_ge(top_ready, 4)
            pool.wait_ge(fills_made, 6)
            for a in range(2):
                pool.wait_ge(xn_stored[a], 16 * NPAIR)
                pool.wait_ge(y_stored[a], 16 * NPAIR)
            pool.sem_inc(ye_free, 1)
            fetch(0, 2)

            def expert(e, more):
                if more:
                    pool.wait_ge(x_turned, KC * e + KC)
                    fetch(e + 1, 4 * e + 4)
                pool.tensor_copy(i_now[:, 2:3], i_top_p[:, bass.ds(e, 1)]).then_inc(idx_copied, 1)
                pool.tensor_copy(i_now[0:CAP_S, 3:4], i_top_s[0:CAP_S, bass.ds(e, 1)]).then_inc(idx_copied, 1)
                pool.wait_ge(idx_copied, 4 * e + (6 if more else 4))
                pool.wait_ge(ye_ready, 4 * e + 5)
                pool.sem_inc(pool_steps, 1)
                pool.indirect_dma_start(y_p[0], bass.IndirectOffsetOnAxis(i_now[:, 2:3], axis=0), ye_p[:, :], None,
                                        compute_op=ALU.add).then_inc(scattered, 16)
                pool.indirect_dma_start(y_s[0], bass.IndirectOffsetOnAxis(i_now[0:CAP_S, 3:4], axis=0), ye_s[:, :], None,
                                        compute_op=ALU.add).then_inc(scattered, 16)
                pool.wait_ge(scattered, 32 * e + 32)
                pool.sem_inc(ye_free, 1)

            with pool.Fori(0, NE - 1) as e:
                expert(e, True)
            expert(NE - 1, False)

        @block.scalar
        def _(act):
            act.wait_ge(cols_ready, 1)
            act.activation(silu_c[:, :], cols[:, ROW_C:ROW_C + 2 * KC], ACT.Silu).then_inc(silu_ready, 1)

            def copy_rows(b):
                act.wait_ge(rows_ready, b + 1)
                if b >= 2:
                    act.wait_ge(rows_turned, b - 1)
                act.activation(mod_rows[:, b % 2, :], bank(2 + b % 2)[0:2, :], ACT.Copy).then_inc(rows_copied, 1)

            for b in range(ADA_FIRST):
                copy_rows(b)

            def square_x(p):
                act.wait_ge(x_loaded, 16 * (p + 1))
                if p:
                    act.wait_ge(x_recip, p)
                for a in range(2):
                    if p or a:
                        act.wait_ge(x_squared, 2 * p + a)
                    act.activation(junk[:, :], x_in[:, a, :], ACT.Square, accum_out=ss_x[:, a:a + 1]).then_inc(x_squared, 1)
                act.wait_ge(x_squared, 2 * p + 2)
                act.activation(rt_x[:, :], ss_x[:, :], ACT.Sqrt, scale=1.0 / D, bias=eps_col[:, :]).then_inc(x_root, 1)

            def x_out(p):
                for i in range(0, 4, 2):
                    n = turn_at["x", p] + i
                    act.wait_ge(t_ready[n % 2], n // 2 + 1)
                    for c in range(2):
                        k = 2 * i + c
                        last = act.activation(h_t[:, p % 2, k, :], bank(n % 2)[:, 256 * c:256 * (c + 1)], ACT.Identity,
                                              scale=a1[:, k, group(p):group(p) + 1],
                                              bias=mod[:, SHIFT1 + k, group(p):group(p) + 1])
                    last.then_inc(t_free[n % 2], 1)

            def high_out(p, a):
                t = 2 * p + a
                for i in range(3):
                    n = turn_at["q", p, a] + i
                    act.wait_ge(t_ready[n % 2], n // 2 + 1)
                    if i < 2:
                        src = bank(n % 2)[0:HD, :].rearrange("d (h q) -> d h q", h=4)
                        last = act.activation(q_st[0:HD, t, 4 * i:4 * i + 4, :], src, ACT.Copy)
                    else:
                        src = bank(n % 2)[0:HD, 0:NKV * P].rearrange("d (j q) -> d j q", j=NKV)
                        act.activation(k_hi[0:HD, :, P * t:P * (t + 1)], src, ACT.Copy)
                        last = act.activation(k_hi[HD:P, :, P * t:P * (t + 1)], src, ACT.Copy)
                    last.then_inc(high_ready, 1)

            def copies(p, a):
                q = 2 * p + a
                if q >= 2:
                    n = turn_at["q", p - 1, a] + 2
                    act.wait_ge(t_ready[n % 2], n // 2 + 1)
                act.wait_ge(qkv_ready, 2 * q + 1)
                act.activation(qk[a][:, 0:NH, :], bank(4 + a).rearrange("p (h d) -> p h d", h=NH), ACT.Copy).then_inc(qkv_copied, 1)
                act.wait_ge(qkv_ready, 2 * q + 2)
                act.activation(qk[a][:, NH:NH + NKV, :], bank(6 + a)[:, 0:DKV].rearrange("p (h d) -> p h d", h=NKV), ACT.Copy)
                act.activation(v_one[:, q, :, 0:HD], bank(6 + a)[:, DKV:2 * DKV].rearrange("p (h d) -> p h d", h=NKV),
                               ACT.Copy).then_inc(qkv_copied, 1)
                act.wait_ge(sq_summed, q + 1)
                act.activation(rt_q[:, a, :], ss_q[:, a, :], ACT.Sqrt, scale=1.0 / HD, bias=eps_col[:, :]).then_inc(q_root, 1)

            act.wait_ge(fills_made, 6)
            square_x(0)
            act.wait_ge(scale_ready, 1)
            x_out(0)
            for p in range(NPAIR):
                if p + 1 < NPAIR:
                    square_x(p + 1)
                for i in range(CC):
                    n = CC * p + i
                    act.wait_ge(u_ready, n + 1)
                    if n >= 2:
                        act.wait_ge(u_gated, n - 1)
                    act.activation(sig[:, n % 2, :], bank(2 + n % 2)[:, 256:512], ACT.Sigmoid).then_inc(sig_ready, 1)
                if p:
                    high_out(p - 1, 1)
                copies(p, 0)
                if p + 1 < NPAIR:
                    x_out(p + 1)
                copies(p, 1)
                high_out(p, 0)
            high_out(NPAIR - 1, 1)

            for b in range(ADA_FIRST, ADA_BLOCKS):
                copy_rows(b)
            for n in range(4):
                act.wait_ge(gate_rows_ready, n + 1)
                act.activation(gate1_row[:, n // 2, 512 * (n % 2):512 * (n % 2) + 512], bank(2 + n % 2), ACT.Copy).then_inc(gate_rows_copied, 1)

            act.sem_inc(turn_bank_free, 2)

            def exponent(n, h, nk):
                act.wait_ge(max_ready, n + 1)
                act.activation(probs[:, h % 2, 0:P * nk], two[h % 2][:, :, :].rearrange("p b n -> p (b n)")[:, 0:P * nk], ACT.Exp,
                               bias=negmax[:, h:h + 1]).then_inc(probs_ready, 1)

            def probs_out(n, h, nk):
                act.wait_ge(weighed, n + 1)
                for half in range(2):
                    act.wait_ge(turned, 2 * n + half + 1)
                    kk = nk // 2
                    act.activation(probs_t[:, kk * half:kk * half + kk, h, :],
                                   bank(4 + half)[:, 0:kk * P].rearrange("p (k q) -> p k q", k=kk), ACT.Copy).then_inc(turn_bank_free, 1)

            def mix_out(step, t, j):
                act.wait_ge(out_turned, step + 1)
                act.sem_inc(act_steps, 1)
                act.activation(mix_t[:, 2 * j:2 * j + 2, bass.ds(t * P, P)], bank(7)[:, 0:2 * P].rearrange("p (c q) -> p c q", c=2),
                               ACT.Copy).then_inc(out_copied, 1)

            exponent(0, 0, phases[0][2])
            for i, (j, t0, nt, s0) in enumerate(phases):
                def soft(l, first, last):
                    n = (l + s0) * QPK
                    nxt_nk = nt if not last else phases[i + 1][2] if i + 1 < len(phases) else None
                    for h in range(QPK):
                        if h + 1 < QPK:
                            exponent(n + h + 1, h + 1, nt)
                        elif nxt_nk is not None:
                            exponent(n + QPK, 0, nxt_nk)
                        probs_out(n + h, h, nt)
                        if h == 2 and not (first and i == 0):
                            mix_out(*last_tile(i, l, first))
                steps_of(act, nt, soft)
            mix_out(*last_tile(len(phases) - 1, phases[-1][2], False))

            for s, (o, n) in enumerate(((0, 512), (512, 512), (C_SAMPLE, SS_TOK))):
                for c in range(CC):
                    act.wait_ge(centred, CC * s + c + 1)
                    if s and c == 0:
                        act.wait_ge(var_ready, s)
                    act.activation(sq_c[:, c, 0:n], c_t[:, c, o:o + n], ACT.Square).then_inc(squared, 1)
                act.wait_ge(var_ready, s + 1)
                act.activation(rt_c[:, 0:n], bank(1)[:, 0:n], ACT.Sqrt, scale=1.0 / DC, bias=eps_col[:, :]).then_inc(root_ready, 1)
            for s, (o, n) in enumerate(((0, 512), (512, 512), (C_SAMPLE, SS_TOK))):
                for c in range(CC):
                    act.wait_ge(scaled, CC * s + c + 1)
                    act.activation(c_t[:, c, o:o + n], c_t[:, c, o:o + n], ACT.Silu, scale=cols[:, ROW_LG + c:ROW_LG + c + 1],
                                   bias=cols[:, ROW_LB + c:ROW_LB + c + 1]).then_inc(conv_out, 1)

            def norm2(q):
                a = q % 2
                act.wait_ge(x1_ready, q + 1)
                if q >= 2:
                    act.wait_ge(xn_stored[a], 16 * (q // 2))
                    act.wait_ge(t2_ready[1], 2 * ((q - 2) // 2) + 2)
                if q:
                    act.wait_ge(x1_recip, q)
                act.activation(xn2[:, a, :], x1[:, a, :], ACT.Square, accum_out=ss_x[:, 0:1]).then_inc(x1_squared, 1)
                act.wait_ge(x1_squared, q + 1)
                act.activation(rt_x[:, 0:1], ss_x[:, 0:1], ACT.Sqrt, scale=1.0 / D, bias=eps_col[:, :]).then_inc(x1_root, 1)

            def h2_out(p):
                for i in range(0, 4, 2):
                    n = 4 * p + i
                    act.wait_ge(t2_ready[n % 2], n // 2 + 1)
                    for c in range(2):
                        k = 2 * i + c
                        last = act.activation(h2_t[:, p % 2, k, :], bank(4 + n % 2)[:, 256 * c:256 * (c + 1)], ACT.Identity,
                                              scale=a2[:, k, group(p):group(p) + 1],
                                              bias=mod[:, SHIFT2 + k, group(p):group(p) + 1])
                    last.then_inc(t2_free[n % 2], 1)

            def logits_out(p):
                act.wait_ge(logits_ready, p + 1)
                act.activation(logits_t[:, 2 * P * p:2 * P * (p + 1)], bank(6)[0:NE, 0:2 * P], ACT.Copy).then_inc(logits_copied, 1)

            for p in range(NPAIR):
                norm2(2 * p)
                norm2(2 * p + 1)
                h2_out(p)
                logits_out(p)

            act.wait_ge(router_shifted, 1)
            act.activation(aff[:, :, :], aff[:, :, :], ACT.Exp).then_inc(router_exp, 1)

            def y_out(e, half):
                act.wait_ge(y_turned, 2 * e + half + 1)
                act.sem_inc(act_steps, 1)
                act.activation(ye_p[:, 512 * half:512 * half + 512], bank(6), ACT.Copy,
                               scale=g_top_p[:, bass.ds(e, 1)]).then_inc(ye_ready, 1)
                act.activation(ye_s[:, 512 * half:512 * half + 512], bank(7)[0:CAP_S, :], ACT.Copy,
                               scale=g_top_s[0:CAP_S, bass.ds(e, 1)]).then_inc(ye_ready, 1)

            act.wait_ge(top_ready, 4)
            act.sem_inc(ye_ready, 1)
            with act.Fori(0, NE) as e:
                for m in range(KC):
                    act.wait_ge(gate_ready, e * KC + m + 1)
                    act.activation(sil[:, m % 2, :], bank(m % 2)[:, 0:CAP], ACT.Silu).then_inc(silu_done, 1)
                act.wait_ge(ye_free, e + 1)
                y_out(e, 0)
                y_out(e, 1)

        @block.tensor
        def _(pe):
            pe.wait_ge(ident_made, 2)
            pe.wait_ge(rows_loaded, 16 * 9)
            pe.transpose(bank(0)[:, 0:ROWS], rows[:, :], ident[0:ROWS, 0:ROWS])
            for c in range(CC):
                last = pe.transpose(bank(0)[:, 128 + TAPS * c:128 + TAPS * (c + 1)], taps_row[:, P * c:P * (c + 1)],
                                    ident[0:TAPS, 0:TAPS])
            last.then_inc(cols_turned, 1)

            silu_pair = silu_c[:, :].rearrange("p (g k) -> p k g", g=2)

            def mod_block(b, w, loads):
                if b == 0:
                    pe.wait_ge(silu_ready, 1)
                if b >= 2:
                    pe.wait_ge(rows_copied, b - 1)
                pe.wait_ge(ada_loaded[loads[0]], 16 * loads[1])
                for k in range(KC):
                    last = pe.matmul(bank(2 + b % 2)[0:2, :], silu_pair[:, k, :], w[:, k, :], start=(k == 0), stop=(k == KC - 1))
                last.then_inc(rows_ready, 1)

            def mod_turn(b):
                pe.wait_ge(rows_copied, b + 1)
                for j in range(4):
                    last = pe.transpose(bank(7)[:, 2 * (4 * b + j):2 * (4 * b + j) + 2], mod_rows[:, b % 2, P * j:P * (j + 1)],
                                        ident[0:2, 0:2])
                last.then_inc(rows_turned, 1)

            for b in range(ADA_FIRST):
                mod_block(b, ada[b % 3], (b % 3, b // 3 + 1))
                if b:
                    mod_turn(b - 1)
            mod_turn(ADA_FIRST - 1)

            def turn_x(p):
                pe.wait_ge(x_normed, 2 * p + 2)
                for i in range(4):
                    n = turn_at["x", p] + i
                    if n >= 2:
                        pe.wait_ge(t_free[n % 2], n // 2)
                    for c in range(2):
                        for a in range(2):
                            last = pe.transpose(bank(n % 2)[:, 256 * c + P * a:256 * c + P * (a + 1)],
                                                x_in[:, a, P * (2 * i + c):P * (2 * i + c + 1)], ident[:, :])
                    last.then_inc(t_ready[n % 2], 1)

            def turn_q(p, a):
                pe.wait_ge(rotated, 2 * p + a + 1)
                for i in range(3):
                    n = turn_at["q", p, a] + i
                    pe.wait_ge(t_free[n % 2], n // 2)
                    for h in range(4 if i < 2 else NKV):
                        last = pe.transpose(bank(n % 2)[0:HD, P * h:P * (h + 1)], qk[a][:, 4 * i + h, :], ident[:, :])
                    last.then_inc(t_ready[n % 2], 1)

            def project_u(p):
                for b in range(2):
                    n = turn_at["x", p] + 2 + b
                    pe.wait_ge(t_free[n % 2], n // 2 + 1)
                for i in range(CC):
                    n = CC * p + i
                    if n >= 2:
                        pe.wait_ge(u_gated, n - 1)
                    for part in range(2):
                        col = NQKV + DC * part + P * i
                        for k in range(KC):
                            last = pe.matmul(bank(2 + n % 2)[:, 256 * part:256 * part + 256], w_in_sb[:, k, col:col + P],
                                             h_t[:, p % 2, k, :], start=(k == 0), stop=(k == KC - 1))
                    last.then_inc(u_ready, 1)

            def project_qkv(p, a):
                q = 2 * p + a
                if q >= 2:
                    pe.wait_ge(qkv_copied, 2 * q - 2)
                for b, c0, n in ((4 + a, 0, DA), (6 + a, DA, 2 * DKV)):
                    for k in range(KC):
                        last = pe.matmul(bank(b)[:, 0:n], h_t[:, p % 2, k, P * a:P * (a + 1)], w_in_sb[:, k, c0:c0 + n],
                                         start=(k == 0), stop=(k == KC - 1))
                    last.then_inc(qkv_ready, 1)

            turn_x(0)
            pe.wait_ge(wu_loaded, 16)
            pe.wait_ge(rows_copied, ADA_FIRST)
            for p in range(NPAIR):
                project_u(p)
                if p:
                    turn_q(p - 1, 1)
                if p == 0:
                    pe.wait_ge(wqkv_loaded, 16)
                    pe.wait_ge(mod_ready, 1)
                project_qkv(p, 0)
                if p + 1 < NPAIR:
                    turn_x(p + 1)
                project_qkv(p, 1)
                turn_q(p, 0)
            turn_q(NPAIR - 1, 1)

            pe.wait_ge(u_gated, CC * NPAIR)
            pe.wait_ge(qkv_copied, 2 * NT)
            for b in range(ADA_FIRST, ADA_BLOCKS):
                i = b - ADA_FIRST
                prior = 2 if i % 3 == 0 else 1
                mod_block(b, ada2[i % 3], (i % 3, prior + i // 3 + 1))
                if i:
                    mod_turn(b - 1)
            mod_turn(ADA_BLOCKS - 1)
            pe.wait_ge(rows_copied, ADA_BLOCKS)
            for n in range(4):
                pe.wait_ge(diag_ready, 4 * n + 4)
                if n >= 2:
                    pe.wait_ge(gate_rows_copied, n - 1)
                for i in range(4):
                    last = pe.matmul(bank(2 + n % 2)[:, P * i:P * (i + 1)], ones[:, :], diag[:, n % 2, i, :], start=True, stop=True)
                last.then_inc(gate_rows_ready, 1)

            pe.wait_ge(gate_rows_copied, 4)
            last_turn = n_turns[0] - 1
            for n in (last_turn - 1, last_turn):
                pe.wait_ge(t_free[n % 2], n // 2 + 1)

            def scores(n, h, j, t0, nk, first=False):
                pe.wait_ge(q_copied, n + 1)
                if not first:
                    pe.wait_ge(probs_ready, n - 1)
                k0 = P * t0
                for c in range(0, P * nk, 512):
                    w = min(512, P * nk - c)
                    for part, ks in enumerate((k_hi, k_lo)):
                        last = pe.matmul(two[h % 2][:, c // 512, 0:w], q_now[:, h % 2, :], ks[:, j, k0 + c:k0 + c + w],
                                         start=(part == 0), stop=(part == 1))
                last.then_inc(scores_ready, 1)

            def turn_probs(n, h, nk):
                pe.wait_ge(probs_ready, n + 1)
                kk = nk // 2
                for half in range(2):
                    pe.wait_ge(turn_bank_free, 2 * n + half + 1)
                    for k in range(kk):
                        last = pe.transpose(bank(4 + half)[:, P * k:P * (k + 1)],
                                            probs[:, h % 2, P * (kk * half + k):P * (kk * half + k + 1)], ident[:, :])
                    last.then_inc(turned, 1)

            def weigh(n, step, h, j, t0, nk):
                pe.wait_ge(turn_bank_free, 2 * n + 4)
                if h == 0:
                    pe.wait_ge(out_divided, step + 1)
                for k in range(nk):
                    last = pe.matmul(bank(6)[:, (HD + 1) * h:(HD + 1) * (h + 1)], probs_t[:, k, h, :], v_one[:, t0 + k, j, :],
                                     start=(k == 0), stop=(k == nk - 1))
                last.then_inc(weighed, 1)

            def turn_out(step):
                pe.wait_ge(out_divided, step + 2)
                pe.wait_ge(out_copied, step + 1)
                for c in range(2):
                    last = pe.transpose(bank(7)[:, P * c:P * (c + 1)],
                                        out_rows[:, 2 * c:2 * c + 2, :].rearrange("q h d -> q (h d)"), ident[:, :])
                last.then_inc(out_turned, 1)

            pe.sem_inc(weighed, QPK)
            pe.sem_inc(out_divided, 1)
            pe.sem_inc(out_copied, 1)
            j0, t00, nt0, _ = phases[0]
            scores(0, 0, j0, t00, nt0, first=True)
            scores(1, 1, j0, t00, nt0, first=True)
            for i, (j, t0, nt, s0) in enumerate(phases):
                def attend(l, first, last):
                    step = l + s0
                    n = step * QPK
                    ahead = (j, t0, nt) if not last else phases[i + 1][0:3] if i + 1 < len(phases) else None
                    behind = (j, t0, nt) if not first else phases[i - 1][0:3] if i else None
                    for h in range(QPK):
                        turn_probs(n + h, h, nt)
                        if h < 2:
                            scores(n + h + 2, h + 2, j, t0, nt)
                        elif ahead is not None:
                            scores(n + h + 2, h - 2, *ahead)
                        if h:
                            weigh(n + h - 1, step, h - 1, j, t0, nt)
                        elif behind is not None:
                            weigh(n - 1, step, QPK - 1, *behind)
                        if h == 2 and behind is not None:
                            turn_out(l + (s0 - 1))
                steps_of(pe, nt, attend)
            weigh(HEADS_ALL - 1, STEPS - 1, QPK - 1, *phases[-1][0:3])
            turn_out(STEPS - 1)

            pe.wait_ge(probs_ready, HEADS_ALL)
            for c in range(CC):
                pe.wait_ge(conv_done[c], TAPS)
            for s, (o, n) in enumerate(((0, 512), (512, 512), (C_SAMPLE, SS_TOK))):
                if s:
                    pe.wait_ge(centred, CC * s)
                for c in range(CC):
                    last = pe.matmul(bank(0)[:, 0:n], ones[:, :], c_t[:, c, o:o + n], start=(c == 0), stop=(c == CC - 1))
                last.then_inc(mean_ready, 1)
                pe.wait_ge(squared, CC * (s + 1))
                if s:
                    pe.wait_ge(root_ready, s)
                for c in range(CC):
                    last = pe.matmul(bank(1)[:, 0:n], ones[:, :], sq_c[:, c, 0:n], start=(c == 0), stop=(c == CC - 1))
                last.then_inc(var_ready, 1)

            def project_out(q):
                if q >= 2:
                    pe.wait_ge(mix_gated, q - 1)
                p = q // 2
                o = C_SAMPLE + P * (q % 2) if group(p) else P * q
                for half in range(2):
                    for k in range(KC):
                        lhs = mix_t[:, k, P * q:P * (q + 1)] if k < CC else c_t[:, k - CC, o:o + P]
                        last = pe.matmul(two[q % 2][:, half, :], lhs, w_out_sb[:, k, 512 * half:512 * half + 512],
                                         start=(k == 0), stop=(k == KC - 1))
                last.then_inc(mix_ready, 1)

            def turn_x1(p):
                pe.wait_ge(xn2_ready, 2 * p + 2)
                for i in range(4):
                    n = 4 * p + i
                    if n >= 2:
                        pe.wait_ge(t2_free[n % 2], n // 2)
                    for c in range(2):
                        for a in range(2):
                            last = pe.transpose(bank(4 + n % 2)[:, 256 * c + P * a:256 * c + P * (a + 1)],
                                                xn2[:, a, P * (2 * i + c):P * (2 * i + c + 1)], ident[:, :])
                    last.then_inc(t2_ready[n % 2], 1)

            def route(p):
                for b in range(2):
                    pe.wait_ge(t2_free[b], 2 * p + 2)
                if p:
                    pe.wait_ge(logits_copied, p)
                for k in range(KC):
                    last = pe.matmul(bank(6)[0:NE, 0:2 * P], router[:, k, :], h2_t[:, p % 2, k, :], start=(k == 0), stop=(k == KC - 1))
                last.then_inc(logits_ready, 1)

            pe.wait_ge(w_out_loaded, 16)
            pe.wait_ge(root_ready, 3)
            pe.wait_ge(conv_out, 3 * CC)
            pe.wait_ge(out_copied, STEPS + 1)
            pe.wait_ge(router_loaded, 16)
            for p in range(NPAIR):
                project_out(2 * p)
                if p:
                    turn_x1(p - 1)
                project_out(2 * p + 1)
                if p:
                    route(p - 1)
            turn_x1(NPAIR - 1)
            route(NPAIR - 1)

            pe.wait_ge(logits_copied, NPAIR)
            pe.wait_ge(mix_gated, NT)
            for t in range(NT):
                last = pe.transpose(bank(0)[:, NE * t:NE * (t + 1)], logits_t[:, P * t:P * (t + 1)], ident[0:NE, 0:NE])
            last.then_inc(logits_turned, 1)
            pe.wait_ge(aff_ready, 1)
            for t in range(NT):
                b, o = (1 + t // 4, P * (t % 4))
                last = pe.transpose(bank(b)[0:NE, o:o + P], aff[:, t, :], ident[:, :])
                if t in (3, 7, 9):
                    last.then_inc(aff_turned, 1)
            pe.wait_ge(top_float, 4)
            for i in range(2):
                pe.transpose(bank(0)[:, NE * i:NE * (i + 1)], top_p[:, i, :], ident[0:NE, 0:NE])
            for i in range(2):
                last = pe.transpose(bank(0)[0:CAP_S, NE * (2 + i):NE * (3 + i)], top_s[:, i, :], ident[0:NE, 0:NE])
            last.then_inc(top_turned, 1)

            def turn_token(e, k):
                pe.transpose(bank(k % 2)[:, 0:CAP_P], xg_p[:, P * k:P * (k + 1)], ident[:, :])
                pe.transpose(bank(k % 2)[:, CAP_P:CAP], xg_s[:, P * k:P * (k + 1)], ident[0:CAP_S, 0:CAP_S]).then_inc(x_turned, 1)

            def turn_y(e, m):
                pe.wait_ge(y_scaled, e * KC + m + 3)
                if m % 4 == 0:
                    pe.wait_ge(ye_ready, 4 * e + 1 + m // 2)
                o = P * (m % 4)
                pe.transpose(bank(6)[:, o:o + P], y_t[:, m, 0:CAP_P], ident[:, :])
                last = pe.transpose(bank(7)[0:CAP_S, o:o + P], y_t[:, m, CAP_P:CAP], ident[:, :])
                if m % 4 == 3:
                    last.then_inc(y_turned, 1)

            def columns(b, w, m, x, ready, n):
                for k in range(KC):
                    if ready is not None:
                        pe.wait_ge(ready, n + k + 1)
                    last = pe.matmul(bank(b)[:, 0:CAP], w[:, m // 2, k, P * (m % 2):P * (m % 2) + P], x[:, k, :],
                                     start=(k == 0), stop=(k == KC - 1))
                return last

            def expert(e, more):
                pe.wait_ge(x_scaled, KC * e + KC)
                for m in range(KC):
                    pe.wait_ge(hid_ready, KC * e + m + 1)
                    if m % 2 == 0:
                        pe.wait_ge(gate_w_loaded[m // 2], 16 * e + 16)
                    columns(m % 2, gate_w_sb, m, xe_t, None, 0).then_inc(gate_ready, 1)
                    if m % 2 == 0:
                        pe.wait_ge(up_w_loaded[m // 2], 16 * e + 16)
                    columns(2 + m % 2, up_w_sb, m, xe_t, None, 0).then_inc(up_ready, 1)
                for m in range(KC):
                    pe.wait_ge(y_scaled, KC * e + m + 1)
                    if m % 2 == 0:
                        pe.wait_ge(down_w_loaded[m // 2], 16 * e + 16)
                    columns(4 + m % 2, down_w_sb, m, hid, hid_ready if m == 0 else None, KC * e + 2).then_inc(down_ready, 1)
                    if more:
                        if m == 0:
                            pe.wait_ge(gathered, 32 * e + 64)
                        if m >= 2:
                            pe.wait_ge(x_scaled, KC * e + KC + m - 1)
                        turn_token(e + 1, m)
                    if m:
                        turn_y(e, m - 1)
                turn_y(e, KC - 1)

            pe.wait_ge(gathered, 32)
            pe.wait_ge(top_ready, 4)
            for k in range(KC):
                if k >= 2:
                    pe.wait_ge(x_scaled, k - 1)
                turn_token(0, k)
            with pe.Fori(0, NE - 1) as e:
                expert(e, True)
            expert(NE - 1, False)

        @block.vector
        def _(dve):
            dve.wait_ge(cols_turned, 1)
            dve.tensor_copy(cols[:, :], bank(0)[:, 0:ROWS]).then_inc(cols_ready, 1)
            dve.tensor_copy(taps[:, :, :], bank(0)[:, 128:128 + CC * TAPS].rearrange("p (c t) -> p c t", c=CC)).then_inc(cols_ready, 1)
            dve.wait_ge(gains_loaded, 64)
            dve.tensor_scalar(gains[:, 0, :], gains[:, 0, :], HD ** -0.5, None, ALU.mult).then_inc(gains_scaled, 1)
            dve.wait_ge(gains_scaled, 1)
            dve.tensor_scalar(ngains[:, :, :], gains[:, :, :], -1.0, None, ALU.mult).then_inc(gains_scaled, 1)
            dve.wait_ge(gains_scaled, 2)
            for g in range(2):
                gain = gains[:, g, :].rearrange("p (i b) -> p i b", b=2)
                ngain = ngains[:, g, :].rearrange("p (i b) -> p i b", b=2)
                out_c = rope_c[:, :, g, :].rearrange("p t (i b) -> p t i b", b=2)
                out_s = rope_s[:, :, g, :].rearrange("p t (i b) -> p t i b", b=2)

                def over_tiles(v):
                    return v.unsqueeze(1).to_broadcast([P, 8, HD // 2])
                for b in range(2):
                    dve.tensor_tensor(out_c[:, :, :, b], cos_sb[:, :, :], over_tiles(gain[:, :, b]), ALU.mult).then_inc(tables_ready, 1)
                dve.tensor_tensor(out_s[:, :, :, 0], sin_sb[:, :, :], over_tiles(ngain[:, :, 1]), ALU.mult).then_inc(tables_ready, 1)
                dve.tensor_tensor(out_s[:, :, :, 1], sin_sb[:, :, :], over_tiles(gain[:, :, 0]), ALU.mult).then_inc(tables_ready, 1)

            def norm_x(p):
                dve.wait_ge(x_root, p + 1)
                dve.reciprocal(rs_x[:, :], rt_x[:, :]).then_inc(x_recip, 1)
                dve.wait_ge(x_recip, p + 1)
                for a in range(2):
                    dve.tensor_scalar(x_in[:, a, :], x_in[:, a, :], rs_x[:, a:a + 1], None, ALU.mult).then_inc(x_normed, 1)

            norm_x(0)
            dve.wait_ge(rows_turned, ADA_FIRST)
            dve.wait_ge(cols_ready, 2)

            def mod_cols(c0, c1):
                bias = cols[:, ROW_AB + c0:ROW_AB + c1].unsqueeze(2).to_broadcast([P, c1 - c0, 2])
                dve.tensor_tensor(mod[:, c0:c1, :], bank(7)[:, 2 * c0:2 * c1].rearrange("p (c g) -> p c g", g=2), bias,
                                  ALU.add).then_inc(mod_ready, 1)

            mod_cols(0, GATE1)
            dve.wait_ge(mod_ready, 1)

            def scale_of(out, norm_row, scale_col):
                gain = cols[:, norm_row:norm_row + KC].unsqueeze(2).to_broadcast([P, KC, 2])
                dve.scalar_tensor_tensor(out=out[:, :, :], in0=mod[:, scale_col:scale_col + KC, :], scalar=1.0, in1=gain,
                                         op0=ALU.add, op1=ALU.mult).then_inc(scale_ready, 1)

            scale_of(a1, ROW_NMIX, SCALE1)
            dve.wait_ge(scale_ready, 1)

            def x_out(p):
                g = group(p)
                for i in range(1, 4, 2):
                    n = turn_at["x", p] + i
                    dve.wait_ge(t_ready[n % 2], n // 2 + 1)
                    for c in range(2):
                        k = 2 * i + c
                        last = dve.tensor_scalar(h_t[:, p % 2, k, :], bank(n % 2)[:, 256 * c:256 * (c + 1)], a1[:, k, g:g + 1],
                                                 mod[:, SHIFT1 + k, g:g + 1], ALU.mult, ALU.add)
                    last.then_inc(t_free[n % 2], 1)

            def low_out(p, a):
                t = 2 * p + a
                for i in range(3):
                    n = turn_at["q", p, a] + i
                    dve.wait_ge(high_ready, 3 * t + i + 1)
                    if i < 2:
                        src = bank(n % 2)[0:HD, :].rearrange("d (h q) -> d h q", h=4)
                        last = dve.tensor_tensor(q_st[HD:P, t, 4 * i:4 * i + 4, :], src,
                                                 q_st[0:HD, t, 4 * i:4 * i + 4, :].bitcast(F32), ALU.subtract)
                    else:
                        src = bank(n % 2)[0:HD, 0:NKV * P].rearrange("d (j q) -> d j q", j=NKV)
                        for lo in (0, HD):
                            last = dve.tensor_tensor(k_lo[lo:lo + HD, :, P * t:P * (t + 1)], src,
                                                     k_hi[0:HD, :, P * t:P * (t + 1)].bitcast(F32), ALU.subtract)
                    last.then_inc(t_free[n % 2], 1)

            def qk_norm(q):
                a = q % 2
                dve.wait_ge(sq_ready, q + 1)
                dve.tensor_reduce(ss_q[:, a, :], sq[:, :, :], AX.X, ALU.add).then_inc(sq_summed, 1)
                dve.wait_ge(q_root, q + 1)
                dve.reciprocal(rs_q[:, a, :], rt_q[:, a, :]).then_inc(q_recip, 1)
                dve.wait_ge(q_recip, q + 1)
                dve.tensor_tensor(qk[a][:, :, :], qk[a][:, :, :], rs_q[:, a, :].unsqueeze(2).to_broadcast([P, 10, HD]),
                                  ALU.mult).then_inc(q_normed, 1)
                dve.wait_ge(q_normed, q + 1)
                for g, h0, nh in ((0, 0, NH), (1, NH, NKV)):
                    tab = rope_c[:, q % 8, g:g + 1, :].to_broadcast([P, nh, HD])
                    dve.tensor_tensor(rot1[:, h0:h0 + nh, :], qk[a][:, h0:h0 + nh, :], tab, ALU.mult).then_inc(rot1_ready, 1)
                dve.wait_ge(rot1_ready, 2 * q + 2)
                dve.wait_ge(rot2_ready, q + 1)
                dve.tensor_tensor(qk[a][:, :, :], rot1[:, :, :], rot2[:, :, :], ALU.add).then_inc(rotated, 1)

            x_out(0)
            for p in range(NPAIR):
                if p + 1 < NPAIR:
                    norm_x(p + 1)
                for i in range(CC):
                    n = CC * p + i
                    dve.wait_ge(sig_ready, n + 1)
                    dve.tensor_tensor(a_t[:, i, a_cols(p):a_cols(p) + 2 * P], bank(2 + n % 2)[:, 0:256], sig[:, n % 2, :],
                                      ALU.mult).then_inc(u_gated, 1)
                if p:
                    low_out(p - 1, 1)
                qk_norm(2 * p)
                if p + 1 < NPAIR:
                    x_out(p + 1)
                qk_norm(2 * p + 1)
                low_out(p, 0)
            low_out(NPAIR - 1, 1)

            dve.wait_ge(u_gated, CC * NPAIR)
            dve.wait_ge(fills_made, 6)

            def tap(c, k, n):
                dve.wait_ge(conv_done[c], n)
                dve.scalar_tensor_tensor(out=c_t[:, c, :], in0=a_t[:, c, bass.ds(k, C_LEN)], scalar=taps[:, c, bass.ds(k, 1)],
                                         in1=c_t[:, c, :], op0=ALU.mult, op1=ALU.add).then_inc(conv_done[c], 1)

            dve.wait_ge(rotated, NT)
            n = n_turns[0] - 1
            dve.wait_ge(t_ready[n % 2], n // 2 + 1)
            for c in range(CC):
                dve.tensor_scalar(c_t[:, c, :], conv_slices(c, 0), taps[:, c, 0:1], cols[:, ROW_CB + c:ROW_CB + c + 1],
                                  ALU.mult, ALU.add).then_inc(conv_done[c], 1)
            for k in range(1, TAPS_FIRST):
                for c in range(CC):
                    tap(c, k, k)
            dve.wait_ge(rows_turned, ADA_BLOCKS)
            mod_cols(GATE1, 6 * KC)
            dve.wait_ge(mod_ready, 2)
            scale_of(a2, ROW_NFFN, SCALE2)
            for n in range(4):
                if n >= 2:
                    dve.wait_ge(gate_rows_ready, n - 1)
                for i in range(4):
                    k = GATE1 + 4 * (n % 2) + i
                    dve.tensor_scalar(diag[:, n % 2, i, :], ident[:, :], mod[:, k, n // 2:n // 2 + 1], None, ALU.mult).then_inc(diag_ready, 1)

            def maximum(n, h, nk):
                dve.wait_ge(scores_ready, n + 1)
                dve.tensor_reduce(negmax[:, h:h + 1], two[h % 2][:, :, :].rearrange("p b n -> p (b n)")[:, 0:P * nk], AX.X,
                                  ALU.max, negate=True).then_inc(max_ready, 1)

            def divide(step):
                dve.wait_ge(weighed, step * QPK + 2 * QPK)
                o = bank(6)[:, 0:QPK * (HD + 1)].rearrange("q (h d) -> q h d", h=QPK)
                dve.reciprocal(rsum[:, :, :], o[:, :, HD:HD + 1]).then_inc(sums_inverted, 1)
                dve.wait_ge(sums_inverted, step + 1)
                dve.tensor_tensor(out_rows[:, :, :], o[:, :, 0:HD], rsum[:, :, :].to_broadcast([P, QPK, HD]), ALU.mult).then_inc(out_divided, 1)

            maximum(0, 0, phases[0][2])
            maximum(1, 1, phases[0][2])
            for i, (j, t0, nt, s0) in enumerate(phases):
                chunks = (2 * j, 2 * j + 1) if t0 == 0 else ()

                def between(l, first, last):
                    n = (l + s0) * QPK
                    nxt_nk = nt if not last else phases[i + 1][2] if i + 1 < len(phases) else None

                    def some(m):
                        for c in chunks:
                            k = l * TAPS_STEP + (TAPS_FIRST + m)
                            tap(c, k, k)
                    maximum(n + 2, 2, nt)
                    if not (first and i == 0):
                        divide(l + (s0 - 1))
                    some(0)
                    maximum(n + 3, 3, nt)
                    some(1)
                    if nxt_nk is not None:
                        maximum(n + 4, 0, nxt_nk)
                    some(2)
                    if nxt_nk is not None:
                        maximum(n + 5, 1, nxt_nk)
                steps_of(dve, nt, between)
            divide(STEPS - 1)

            for s, (o, n) in enumerate(((0, 512), (512, 512), (C_SAMPLE, SS_TOK))):
                dve.wait_ge(mean_ready, s + 1)
                for c in range(CC):
                    dve.scalar_tensor_tensor(out=c_t[:, c, o:o + n], in0=bank(0)[:, 0:n], scalar=-1.0 / DC, in1=c_t[:, c, o:o + n],
                                             op0=ALU.mult, op1=ALU.add).then_inc(centred, 1)
                dve.wait_ge(root_ready, s + 1)
                dve.reciprocal(rs_c[:, 0:n], rt_c[:, 0:n]).then_inc(inv_ready, 1)
                dve.wait_ge(inv_ready, s + 1)
                dve.wait_ge(squared, CC * (s + 1))
                for c in range(CC):
                    dve.tensor_tensor(c_t[:, c, o:o + n], c_t[:, c, o:o + n], rs_c[:, 0:n], ALU.mult).then_inc(scaled, 1)

            def gate_mix(q):
                a = q % 2
                dve.wait_ge(mix_ready, q + 1)
                if q >= 2:
                    dve.wait_ge(y_stored[a], 16 * (q // 2))
                    dve.wait_ge(xn2_ready, q - 1)
                g = group(q // 2)
                dve.tensor_tensor(x1[:, a, :], two[a][:, :, :].rearrange("p b n -> p (b n)"), gate1_row[:, g, :], ALU.mult).then_inc(mix_gated, 1)

            def norm_x1(q):
                a = q % 2
                dve.wait_ge(x1_root, q + 1)
                dve.reciprocal(rs_x[:, 0:1], rt_x[:, 0:1]).then_inc(x1_recip, 1)
                dve.wait_ge(x1_recip, q + 1)
                dve.tensor_scalar(xn2[:, a, :], x1[:, a, :], rs_x[:, 0:1], None, ALU.mult).then_inc(xn2_ready, 1)

            def h2_out(p):
                g = group(p)
                for i in range(1, 4, 2):
                    n = 4 * p + i
                    dve.wait_ge(t2_ready[n % 2], n // 2 + 1)
                    for c in range(2):
                        k = 2 * i + c
                        last = dve.tensor_scalar(h2_t[:, p % 2, k, :], bank(4 + n % 2)[:, 256 * c:256 * (c + 1)], a2[:, k, g:g + 1],
                                                 mod[:, SHIFT2 + k, g:g + 1], ALU.mult, ALU.add)
                    last.then_inc(t2_free[n % 2], 1)

            dve.wait_ge(gate_rows_copied, 4)
            dve.wait_ge(scale_ready, 2)
            gate_mix(0)
            norm_x1(0)
            gate_mix(1)
            norm_x1(1)
            for p in range(1, NPAIR):
                gate_mix(2 * p)
                h2_out(p - 1)
                norm_x1(2 * p)
                gate_mix(2 * p + 1)
                norm_x1(2 * p + 1)
            h2_out(NPAIR - 1)

            dve.wait_ge(logits_turned, 1)
            lg = bank(0)[:, 0:NT * NE].rearrange("p (t e) -> p t e", e=NE)
            dve.tensor_reduce(smx[:, 0, :], lg, AX.X, ALU.max).then_inc(router_max, 1)
            dve.wait_ge(router_max, 1)
            dve.tensor_tensor(aff[:, :, :], lg, smx[:, 0, :].unsqueeze(2).to_broadcast([P, NT, NE]), ALU.subtract).then_inc(router_shifted, 1)
            dve.wait_ge(router_exp, 1)
            dve.tensor_reduce(smx[:, 1, :], aff[:, :, :], AX.X, ALU.add).then_inc(router_sum, 1)
            dve.wait_ge(router_sum, 1)
            dve.reciprocal(smx[:, 2, :], smx[:, 1, :]).then_inc(router_inv, 1)
            dve.wait_ge(router_inv, 1)
            dve.tensor_tensor(aff[:, :, :], aff[:, :, :], smx[:, 2, :].unsqueeze(2).to_broadcast([P, NT, NE]), ALU.mult).then_inc(aff_ready, 1)
            for i in range(2):
                dve.wait_ge(aff_turned, i + 1)
                dve.tensor_copy(aff_p[:, 512 * i:512 * i + 512], bank(1 + i)[0:NE, :]).then_inc(aff_copied, 1)
            dve.wait_ge(aff_turned, 3)
            dve.tensor_copy(aff_s[:, :], bank(3)[0:NE, 0:SS_TOK]).then_inc(aff_copied, 1)
            dve.wait_ge(aff_copied, 3)

            def top_eight(vals, top, idx, r, step):
                if r:
                    dve.wait_ge(step, 3 * r)
                dve.max(top[:, 0, 8 * r:8 * r + 8], vals[:, :]).then_inc(step, 1)
                dve.wait_ge(step, 3 * r + 1)
                dve.max_index(idx[:, 8 * r:8 * r + 8], top[:, 0, 8 * r:8 * r + 8], vals[:, :]).then_inc(step, 1)
                dve.wait_ge(step, 3 * r + 2)
                dve.match_replace(vals[:, :], top[:, 0, 8 * r:8 * r + 8], vals[:, :], LOWEST).then_inc(step, 1)

            for r in range(CAP_P // 8):
                top_eight(aff_p, top_p, idx_p, r, top_p_step)
                if r < CAP_S // 8:
                    top_eight(aff_s, top_s, idx_s, r, top_s_step)
            dve.wait_ge(top_p_step, 3 * CAP_P // 8)
            dve.wait_ge(top_s_step, 3 * CAP_S // 8)
            dve.tensor_copy(top_p[:, 1, :], idx_p[:, :]).then_inc(top_float, 2)
            dve.tensor_copy(top_s[:, 1, :], idx_s[:, :]).then_inc(top_float, 2)
            dve.wait_ge(top_turned, 1)
            dve.tensor_copy(g_top_p[:, 0:NE], bank(0)[:, 0:NE]).then_inc(top_ready, 1)
            dve.tensor_copy(i_top_p[:, 0:NE], bank(0)[:, NE:2 * NE]).then_inc(top_ready, 1)
            dve.tensor_copy(g_top_s[0:CAP_S, 0:NE], bank(0)[0:CAP_S, 2 * NE:3 * NE]).then_inc(top_ready, 1)
            dve.tensor_copy(i_top_s[0:CAP_S, 0:NE], bank(0)[0:CAP_S, 3 * NE:4 * NE]).then_inc(top_ready, 1)

            def token_out(e, k):
                dve.wait_ge(x_turned, KC * e + k + 1)
                b = bank(k % 2)
                dve.tensor_scalar(xe_t[:, k, 0:CAP_P], b[:, 0:CAP_P], a2[:, k, 0:1], mod[:, SHIFT2 + k, 0:1], ALU.mult, ALU.add)
                dve.tensor_scalar(xe_t[:, k, CAP_P:CAP], b[:, CAP_P:CAP], a2[:, k, 1:2], mod[:, SHIFT2 + k, 1:2],
                                  ALU.mult, ALU.add).then_inc(x_scaled, 1)

            def expert(e, more):
                for m in range(KC):
                    dve.wait_ge(silu_done, KC * e + m + 1)
                    dve.wait_ge(up_ready, KC * e + m + 1)
                    dve.tensor_tensor(hid[:, m, :], sil[:, m % 2, :], bank(2 + m % 2)[:, 0:CAP], ALU.mult).then_inc(hid_ready, 1)
                for m in range(KC):
                    dve.wait_ge(down_ready, KC * e + m + 1)
                    b = bank(4 + m % 2)
                    dve.tensor_scalar(y_t[:, m, 0:CAP_P], b[:, 0:CAP_P], mod[:, GATE2 + m, 0:1], None, ALU.mult)
                    dve.tensor_scalar(y_t[:, m, CAP_P:CAP], b[:, CAP_P:CAP], mod[:, GATE2 + m, 1:2], None, ALU.mult).then_inc(y_scaled, 1)
                    if more:
                        token_out(e + 1, m)

            dve.sem_inc(hid_ready, 2)
            dve.sem_inc(y_scaled, 2)
            for k in range(KC):
                token_out(0, k)
            with dve.Fori(0, NE - 1) as e:
                expert(e, True)
            expert(NE - 1, False)


def rope_tables():
    pos = np.arange(SP_TOK)
    inv = (10000.0 ** (-np.arange(0, HD // 2, 2, dtype=np.float32) / np.float32(HD // 2))).astype(np.float32)
    row = (pos // 64).astype(np.float32)
    col = (pos % 64).astype(np.float32)
    ang = np.concatenate([row[:, None] * inv, col[:, None] * inv], axis=-1)
    return np.cos(ang).astype(np.float32), np.sin(ang).astype(np.float32)


_INS = ["x_prompt", "x_sample", "c_prompt", "c_sample", "ada_w", "ada_b", "norm_mix", "w_in", "q_norm", "k_norm",
        "conv_w", "conv_b", "conv_ln_g", "conv_ln_b", "w_out", "norm_ffn", "w_router", "w_gate", "w_up", "w_down"]


def kernel(**inputs):
    import concourse.bacc as bacc
    from concourse.bass_utils import run_bass_kernel_spmd

    nc = bacc.Bacc("TRN2", target_bir_lowering=False, num_devices=1)
    arrays, args = {}, []
    for name in _INS:
        arrays[f"in_{name}"] = np.ascontiguousarray(inputs[name])
    arrays["in_rope_cos"], arrays["in_rope_sin"] = rope_tables()
    for name, a in arrays.items():
        args.append(nc.dram_tensor(name, a.shape, mybir.dt.from_np(a.dtype), kind="ExternalInput").ap())
    for name, shape in (("out_prompt", (1, SP_TOK, D)), ("out_sample", (1, SS_TOK, D))):
        args.append(nc.dram_tensor(name, shape, F32, kind="ExternalOutput").ap())
    encoder_layer(nc, *args)
    r = run_bass_kernel_spmd(nc, [arrays], core_ids=[0])
    return r.results[0]["out_prompt"], r.results[0]["out_sample"]
```

```python
from contextlib import ExitStack

import numpy as np

import concourse.bass as bass
from concourse import mybir

F32 = mybir.dt.float32
F32R = mybir.dt.float32r
U32 = mybir.dt.uint32
ACT = mybir.ActivationFunctionType
ALU = mybir.AluOpType
AX = mybir.AxisListType

P = 128
D = 1024
KC = D // P
SP_TOK, SS_TOK = 1024, 256
TOK = SP_TOK + SS_TOK
NT = TOK // P
NPAIR = NT // 2
HD = 64
NH = 8
NKV = 2
QPK = NH // NKV
DA = NH * HD
DKV = NKV * HD
DC = D - DA
CC = DC // P
TAPS = 31
PAD = TAPS // 2
D_IN = DA + 2 * DKV + 2 * DC
NQKV = DA + 2 * DKV
NE = 16
CAP_P = 2 * SP_TOK // NE
CAP_S = 2 * SS_TOK // NE
CAP = CAP_P + CAP_S
EPS = 1e-6
LOWEST = -1.0

A_PROMPT = PAD
A_SAMPLE = PAD + SP_TOK + 2 * PAD
A_LEN = A_SAMPLE + SS_TOK + PAD
A_ROW = A_LEN + 4
C_SAMPLE = SP_TOK + 2 * PAD
SPANS = ((0, SP_TOK // 2), (SP_TOK // 2, SP_TOK // 2), (C_SAMPLE, SS_TOK))
SPAN = SP_TOK // 2
PROMPT_TILES = SP_TOK // P
STEP_TAPS = 2
assert STEP_TAPS * 2 * PROMPT_TILES >= TAPS

SHIFT1, SCALE1, GATE1, SHIFT2, SCALE2, GATE2 = (i * KC for i in range(6))
ADA_BLOCK = 512
ADA_FIRST = 2 * D // ADA_BLOCK
ADA_BLOCKS = 6 * D // ADA_BLOCK
ADA_LATE = ADA_BLOCKS - D // ADA_BLOCK

ROW_C, ROW_NMIX, ROW_NFFN, ROW_CB, ROW_LG, ROW_LB, ROW_AB = 0, 16, 24, 32, 36, 40, 44
ROWS = ROW_AB + 48


def encoder_layer(nc, x_p, x_s, c_p, c_s, ada_w, ada_b, norm_mix, w_in, q_norm, k_norm, conv_w, conv_b,
                  ln_g, ln_b, w_out, norm_ffn, w_router, w_gate, w_up, w_down, rope_cos, rope_sin,
                  y_p, y_s):
    xn_p = nc.dram_tensor("xn_prompt", (SP_TOK, D), F32).ap()
    xn_s = nc.dram_tensor("xn_sample", (SS_TOK, D), F32).ap()

    base = 16512
    small = base
    Z1 = small + 16384
    Z2 = Z1 + 81920
    Z3 = Z2 + 93184
    at = {"small": small}

    def put(name, shape, dt, offset):
        return nc.alloc_sbuf_tensor_at(name, shape, dt, offset=offset)

    def keep(name, shape, dt=F32):
        n = int(np.prod(shape[1:])) * 4
        t = put(name, shape, dt, at["small"])
        at["small"] += (n + 31) // 32 * 32
        assert at["small"] <= Z1
        return t

    ident = keep("ident", [P, P])
    ones = keep("ones", [P, P])
    cols = keep("cols", [P, ROWS])
    taps = keep("taps", [P, CC, TAPS])
    silu_c = keep("silu_c", [P, 2 * KC])
    mod = keep("mod", [P, 6 * KC, 2])
    a1 = keep("a1", [P, KC, 2])
    a2 = keep("a2", [P, KC, 2])
    ss_x = keep("ss_x", [P, 2])
    rt_x = keep("rt_x", [P, 2])
    rs_x = keep("rs_x", [P, 2])
    ss_q = keep("ss_q", [P, 2, 10])
    rt_q = keep("rt_q", [P, 2, 10])
    rs_q = keep("rs_q", [P, 2, 10])
    negmax = keep("negmax", [P, 4])
    router = keep("router", [P, KC, NE])
    eps_col = keep("eps_col", [P, 1])
    g_top_p = keep("g_top_p", [P, NE])
    g_top_s = keep("g_top_s", [P, NE])
    i_top_p = keep("i_top_p", [P, NE], U32)
    i_top_s = keep("i_top_s", [P, NE], U32)
    i_now = keep("i_now", [P, 4], U32)
    smx = keep("smx", [P, 3, NT])
    mod_rows = keep("mod_rows", [2, 2, ADA_BLOCK])
    rope_c = put("rope_c", [P, 8, 2, HD], F32, at["small"])
    rope_s = put("rope_s", [P, 8, 2, HD], F32, at["small"] + 4096)
    gate1_row = put("gate1_row", [P, 2, D], F32, at["small"])
    assert at["small"] + 8192 <= Z1, at["small"] + 8192 - Z1

    x_in = put("x_in", [P, 2, D], F32, Z1)
    h_t = put("h_t", [P, 2, KC, 2 * P], F32, Z1 + 8192)
    w_in_sb = put("w_in_sb", [P, KC, D_IN], F32, Z1 + 24576)
    ada = [put(f"ada{i}", [P, KC, ADA_BLOCK], F32, Z2 + 16384 * i) for i in range(3)]
    rows = put("rows", [ROWS, P], F32, Z3)
    taps_row = put("taps_row", [TAPS, DC], F32, Z3 + 512)
    gains = put("gains", [P, 2, HD], F32, Z3 + 2560)
    ngains = put("ngains", [P, 2, HD], F32, Z3 + 3072)
    cos_sb = put("cos_sb", [P, 8, HD // 2], F32, Z1 + 16384)
    sin_sb = put("sin_sb", [P, 8, HD // 2], F32, Z1 + 17408)
    q_st = put("q_st", [P, NT, NH, P], F32R, Z2)
    k_hi = put("k_hi", [P, NKV, TOK], F32R, Z2 + 40960)
    k_lo = put("k_lo", [P, NKV, TOK], F32R, Z2 + 51200)
    v_one = put("v_one", [P, NT, NKV, HD + 1], F32, Z2 + 61440)
    a_t = put("a_t", [P, CC, A_ROW], F32, Z2 + 71680)
    junk = put("junk", [P, D], F32, Z3 + 4096)
    qk = [put(f"qk{i}", [P, 10, HD], F32, Z3 + 8192 + 2560 * i) for i in range(2)]
    sq = put("sq", [P, 10, HD], F32, Z3 + 13312)
    rot1 = sq
    rot2 = put("rot2", [P, 10, HD], F32, Z3 + 15872)
    sig = put("sig", [P, 2, 2 * P], F32, Z3 + 18432)
    ada2 = [put(f"ada2_{i}", [P, KC, ADA_BLOCK], F32, o) for i, o in enumerate((Z1, Z1 + 32768, Z1 + 49152, Z1 + 65536))]
    ada3 = [put(f"ada3_{i}", [P, KC, ADA_BLOCK], F32, Z2 + 32768 + 16384 * i) for i in range(2)]
    diag = [put(f"diag{i}", [P, 2, 4, P], F32, o) for i, o in enumerate((Z1 + 28672, Z3 + 16384))]
    c_t = [put(f"c_t{i}", [P, CC, n], F32, Z3 + 8192 * i) for i, (_, n) in enumerate(SPANS)]
    w_out_sb = put("w_out_sb", [P, KC, D], F32, Z1)
    probs = put("probs", [P, 2, SP_TOK], F32, Z1 + 32768)
    probs_t = put("probs_t", [P, KC, QPK, P], F32, Z1 + 40960)
    mix_t = put("mix_t", [P, CC, TOK], F32, Z1 + 57344)
    q_now = put("q_now", [P, 2, P], F32R, Z1 + 77824)
    out_rows = put("out_rows", [P, QPK, HD], F32, Z1 + 78848)
    rsum = put("rsum", [P, QPK, 1], F32, Z1 + 79872)
    sq_c = [put(f"sq_c{i}", [P, CC, SPANS[i][1]], F32, o) for i, o in enumerate((Z1 + 16384, Z1 + 45056, Z2 + 88064))]
    rt_c = [put(f"rt_c{i}", [P, SPANS[i][1]], F32, o) for i, o in enumerate((Z1 + 24576, Z1 + 53248, Z2 + 92160))]
    rs_c = [put(f"rs_c{i}", [P, SPAN], F32, o) for i, o in enumerate((Z1 + 26624, Z1 + 55296))]
    x_again = put("x_again", [P, 2, D], F32, Z1 + 32768)
    x1 = put("x1", [P, 2, D], F32, Z1 + 40960)
    xn2 = put("xn2", [P, 2, D], F32, Z1 + 49152)
    h2_t = put("h2_t", [P, KC, 2 * P], F32, Z2 + 65536)
    w_hi = put("w_hi", [P, KC, D], F32R, Z2)
    w_lo = put("w_lo", [P, KC, D], F32R, Z1)
    s_hi = put("s_hi", [P, 2, KC, P], F32R, Z2 + 73728)
    mix_lo = put("mix_lo", [P, CC, TOK], F32R, Z1 + 57344)
    c_lo = [put(f"c_lo{i}", [P, CC, n], F32R, Z3 + 8192 * i) for i, (_, n) in enumerate(SPANS)]
    logits_t = put("logits_t", [NE, TOK], F32, Z2 + 81920)
    HALF = SP_TOK // 2
    HT = HALF // P
    LOW2 = 32
    RANKED = LOW2 + NE
    aff_h = put("aff_h", [P, HT, 3, NE], F32, Z2 + 87040)
    aff_r = put("aff_r", [P, SS_TOK // P, NE], F32, Z2 + 87808)
    aff_p = put("aff_p", [RANKED, HALF], F32, Z1 + 77824)
    flip = put("flip", [P, P], F32, Z3 + 20480)
    top_sb = put("top_sb", [P, 2, RANKED], F32, Z2 + 91648)
    from_low = put("from_low", [P, NE], F32, Z2 + 92032)
    idx_step = put("idx_step", [P, NE], F32, Z2 + 92096)
    aff_s = put("aff_s", [NE, SS_TOK], F32, Z2 + 88064)
    top_p = put("top_p", [RANKED, 2, CAP_P], F32, Z2 + 89088)
    top_s = put("top_s", [NE, 2, CAP_S], F32, Z2 + 90112)
    idx_p = put("idx_p", [RANKED, CAP_P], U32, Z2 + 90624)
    idx_s = put("idx_s", [NE, CAP_S], U32, Z2 + 91136)
    MC = 256
    NS = D // MC
    gate_w_sb = put("gate_w_sb", [P, NS, KC, MC], F32, Z2)
    up_w_sb = put("up_w_sb", [P, NS, KC, MC], F32, Z2 + 32768)
    down_w_sb = put("down_w_sb", [P, NS, KC, MC], F32, Z1)
    xg_p = put("xg_p", [CAP_P, D], F32, Z1 + 32768)
    xg_s = put("xg_s", [CAP_S, D], F32, Z1 + 36864)
    ye_p = put("ye_p", [CAP_P, D], F32, Z1 + 40960)
    ye_s = put("ye_s", [CAP_S, D], F32, Z1 + 45056)
    xe_t = put("xe_t", [P, KC, CAP], F32, Z1 + 49152)
    hid = put("hid", [P, KC, CAP], F32, Z1 + 54272)
    y_t = put("y_t", [P, KC, CAP], F32, Z1 + 59392)
    sil = put("sil", [P, 2, CAP], F32, Z1 + 64512)

    with ExitStack() as ctx:
        two = [ctx.enter_context(nc.psum_tensor(f"banks{2 * i}", [P, 2, 512], F32)) for i in range(4)]

        def bank(k):
            return two[k // 2][:, k % 2, :]

        def sem(name):
            return ctx.enter_context(nc.semaphore(name))

        rows_loaded = sem("rows_loaded")
        gains_loaded = sem("gains_loaded")
        router_loaded = sem("router_loaded")
        ada_loaded = [sem(f"ada_loaded{i}") for i in range(4)]
        ada3_loaded = sem("ada3_loaded")
        wu_loaded = sem("wu_loaded")
        wqkv_loaded = sem("wqkv_loaded")
        w_out_loaded = sem("w_out_loaded")
        x_loaded = sem("x_loaded")
        ident_made = sem("ident_made")
        fills_made = sem("fills_made")
        cols_turned = sem("cols_turned")
        cols_ready = sem("cols_ready")
        silu_ready = sem("silu_ready")
        rows_ready = sem("rows_ready")
        rows_copied = sem("rows_copied")
        rows_turned = sem("rows_turned")
        mod_ready = sem("mod_ready")
        scale_ready = sem("scale_ready")
        gains_scaled = sem("gains_scaled")
        tables_ready = sem("tables_ready")
        x_squared = sem("x_squared")
        x_root = sem("x_root")
        x_recip = sem("x_recip")
        x_normed = sem("x_normed")
        t_ready = [sem(f"t_ready{i}") for i in range(2)]
        t_free = [sem(f"t_free{i}") for i in range(2)]
        u_ready = sem("u_ready")
        sig_ready = sem("sig_ready")
        u_gated = sem("u_gated")
        qkv_ready = sem("qkv_ready")
        qkv_copied = sem("qkv_copied")
        sq_ready = sem("sq_ready")
        sq_summed = sem("sq_summed")
        q_root = sem("q_root")
        q_recip = sem("q_recip")
        q_normed = sem("q_normed")
        rot1_ready = sem("rot1_ready")
        rot2_ready = sem("rot2_ready")
        rotated = sem("rotated")
        high_ready = sem("high_ready")
        diag_ready = sem("diag_ready")
        gate_rows_ready = sem("gate_rows_ready")
        gate_rows_copied = sem("gate_rows_copied")
        conv_done = [[sem(f"conv_done{s}_{c}") for c in range(CC)] for s in range(len(SPANS))]
        q_copied = sem("q_copied")
        scores_ready = sem("scores_ready")
        max_ready = sem("max_ready")
        probs_ready = sem("probs_ready")
        turned = sem("turned")
        turn_bank_free = sem("turn_bank_free")
        weighed = sem("weighed")
        sums_inverted = sem("sums_inverted")
        out_divided = sem("out_divided")
        out_turned = sem("out_turned")
        out_copied = sem("out_copied")
        mean_ready = sem("mean_ready")
        centred = sem("centred")
        squared = sem("squared")
        var_ready = sem("var_ready")
        root_ready = sem("root_ready")
        inv_ready = sem("inv_ready")
        scaled = sem("scaled")
        conv_out = sem("conv_out")
        w_hi_ready = sem("w_hi_ready")
        w_lo_ready = sem("w_lo_ready")
        s_hi_ready = sem("s_hi_ready")
        s_lo_ready = sem("s_lo_ready")
        x_reloaded = sem("x_reloaded")
        mix_ready = sem("mix_ready")
        mix_gated = sem("mix_gated")
        x1_ready = sem("x1_ready")
        x1_squared = sem("x1_squared")
        x1_root = sem("x1_root")
        x1_recip = sem("x1_recip")
        xn2_ready = sem("xn2_ready")
        y_stored = [sem(f"y_stored{a}") for a in range(2)]
        xn_stored = [sem(f"xn_stored{a}") for a in range(2)]
        t2_ready = [sem(f"t2_ready{i}") for i in range(2)]
        t2_free = [sem(f"t2_free{i}") for i in range(2)]
        logits_ready = sem("logits_ready")
        logits_copied = sem("logits_copied")
        logits_turned = sem("logits_turned")
        router_max = sem("router_max")
        router_shifted = sem("router_shifted")
        router_exp = sem("router_exp")
        router_sum = sem("router_sum")
        router_inv = sem("router_inv")
        aff_ready = sem("aff_ready")
        aff_turned = sem("aff_turned")
        aff_copied = sem("aff_copied")
        top_p_step = sem("top_p_step")
        top_s_step = sem("top_s_step")
        flip_made = sem("flip_made")
        padding_made = sem("padding_made")
        top_float = sem("top_float")
        top_copied = sem("top_copied")
        top_flipped = sem("top_flipped")
        idx_chosen = sem("idx_chosen")
        top_turned = sem("top_turned")
        top_ready = sem("top_ready")
        gate_w_loaded = [sem(f"gate_w_loaded{i}") for i in range(NS)]
        up_w_loaded = [sem(f"up_w_loaded{i}") for i in range(NS)]
        down_w_loaded = [sem(f"down_w_loaded{i}") for i in range(NS)]
        idx_copied = sem("idx_copied")
        gathered = sem("gathered")
        gate_ready = sem("gate_ready")
        up_ready = sem("up_ready")
        silu_done = sem("silu_done")
        hid_ready = sem("hid_ready")
        x_turned = sem("x_turned")
        x_scaled = sem("x_scaled")
        down_ready = sem("down_ready")
        y_scaled = sem("y_scaled")
        y_turned = sem("y_turned")
        ye_ready = sem("ye_ready")
        scattered = sem("scattered")
        ye_free = sem("ye_free")
        act_steps = sem("act_steps")
        pool_steps = sem("pool_steps")

        turn_at = {}
        n_turns = [0]

        def order(key, uses):
            turn_at[key] = n_turns[0]
            n_turns[0] += uses

        order(("x", 0), 4)
        for p in range(1, NPAIR + 1):
            if p > 1:
                order(("q", p - 2, 0), 3)
                order(("q", p - 2, 1), 3)
            if p < NPAIR:
                order(("x", p), 4)
        order(("q", NPAIR - 1, 0), 3)
        order(("q", NPAIR - 1, 1), 3)

        def group(p):
            return 1 if p == NPAIR - 1 else 0

        def x_rows(p):
            src = x_s[0] if group(p) else x_p[0, 2 * P * p:2 * P * (p + 1), :]
            return src.rearrange("(a q) d -> q a d", q=P)

        def a_cols(p):
            return A_SAMPLE if group(p) else A_PROMPT + 2 * P * p

        def attention_phases():
            n = 0
            for t0, nt in ((0, SP_TOK // P), (SP_TOK // P, SS_TOK // P)):
                for j in range(NKV):
                    yield j, t0, nt, n
                    n += nt

        phases = list(attention_phases())
        STEPS = sum(ph[2] for ph in phases)
        HEADS_ALL = STEPS * QPK

        def steps_of(eng, nt, step):
            step(0, True, False)
            if nt > 2:
                with eng.Fori(1, nt - 1) as r:
                    step(r, False, False)
            step(nt - 1, False, True)

        def last_tile(i, l, first):
            j, t0, _, s0 = phases[i]
            if first:
                pj, pt0, pnt, _ = phases[i - 1]
                return s0 - 1, pt0 + pnt - 1, pj
            return l + (s0 - 1), l + (t0 - 1), j

        MEAN_BANK = (0, 1, 3)
        VAR_BANK = (1, 1, 3)

        def tile_parts(t_mix, t_c, q):
            o = P * (q % (SPAN // P))
            return t_mix[:, :, P * q:P * (q + 1)], t_c[q // (SPAN // P)][:, :, o:o + P]

        block = ctx.enter_context(nc.Block())

        @block.sync
        def _(sp):
            for r, src, n in ((ROW_C, c_p[0], KC), (ROW_C + KC, c_s[0], KC), (ROW_NMIX, norm_mix[0], KC),
                              (ROW_NFFN, norm_ffn[0], KC), (ROW_CB, conv_b[0], CC), (ROW_LG, ln_g[0], CC),
                              (ROW_LB, ln_b[0], CC), (ROW_AB, ada_b[0], 6 * KC)):
                sp.dma_start(rows[r:r + n, :], src.rearrange("(k q) -> k q", q=P)).then_inc(rows_loaded, 16)
            sp.dma_start(taps_row[:, :], conv_w[0, :, 0, :]).then_inc(rows_loaded, 16)
            ada_view = ada_w[0].rearrange("(k q) (b n) -> b q k n", q=P, n=ADA_BLOCK)
            for b in range(ADA_FIRST):
                if b >= 3:
                    sp.wait_ge(rows_ready, b - 2)
                sp.dma_start(ada[b % 3][:, :, :], ada_view[b]).then_inc(ada_loaded[b % 3], 16)
                if b == 1:
                    sp.dma_start(x_in[:, :, :], x_rows(0)).then_inc(x_loaded, 16)
                    sp.dma_start(gains[:, 0, :], q_norm[0].partition_broadcast(P)).then_inc(gains_loaded, 16)
                    sp.dma_start(gains[:, 1, :], k_norm[0].partition_broadcast(P)).then_inc(gains_loaded, 16)
                    sp.dma_start(cos_sb[:, :, :], rope_cos.rearrange("(t q) i -> q t i", q=P)).then_inc(gains_loaded, 16)
                    sp.dma_start(sin_sb[:, :, :], rope_sin.rearrange("(t q) i -> q t i", q=P)).then_inc(gains_loaded, 16)
            w_view = w_in[0].rearrange("(k q) n -> q k n", q=P)
            sp.dma_start(w_in_sb[:, :, NQKV:], w_view[:, :, NQKV:]).then_inc(wu_loaded, 16)
            sp.dma_start(w_in_sb[:, :, 0:NQKV], w_view[:, :, 0:NQKV]).then_inc(wqkv_loaded, 16)
            sp.dma_start(router[:, :, :], w_router[0].rearrange("(k q) e -> q k e", q=P)).then_inc(router_loaded, 16)
            for p in range(1, NPAIR):
                n = turn_at["x", p - 1] + 3
                sp.wait_ge(t_ready[n % 2], n // 2 + 1)
                sp.dma_start(x_in[:, :, :], x_rows(p)).then_inc(x_loaded, 16)
            n = turn_at["x", NPAIR - 1] + 3
            sp.wait_ge(t_ready[n % 2], n // 2 + 1)
            sp.wait_ge(qkv_ready, 2 * NT - 4)
            for b in range(ADA_FIRST, ADA_LATE):
                i = b - ADA_FIRST
                if i == 1:
                    sp.wait_ge(qkv_ready, 2 * NT)
                if i >= 4:
                    sp.wait_ge(rows_ready, b - 3)
                sp.dma_start(ada2[i % 4][:, :, :], ada_view[b]).then_inc(ada_loaded[i % 4], 16)
            sp.wait_ge(rows_ready, ADA_FIRST + 5)
            sp.wait_ge(scaled, CC)
            sp.dma_start(w_out_sb[:, :, :], w_out[0].rearrange("(k q) n -> q k n", q=P)).then_inc(w_out_loaded, 16)
            gate_view = w_gate[0].rearrange("e (k q) (s n) -> e s q k n", q=P, n=MC)
            up_view = w_up[0].rearrange("e (k q) (s n) -> e s q k n", q=P, n=MC)
            down_view = w_down[0].rearrange("e (k q) (s n) -> e s q k n", q=P, n=MC)
            for p in range(NPAIR):
                if p == 0:
                    sp.wait_ge(conv_out, 3 * CC)
                    sp.wait_ge(out_copied, STEPS + 1)
                else:
                    sp.wait_ge(x1_ready, 2 * p)
                sp.dma_start(x_again[:, :, :], x_rows(p)).then_inc(x_reloaded, 16)
                if p == 0:
                    for i in range(2):
                        sp.dma_start(ada3[i][:, :, :], ada_view[ADA_LATE + i]).then_inc(ada3_loaded, 16)
                for a in range(2):
                    q = 2 * p + a
                    dst_y = y_s[0] if group(p) else y_p[0, 2 * P * p:2 * P * (p + 1)]
                    dst_n = xn_s if group(p) else xn_p[2 * P * p:2 * P * (p + 1)]
                    sp.wait_ge(x1_ready, q + 1)
                    sp.dma_start(dst_y[P * a:P * (a + 1), :], x1[:, a, :]).then_inc(y_stored[a], 16)
                    sp.wait_ge(xn2_ready, q + 1)
                    sp.dma_start(dst_n[P * a:P * (a + 1), :], xn2[:, a, :]).then_inc(xn_stored[a], 16)
            sp.wait_ge(mix_ready, NT)
            for s in range(NS):
                sp.dma_start(gate_w_sb[:, s], gate_view[0, s]).then_inc(gate_w_loaded[s], 16)
            for s in range(NS):
                sp.wait_ge(rows_ready, ADA_LATE + s // 2 + 1)
                sp.dma_start(up_w_sb[:, s], up_view[0, s]).then_inc(up_w_loaded[s], 16)
            sp.wait_ge(gathered, 32)
            for s in range(NS):
                sp.dma_start(down_w_sb[:, s], down_view[0, s]).then_inc(down_w_loaded[s], 16)
            with sp.Fori(1, NE) as e:
                for s in range(NS):
                    m = 2 * s + 1
                    sp.wait_ge(gate_ready, (e - 1) * KC + m + 1)
                    sp.dma_start(gate_w_sb[:, s], gate_view[e, s]).then_inc(gate_w_loaded[s], 16)
                    sp.wait_ge(up_ready, (e - 1) * KC + m + 1)
                    sp.dma_start(up_w_sb[:, s], up_view[e, s]).then_inc(up_w_loaded[s], 16)
                for s in range(NS):
                    m = 2 * s + 1
                    sp.wait_ge(down_ready, (e - 1) * KC + m + 1)
                    sp.dma_start(down_w_sb[:, s], down_view[e, s]).then_inc(down_w_loaded[s], 16)

        @block.gpsimd
        def _(pool):
            pool.memset(ident[:, :], 0.0).then_inc(ident_made, 1)
            pool.memset(ones[:, :], 1.0).then_inc(fills_made, 1)
            pool.memset(eps_col[:, :], EPS).then_inc(fills_made, 1)
            pool.wait_ge(ident_made, 1)
            pool.affine_select(out=ident[:, :], in_=ident[:, :], compare_op=ALU.not_equal, fill=1.0,
                               base=0, pattern=[[-1, P]], channel_multiplier=1).then_inc(ident_made, 1)
            pool.memset(a_t[:, :, 0:A_PROMPT], 0.0).then_inc(fills_made, 1)
            pool.memset(a_t[:, :, A_PROMPT + SP_TOK:A_SAMPLE], 0.0).then_inc(fills_made, 1)
            pool.memset(a_t[:, :, A_SAMPLE + SS_TOK:A_ROW], 0.0).then_inc(fills_made, 1)
            pool.memset(flip[:, :], 0.0).then_inc(flip_made, 1)
            pool.wait_ge(flip_made, 1)
            pool.affine_select(out=flip[:, :], in_=flip[:, :], compare_op=ALU.not_equal, fill=1.0,
                               base=1 - P, pattern=[[1, P]], channel_multiplier=1).then_inc(flip_made, 1)
            pool.memset(v_one[:, :, :, HD:HD + 1], 1.0).then_inc(fills_made, 1)

            for q in range(NT):
                a = q % 2
                pool.wait_ge(qkv_copied, 2 * q + 2)
                if q:
                    pool.wait_ge(rotated, q)
                pool.tensor_tensor(sq[:, :, :], qk[a][:, :, :], qk[a][:, :, :], ALU.mult).then_inc(sq_ready, 1)
                pool.wait_ge(q_normed, q + 1)
                even = qk[a][:, :, :].rearrange("p h (i b) -> p h i b", b=2)
                out = rot2[:, :, :].rearrange("p h (i b) -> p h i b", b=2)
                tab = rope_s[:, q % 8, :, :].rearrange("p g (i b) -> p g i b", b=2)
                for b in range(2):
                    for g, h0, nh in ((0, 0, NH), (1, NH, NKV)):
                        t = tab[:, g:g + 1, :, b].to_broadcast([P, nh, HD // 2])
                        last = pool.tensor_tensor(out[:, h0:h0 + nh, :, b], even[:, h0:h0 + nh, :, 1 - b], t, ALU.mult)
                last.then_inc(rot2_ready, 1)

            for n in (n_turns[0] - 2, n_turns[0] - 1):
                pool.wait_ge(t_free[n % 2], n // 2 + 1)
            pool.wait_ge(rows_ready, ADA_LATE)

            def copy_q(n, h, t, head):
                if n is not None:
                    pool.wait_ge(scores_ready, n - 1)
                pool.tensor_copy(q_now[:, h % 2, :], q_st[:, t, head, :]).then_inc(q_copied, 1)

            j0, t0, _, _ = phases[0]
            copy_q(None, 0, t0, j0 * QPK)
            copy_q(None, 1, t0, j0 * QPK + 1)
            for i, (j, t0, nt, s0) in enumerate(phases):
                follow = (phases[i + 1][0], phases[i + 1][1]) if i + 1 < len(phases) else None

                def ahead(l, first, last):
                    n = (l + s0) * QPK
                    copy_q(n + 2, 2, l + t0, j * QPK + 2)
                    copy_q(n + 3, 3, l + t0, j * QPK + 3)
                    nxt = follow if last else (j, l + (t0 + 1))
                    if nxt is not None:
                        nj, tile = nxt
                        copy_q(n + 4, 0, tile, nj * QPK)
                        copy_q(n + 5, 1, tile, nj * QPK + 1)
                steps_of(pool, nt, ahead)

            for c in range(CC):
                for span in range(len(SPANS)):
                    pool.wait_ge(conv_done[span][c], TAPS)
            pool.memset(aff_h[:, :, 1, :], 0.0).then_inc(padding_made, 1)

            for q in range(NT):
                p, a = q // 2, q % 2
                pool.wait_ge(x_reloaded, 16 * (p + 1))
                pool.wait_ge(mix_gated, q + 1)
                pool.tensor_tensor(x1[:, a, :], x1[:, a, :], x_again[:, a, :], ALU.add).then_inc(x1_ready, 1)

            def fetch(e, n):
                pool.tensor_copy(i_now[:, 0:1], i_top_p[:, bass.ds(e, 1)]).then_inc(idx_copied, 1)
                pool.tensor_copy(i_now[0:CAP_S, 1:2], i_top_s[0:CAP_S, bass.ds(e, 1)]).then_inc(idx_copied, 1)
                pool.wait_ge(idx_copied, n)
                pool.sem_inc(pool_steps, 1)
                pool.indirect_dma_start(xg_p[:, :], None, xn_p, bass.IndirectOffsetOnAxis(i_now[:, 0:1], axis=0)).then_inc(gathered, 16)
                pool.indirect_dma_start(xg_s[:, :], None, xn_s, bass.IndirectOffsetOnAxis(i_now[0:CAP_S, 1:2], axis=0)).then_inc(gathered, 16)

            pool.wait_ge(top_ready, 4)
            pool.wait_ge(fills_made, 6)
            for a in range(2):
                pool.wait_ge(xn_stored[a], 16 * NPAIR)
                pool.wait_ge(y_stored[a], 16 * NPAIR)
            pool.sem_inc(ye_free, 1)
            fetch(0, 2)

            def expert(e, more):
                if more:
                    pool.wait_ge(x_turned, KC * e + KC)
                    fetch(e + 1, 4 * e + 4)
                pool.tensor_copy(i_now[:, 2:3], i_top_p[:, bass.ds(e, 1)]).then_inc(idx_copied, 1)
                pool.tensor_copy(i_now[0:CAP_S, 3:4], i_top_s[0:CAP_S, bass.ds(e, 1)]).then_inc(idx_copied, 1)
                pool.wait_ge(idx_copied, 4 * e + (6 if more else 4))
                pool.wait_ge(ye_ready, 4 * e + 5)
                pool.sem_inc(pool_steps, 1)
                pool.indirect_dma_start(y_p[0], bass.IndirectOffsetOnAxis(i_now[:, 2:3], axis=0), ye_p[:, :], None,
                                        compute_op=ALU.add).then_inc(scattered, 16)
                pool.indirect_dma_start(y_s[0], bass.IndirectOffsetOnAxis(i_now[0:CAP_S, 3:4], axis=0), ye_s[:, :], None,
                                        compute_op=ALU.add).then_inc(scattered, 16)
                pool.wait_ge(scattered, 32 * e + 32)
                pool.sem_inc(ye_free, 1)

            with pool.Fori(0, NE - 1) as e:
                expert(e, True)
            expert(NE - 1, False)

        @block.scalar
        def _(act):
            act.wait_ge(cols_ready, 1)
            act.activation(silu_c[:, :], cols[:, ROW_C:ROW_C + 2 * KC], ACT.Silu).then_inc(silu_ready, 1)

            def copy_rows(b):
                act.wait_ge(rows_ready, b + 1)
                if b >= 2:
                    act.wait_ge(rows_turned, b - 1)
                act.activation(mod_rows[:, b % 2, :], bank(2 + b % 2)[0:2, :], ACT.Copy).then_inc(rows_copied, 1)

            for b in range(ADA_FIRST):
                copy_rows(b)

            def square_x(p):
                act.wait_ge(x_loaded, 16 * (p + 1))
                if p:
                    act.wait_ge(x_recip, p)
                for a in range(2):
                    if p or a:
                        act.wait_ge(x_squared, 2 * p + a)
                    act.activation(junk[:, :], x_in[:, a, :], ACT.Square, accum_out=ss_x[:, a:a + 1]).then_inc(x_squared, 1)
                act.wait_ge(x_squared, 2 * p + 2)
                act.activation(rt_x[:, :], ss_x[:, :], ACT.Sqrt, scale=1.0 / D, bias=eps_col[:, :]).then_inc(x_root, 1)

            def x_out(p, i):
                n = turn_at["x", p] + i
                act.wait_ge(t_ready[n % 2], n // 2 + 1)
                for c in range(2):
                    k = 2 * i + c
                    last = act.activation(h_t[:, (p + 1) % 2, k, :], bank(n % 2)[:, 256 * c:256 * (c + 1)], ACT.Identity,
                                          scale=a1[:, k, group(p):group(p) + 1],
                                          bias=mod[:, SHIFT1 + k, group(p):group(p) + 1])
                last.then_inc(t_free[n % 2], 1)

            def high_out(p, a, i):
                t = 2 * p + a
                n = turn_at["q", p, a] + i
                act.wait_ge(t_ready[n % 2], n // 2 + 1)
                if i < 2:
                    src = bank(n % 2)[0:HD, :].rearrange("d (h q) -> d h q", h=4)
                    last = act.activation(q_st[0:HD, t, 4 * i:4 * i + 4, :], src, ACT.Copy)
                else:
                    src = bank(n % 2)[0:HD, 0:NKV * P].rearrange("d (j q) -> d j q", j=NKV)
                    act.activation(k_hi[0:HD, :, P * t:P * (t + 1)], src, ACT.Copy)
                    last = act.activation(k_hi[HD:P, :, P * t:P * (t + 1)], src, ACT.Copy)
                last.then_inc(high_ready, 1)

            def copies(p, a):
                q = 2 * p + a
                if q >= 2:
                    n = turn_at["q", p - 1, a] + 2
                    act.wait_ge(t_ready[n % 2], n // 2 + 1)
                act.wait_ge(qkv_ready, 2 * q + 1)
                act.activation(qk[a][:, 0:NH, :], bank(4 + a).rearrange("p (h d) -> p h d", h=NH), ACT.Copy).then_inc(qkv_copied, 1)
                act.wait_ge(qkv_ready, 2 * q + 2)
                act.activation(qk[a][:, NH:NH + NKV, :], bank(6 + a)[:, 0:DKV].rearrange("p (h d) -> p h d", h=NKV), ACT.Copy)
                act.activation(v_one[:, q, :, 0:HD], bank(6 + a)[:, DKV:2 * DKV].rearrange("p (h d) -> p h d", h=NKV),
                               ACT.Copy).then_inc(qkv_copied, 1)
                act.wait_ge(sq_summed, q + 1)
                act.activation(rt_q[:, a, :], ss_q[:, a, :], ACT.Sqrt, scale=1.0 / HD, bias=eps_col[:, :]).then_inc(q_root, 1)

            def sigmoid(p, i):
                n = CC * p + i
                act.wait_ge(u_ready, n + 1)
                if n >= 2:
                    act.wait_ge(u_gated, n - 1)
                act.activation(sig[:, n % 2, :], bank(2 + n % 2)[:, 256:512], ACT.Sigmoid).then_inc(sig_ready, 1)

            act.wait_ge(fills_made, 6)
            square_x(0)
            act.wait_ge(scale_ready, 1)
            x_out(0, 0)
            x_out(0, 2)
            for p in range(NPAIR):
                if p + 1 < NPAIR:
                    square_x(p + 1)
                sigmoid(p, 0)
                if p:
                    high_out(p - 1, 0, 0)
                    high_out(p - 1, 0, 1)
                sigmoid(p, 1)
                if p:
                    high_out(p - 1, 0, 2)
                    high_out(p - 1, 1, 0)
                    high_out(p - 1, 1, 1)
                sigmoid(p, 2)
                if p:
                    high_out(p - 1, 1, 2)
                if p + 1 < NPAIR:
                    x_out(p + 1, 0)
                sigmoid(p, 3)
                if p + 1 < NPAIR:
                    x_out(p + 1, 2)
                copies(p, 0)
                copies(p, 1)
            copy_rows(ADA_FIRST)
            for a in range(2):
                for i in range(3):
                    high_out(NPAIR - 1, a, i)

            def squares(s):
                for c in range(CC):
                    act.wait_ge(centred, CC * s + c + 1)
                    act.activation(sq_c[s][:, c, :], c_t[s][:, c, :], ACT.Square).then_inc(squared, 1)

            def root(s):
                n = SPANS[s][1]
                act.wait_ge(var_ready, s + 1)
                act.activation(rt_c[s][:, :], bank(VAR_BANK[s])[:, 0:n], ACT.Sqrt, scale=1.0 / DC, bias=eps_col[:, :]).then_inc(root_ready, 1)

            def silu_span(s):
                for c in range(CC):
                    act.wait_ge(scaled, CC * s + c + 1)
                    act.activation(c_t[s][:, c, :], c_t[s][:, c, :], ACT.Silu, scale=cols[:, ROW_LG + c:ROW_LG + c + 1],
                                   bias=cols[:, ROW_LB + c:ROW_LB + c + 1]).then_inc(conv_out, 1)

            def gate_row_out(n):
                act.wait_ge(gate_rows_ready, n + 1)
                act.activation(gate1_row[:, n // 2, 512 * (n % 2):512 * (n % 2) + 512], bank(4 + n % 2), ACT.Copy).then_inc(gate_rows_copied, 1)

            for b in range(ADA_FIRST + 1, ADA_LATE):
                copy_rows(b)
                if b == ADA_FIRST + 3:
                    gate_row_out(0)
                    gate_row_out(1)
                if b == ADA_FIRST + 4:
                    gate_row_out(2)
                    gate_row_out(3)
                    squares(0)
                if b == ADA_FIRST + 5:
                    root(0)

            act.sem_inc(turn_bank_free, 2)

            def exponent(n, h, nk):
                act.wait_ge(max_ready, n + 1)
                act.activation(probs[:, h % 2, 0:P * nk], two[h % 2][:, :, :].rearrange("p b n -> p (b n)")[:, 0:P * nk], ACT.Exp,
                               bias=negmax[:, h:h + 1]).then_inc(probs_ready, 1)

            def probs_out(n, h, nk):
                act.wait_ge(weighed, n + 1)
                for half in range(2):
                    act.wait_ge(turned, 2 * n + half + 1)
                    kk = nk // 2
                    act.activation(probs_t[:, kk * half:kk * half + kk, h, :],
                                   bank(4 + half)[:, 0:kk * P].rearrange("p (k q) -> p k q", k=kk), ACT.Copy).then_inc(turn_bank_free, 1)

            def mix_out(step, t, j):
                act.wait_ge(out_turned, step + 1)
                act.sem_inc(act_steps, 1)
                act.activation(mix_t[:, 2 * j:2 * j + 2, bass.ds(t * P, P)], bank(7)[:, 0:2 * P].rearrange("p (c q) -> p c q", c=2),
                               ACT.Copy).then_inc(out_copied, 1)

            def high_weights(k):
                act.wait_ge(w_out_loaded, 16)
                act.wait_ge(q_copied, SP_TOK // P * NKV * QPK)
                act.activation(w_hi[:, k, :], w_out_sb[:, k, :], ACT.Copy).then_inc(w_hi_ready, 1)

            def tile_high(q):
                if q >= 2:
                    act.wait_ge(mix_ready, q - 1)
                act.wait_ge(out_copied, (phases[1][3] + q if q < PROMPT_TILES else phases[3][3] + q - PROMPT_TILES) + 2)
                act.wait_ge(conv_out, CC * (q // (SPAN // P) + 1))
                attn, conv = tile_parts(mix_t, c_t, q)
                act.activation(s_hi[:, q % 2, 0:CC, :], attn, ACT.Copy)
                act.activation(s_hi[:, q % 2, CC:KC, :], conv, ACT.Copy).then_inc(s_hi_ready, 1)

            exponent(0, 0, phases[0][2])
            for i, (j, t0, nt, s0) in enumerate(phases):
                def soft(l, first, last):
                    n = (l + s0) * QPK
                    nxt_nk = nt if not last else phases[i + 1][2] if i + 1 < len(phases) else None
                    for h in range(QPK):
                        if h + 1 < QPK:
                            exponent(n + h + 1, h + 1, nt)
                        elif nxt_nk is not None:
                            exponent(n + QPK, 0, nxt_nk)
                        probs_out(n + h, h, nt)
                        if h == 2 and not (first and i == 0):
                            mix_out(*last_tile(i, l, first))
                if t0 == 0:
                    steps_of(act, nt, soft)
                    if j == 0:
                        silu_span(0)
                else:
                    soft(0, True, False)
                    for k in range(3 if j == 0 else 2):
                        high_weights(6 * j + k)
                    if j == 1:
                        squares(2)
                    soft(1, False, True)
                    if j == 0:
                        for k in range(3, 6):
                            high_weights(k)
                    if j == 1:
                        tile_high(0)
                        tile_high(1)
                    if j == 0:
                        squares(1)
            mix_out(*last_tile(len(phases) - 1, phases[-1][2], False))
            root(1)
            root(2)
            silu_span(1)
            silu_span(2)

            def norm2(q):
                a = q % 2
                act.wait_ge(x1_ready, q + 1)
                if q >= 2:
                    act.wait_ge(xn_stored[a], 16 * (q // 2))
                    act.wait_ge(t2_ready[1], 2 * ((q - 2) // 2) + 2)
                if q:
                    act.wait_ge(x1_recip, q)
                act.activation(xn2[:, a, :], x1[:, a, :], ACT.Square, accum_out=ss_x[:, 0:1]).then_inc(x1_squared, 1)
                act.wait_ge(x1_squared, q + 1)
                act.activation(rt_x[:, 0:1], ss_x[:, 0:1], ACT.Sqrt, scale=1.0 / D, bias=eps_col[:, :]).then_inc(x1_root, 1)

            def h2_out(p):
                if p:
                    act.wait_ge(logits_ready, p)
                for i in range(0, 4, 2):
                    n = 4 * p + i
                    act.wait_ge(t2_ready[n % 2], n // 2 + 1)
                    for c in range(2):
                        k = 2 * i + c
                        last = act.activation(h2_t[:, k, :], bank(4 + n % 2)[:, 256 * c:256 * (c + 1)], ACT.Identity,
                                              scale=a2[:, k, group(p):group(p) + 1],
                                              bias=mod[:, SHIFT2 + k, group(p):group(p) + 1])
                    last.then_inc(t2_free[n % 2], 1)

            def logits_out(p):
                act.wait_ge(logits_ready, p + 1)
                act.activation(logits_t[:, 2 * P * p:2 * P * (p + 1)], bank(6)[0:NE, 0:2 * P], ACT.Copy).then_inc(logits_copied, 1)

            tile_high(2)
            for p in range(NPAIR - 1):
                norm2(2 * p)
                tile_high(2 * p + 3)
                norm2(2 * p + 1)
                h2_out(p)
                if p < NPAIR - 2:
                    tile_high(2 * p + 4)
                logits_out(p)

            def exp_logits(g, v):
                act.wait_ge(router_shifted, g + 1)
                act.activation(v, v, ACT.Exp).then_inc(router_exp, 1)

            exp_logits(0, aff_h[:, :, 0:3:2, :])
            norm2(2 * NPAIR - 2)
            norm2(2 * NPAIR - 1)
            copy_rows(ADA_LATE)
            h2_out(NPAIR - 1)
            logits_out(NPAIR - 1)
            exp_logits(1, aff_r[:, :, :])
            copy_rows(ADA_LATE + 1)

            def y_out(e, half):
                act.wait_ge(y_turned, 2 * e + half + 1)
                act.sem_inc(act_steps, 1)
                act.activation(ye_p[:, 512 * half:512 * half + 512], bank(6), ACT.Copy,
                               scale=g_top_p[:, bass.ds(e, 1)]).then_inc(ye_ready, 1)
                act.activation(ye_s[:, 512 * half:512 * half + 512], bank(7)[0:CAP_S, :], ACT.Copy,
                               scale=g_top_s[0:CAP_S, bass.ds(e, 1)]).then_inc(ye_ready, 1)

            act.wait_ge(top_ready, 4)
            act.sem_inc(ye_ready, 1)
            with act.Fori(0, NE) as e:
                for m in range(KC):
                    act.wait_ge(gate_ready, e * KC + m + 1)
                    act.activation(sil[:, m % 2, :], bank(m % 2)[:, 0:CAP], ACT.Silu).then_inc(silu_done, 1)
                act.wait_ge(ye_free, e + 1)
                y_out(e, 0)
                y_out(e, 1)

        @block.tensor
        def _(pe):
            pe.wait_ge(ident_made, 2)
            pe.wait_ge(rows_loaded, 16 * 9)
            pe.transpose(bank(0)[:, 0:ROWS], rows[:, :], ident[0:ROWS, 0:ROWS])
            for c in range(CC):
                last = pe.transpose(bank(0)[:, 128 + TAPS * c:128 + TAPS * (c + 1)], taps_row[:, P * c:P * (c + 1)],
                                    ident[0:TAPS, 0:TAPS])
            last.then_inc(cols_turned, 1)

            silu_pair = silu_c[:, :].rearrange("p (g k) -> p k g", g=2)

            def mod_block(b, w, loads):
                if b == 0:
                    pe.wait_ge(silu_ready, 1)
                if b >= 2:
                    pe.wait_ge(rows_copied, b - 1)
                pe.wait_ge(ada_loaded[loads[0]], 16 * loads[1])
                mod_product(b, w)

            def mod_product(b, w):
                for k in range(KC):
                    last = pe.matmul(bank(2 + b % 2)[0:2, :], silu_pair[:, k, :], w[:, k, :], start=(k == 0), stop=(k == KC - 1))
                last.then_inc(rows_ready, 1)

            def mod_turn(b, out=7):
                pe.wait_ge(rows_copied, b + 1)
                for j in range(4):
                    last = pe.transpose(bank(out)[:, 2 * (4 * b + j):2 * (4 * b + j) + 2], mod_rows[:, b % 2, P * j:P * (j + 1)],
                                        ident[0:2, 0:2])
                last.then_inc(rows_turned, 1)

            for b in range(ADA_FIRST):
                mod_block(b, ada[b % 3], (b % 3, b // 3 + 1))
                if b:
                    mod_turn(b - 1)
            mod_turn(ADA_FIRST - 1)

            def turn_x(p, i):
                n = turn_at["x", p] + i
                pe.wait_ge(x_normed, 2 * p + 2)
                if n >= 2:
                    pe.wait_ge(t_free[n % 2], n // 2)
                for c in range(2):
                    for a in range(2):
                        last = pe.transpose(bank(n % 2)[:, 256 * c + P * a:256 * c + P * (a + 1)],
                                            x_in[:, a, P * (2 * i + c):P * (2 * i + c + 1)], ident[:, :])
                last.then_inc(t_ready[n % 2], 1)

            def turn_q(p, a, i):
                n = turn_at["q", p, a] + i
                pe.wait_ge(rotated, 2 * p + a + 1)
                pe.wait_ge(t_free[n % 2], n // 2)
                for h in range(4 if i < 2 else NKV):
                    last = pe.transpose(bank(n % 2)[0:HD, P * h:P * (h + 1)], qk[a][:, 4 * i + h, :], ident[:, :])
                last.then_inc(t_ready[n % 2], 1)

            def project_u(p, i, part):
                if i == 0 and part == 0:
                    for b in range(2):
                        n = turn_at["x", p] + 2 + b
                        pe.wait_ge(t_free[n % 2], n // 2 + 1)
                n = CC * p + i
                if n >= 2:
                    pe.wait_ge(u_gated, n - 1)
                col = NQKV + DC * part + P * i
                for k in range(KC):
                    last = pe.matmul(bank(2 + n % 2)[:, 256 * part:256 * part + 256], w_in_sb[:, k, col:col + P],
                                     h_t[:, (p + 1) % 2, k, :], start=(k == 0), stop=(k == KC - 1))
                if part == 1:
                    last.then_inc(u_ready, 1)

            def project_qkv(p, a):
                q = 2 * p + a
                if q >= 2:
                    pe.wait_ge(qkv_copied, 2 * q - 2)
                for b, c0, n in ((4 + a, 0, DA), (6 + a, DA, 2 * DKV)):
                    for k in range(KC):
                        last = pe.matmul(bank(b)[:, 0:n], h_t[:, (p + 1) % 2, k, P * a:P * (a + 1)], w_in_sb[:, k, c0:c0 + n],
                                         start=(k == 0), stop=(k == KC - 1))
                    last.then_inc(qkv_ready, 1)

            for i in range(4):
                turn_x(0, i)
            pe.wait_ge(wu_loaded, 16)
            pe.wait_ge(rows_copied, ADA_FIRST)
            for p in range(NPAIR):
                project_u(p, 0, 0)
                project_u(p, 0, 1)
                project_u(p, 1, 0)
                if p:
                    turn_q(p - 1, 0, 0)
                    turn_q(p - 1, 0, 1)
                project_u(p, 1, 1)
                if p:
                    turn_q(p - 1, 0, 2)
                project_u(p, 2, 0)
                if p:
                    turn_q(p - 1, 1, 0)
                    turn_q(p - 1, 1, 1)
                project_u(p, 2, 1)
                if p:
                    turn_q(p - 1, 1, 2)
                project_u(p, 3, 0)
                if p + 1 < NPAIR:
                    turn_x(p + 1, 0)
                    turn_x(p + 1, 1)
                project_u(p, 3, 1)
                if p + 1 < NPAIR:
                    turn_x(p + 1, 2)
                    turn_x(p + 1, 3)
                if p == 0:
                    pe.wait_ge(wqkv_loaded, 16)
                    pe.wait_ge(mod_ready, 1)
                project_qkv(p, 0)
                project_qkv(p, 1)

            def mod_block2(b):
                i = b - ADA_FIRST
                prior = 1 + (ADA_FIRST - 1 - i % 4) // 3 if i % 4 < 3 else 0
                mod_block(b, ada2[i % 4], (i % 4, prior + i // 4 + 1))

            pe.wait_ge(u_gated, CC * NPAIR)
            mod_block2(ADA_FIRST)
            for a in range(2):
                for i in range(3):
                    turn_q(NPAIR - 1, a, i)
            pe.wait_ge(qkv_copied, 2 * NT)
            def mean(s):
                for c in range(CC):
                    pe.wait_ge(conv_done[s][c], TAPS)
                    last = pe.matmul(bank(MEAN_BANK[s])[:, 0:SPANS[s][1]], ones[:, :], c_t[s][:, c, :], start=(c == 0), stop=(c == CC - 1))
                last.then_inc(mean_ready, 1)

            def variance(s):
                pe.wait_ge(squared, CC * (s + 1))
                for c in range(CC):
                    last = pe.matmul(bank(VAR_BANK[s])[:, 0:SPANS[s][1]], ones[:, :], sq_c[s][:, c, :], start=(c == 0), stop=(c == CC - 1))
                last.then_inc(var_ready, 1)

            def gate_row(n):
                pe.wait_ge(diag_ready, 4 * n + 4)
                if n >= 2:
                    pe.wait_ge(gate_rows_copied, n - 1)
                for i in range(4):
                    last = pe.matmul(bank(4 + n % 2)[:, P * i:P * (i + 1)], ones[:, :], diag[n // 2][:, n % 2, i, :], start=True, stop=True)
                last.then_inc(gate_rows_ready, 1)

            last_turn = n_turns[0] - 1
            for b in range(ADA_FIRST + 1, ADA_LATE):
                mod_block2(b)
                if b == ADA_FIRST + 3:
                    pe.wait_ge(mod_ready, 2)
                mod_turn(b - 1)
                if b == ADA_FIRST + 3:
                    gate_row(0)
                    gate_row(1)
                if b == ADA_FIRST + 4:
                    gate_row(2)
                    gate_row(3)
                    for n in (last_turn - 1, last_turn):
                        pe.wait_ge(t_free[n % 2], n // 2 + 1)
                    mean(0)
                if b == ADA_FIRST + 5:
                    variance(0)
            mod_turn(ADA_LATE - 1)

            pe.wait_ge(gate_rows_copied, 4)
            pe.wait_ge(centred, CC)
            pe.wait_ge(root_ready, 1)

            def scores(n, h, j, t0, nk, first=False):
                pe.wait_ge(q_copied, n + 1)
                if not first:
                    pe.wait_ge(probs_ready, n - 1)
                k0 = P * t0
                for c in range(0, P * nk, 512):
                    w = min(512, P * nk - c)
                    for part, ks in enumerate((k_hi, k_lo)):
                        last = pe.matmul(two[h % 2][:, c // 512, 0:w], q_now[:, h % 2, :], ks[:, j, k0 + c:k0 + c + w],
                                         start=(part == 0), stop=(part == 1))
                last.then_inc(scores_ready, 1)

            def turn_probs(n, h, nk):
                pe.wait_ge(probs_ready, n + 1)
                kk = nk // 2
                for half in range(2):
                    pe.wait_ge(turn_bank_free, 2 * n + half + 1)
                    for k in range(kk):
                        last = pe.transpose(bank(4 + half)[:, P * k:P * (k + 1)],
                                            probs[:, h % 2, P * (kk * half + k):P * (kk * half + k + 1)], ident[:, :])
                    last.then_inc(turned, 1)

            def weigh(n, step, h, j, t0, nk):
                pe.wait_ge(turn_bank_free, 2 * n + 4)
                if h == 0:
                    pe.wait_ge(out_divided, step + 1)
                for k in range(nk):
                    last = pe.matmul(bank(6)[:, (HD + 1) * h:(HD + 1) * (h + 1)], probs_t[:, k, h, :], v_one[:, t0 + k, j, :],
                                     start=(k == 0), stop=(k == nk - 1))
                last.then_inc(weighed, 1)

            def turn_out(step):
                pe.wait_ge(out_divided, step + 2)
                pe.wait_ge(out_copied, step + 1)
                for c in range(2):
                    last = pe.transpose(bank(7)[:, P * c:P * (c + 1)],
                                        out_rows[:, 2 * c:2 * c + 2, :].rearrange("q h d -> q (h d)"), ident[:, :])
                last.then_inc(out_turned, 1)

            pe.sem_inc(weighed, QPK)
            pe.sem_inc(out_divided, 1)
            pe.sem_inc(out_copied, 1)
            j0, t00, nt0, _ = phases[0]
            scores(0, 0, j0, t00, nt0, first=True)
            scores(1, 1, j0, t00, nt0, first=True)
            for i, (j, t0, nt, s0) in enumerate(phases):
                def attend(l, first, last):
                    step = l + s0
                    n = step * QPK
                    ahead = (j, t0, nt) if not last else phases[i + 1][0:3] if i + 1 < len(phases) else None
                    behind = (j, t0, nt) if not first else phases[i - 1][0:3] if i else None
                    for h in range(QPK):
                        turn_probs(n + h, h, nt)
                        if h < 2:
                            scores(n + h + 2, h + 2, j, t0, nt)
                        elif ahead is not None:
                            scores(n + h + 2, h - 2, *ahead)
                        if h:
                            weigh(n + h - 1, step, h - 1, j, t0, nt)
                        elif behind is not None:
                            weigh(n - 1, step, QPK - 1, *behind)
                        if h == 2 and behind is not None:
                            turn_out(l + (s0 - 1))
                if t0 == 0:
                    steps_of(pe, nt, attend)
                elif j == 0:
                    attend(0, True, False)
                    pe.wait_ge(probs_ready, s0 * QPK)
                    mean(1)
                    attend(1, False, True)
                    mean(2)
                else:
                    attend(0, True, False)
                    variance(1)
                    attend(1, False, True)
            weigh(HEADS_ALL - 1, STEPS - 1, QPK - 1, *phases[-1][0:3])
            turn_out(STEPS - 1)
            variance(2)
            pe.wait_ge(probs_ready, HEADS_ALL)

            def project_out(q, half):
                if q >= 2:
                    pe.wait_ge(mix_gated, q - 1)
                attn, conv = tile_parts(mix_lo, c_lo, q)
                pe.wait_ge(s_lo_ready, q + 1)
                for k in range(KC):
                    high = s_hi[:, q % 2, k, :]
                    low = attn[:, k, :] if k < CC else conv[:, k - CC, :]
                    for i, (s, w) in enumerate(((high, w_hi), (high, w_lo), (low, w_hi))):
                        last = pe.matmul(two[q % 2][:, half, :], s, w[:, k, 512 * half:512 * half + 512],
                                         start=(k == 0 and i == 0), stop=(k == KC - 1 and i == 2))
                if half == 1:
                    last.then_inc(mix_ready, 1)

            def turn_x1(p):
                pe.wait_ge(xn2_ready, 2 * p + 2)
                for i in range(4):
                    n = 4 * p + i
                    if n >= 2:
                        pe.wait_ge(t2_free[n % 2], n // 2)
                    for c in range(2):
                        for a in range(2):
                            last = pe.transpose(bank(4 + n % 2)[:, 256 * c + P * a:256 * c + P * (a + 1)],
                                                xn2[:, a, P * (2 * i + c):P * (2 * i + c + 1)], ident[:, :])
                    last.then_inc(t2_ready[n % 2], 1)

            def route(p):
                for b in range(2):
                    pe.wait_ge(t2_free[b], 2 * p + 2)
                if p:
                    pe.wait_ge(logits_copied, p)
                for k in range(KC):
                    last = pe.matmul(bank(6)[0:NE, 0:2 * P], router[:, k, :], h2_t[:, k, :], start=(k == 0), stop=(k == KC - 1))
                last.then_inc(logits_ready, 1)

            pe.wait_ge(w_lo_ready, KC)
            pe.wait_ge(root_ready, 3)
            pe.wait_ge(out_copied, STEPS + 1)
            pe.wait_ge(router_loaded, 16)
            for p in range(NPAIR - 1):
                project_out(2 * p, 0)
                project_out(2 * p, 1)
                if p:
                    turn_x1(p - 1)
                project_out(2 * p + 1, 0)
                project_out(2 * p + 1, 1)
                if p:
                    route(p - 1)

            def mod_block3(b):
                pe.wait_ge(ada3_loaded, 32)
                mod_product(b, ada3[b - ADA_LATE])

            def turn_logits(p0, p1):
                pe.wait_ge(logits_copied, p1)
                for t in range(2 * p0, 2 * p1):
                    i = 2 * (t % HT) + t // HT if t < 2 * HT else t
                    last = pe.transpose(bank(7)[:, NE * i:NE * (i + 1)], logits_t[:, P * t:P * (t + 1)], ident[0:NE, 0:NE])
                last.then_inc(logits_turned, 1)

            project_out(2 * NPAIR - 2, 0)
            turn_x1(NPAIR - 2)
            route(NPAIR - 2)
            turn_logits(0, NPAIR - 1)
            pe.wait_ge(aff_ready, 1)
            pe.wait_ge(padding_made, 1)
            for i in range(HT):
                last = pe.transpose(bank(4)[0:RANKED, P * i:P * (i + 1)], aff_h[:, i, :, :].rearrange("p h e -> p (h e)"), ident[:, :])
            last.then_inc(aff_turned, 1)
            project_out(2 * NPAIR - 2, 1)
            project_out(2 * NPAIR - 1, 0)
            project_out(2 * NPAIR - 1, 1)
            pe.wait_ge(mix_gated, NT)
            mod_block3(ADA_LATE)
            pe.wait_ge(aff_copied, 1)
            turn_x1(NPAIR - 1)
            route(NPAIR - 1)
            turn_logits(NPAIR - 1, NPAIR)
            pe.wait_ge(aff_ready, 2)
            for t in range(SP_TOK // P, NT):
                o = 256 + P * (t - SP_TOK // P)
                last = pe.transpose(bank(7)[0:NE, o:o + P], aff_r[:, t - SP_TOK // P, :], ident[:, :])
            last.then_inc(aff_turned, 1)
            mod_block3(ADA_LATE + 1)
            mod_turn(ADA_LATE, 1)
            mod_turn(ADA_LATE + 1, 1)
            pe.wait_ge(top_float, 4)
            for i in range(2):
                pe.transpose(bank(0)[:, RANKED * i:RANKED * (i + 1)], top_p[:, i, :], ident[0:RANKED, 0:RANKED])
            for i in range(2):
                last = pe.transpose(bank(0)[0:CAP_S, 2 * RANKED + NE * i:2 * RANKED + NE * (i + 1)], top_s[:, i, :], ident[0:NE, 0:NE])
            last.then_inc(top_turned, 1)
            pe.wait_ge(top_copied, 1)
            pe.wait_ge(flip_made, 2)
            pe.matmul(bank(4)[:, 0:2 * NE], flip[:, :], top_sb[:, :, LOW2:RANKED], start=True, stop=True).then_inc(top_flipped, 1)

            def turn_token(e, k):
                pe.transpose(bank(k % 2)[:, 0:CAP_P], xg_p[:, P * k:P * (k + 1)], ident[:, :])
                pe.transpose(bank(k % 2)[:, CAP_P:CAP], xg_s[:, P * k:P * (k + 1)], ident[0:CAP_S, 0:CAP_S]).then_inc(x_turned, 1)

            def turn_y(e, m):
                pe.wait_ge(y_scaled, e * KC + m + 3)
                if m % 4 == 0:
                    pe.wait_ge(ye_ready, 4 * e + 1 + m // 2)
                o = P * (m % 4)
                pe.transpose(bank(6)[:, o:o + P], y_t[:, m, 0:CAP_P], ident[:, :])
                last = pe.transpose(bank(7)[0:CAP_S, o:o + P], y_t[:, m, CAP_P:CAP], ident[:, :])
                if m % 4 == 3:
                    last.then_inc(y_turned, 1)

            def columns(b, w, m, x, ready, n):
                for k in range(KC):
                    if ready is not None:
                        pe.wait_ge(ready, n + k + 1)
                    last = pe.matmul(bank(b)[:, 0:CAP], w[:, m // 2, k, P * (m % 2):P * (m % 2) + P], x[:, k, :],
                                     start=(k == 0), stop=(k == KC - 1))
                return last

            def expert(e, more):
                pe.wait_ge(x_scaled, KC * e + KC)
                for m in range(KC):
                    pe.wait_ge(hid_ready, KC * e + m + 1)
                    if m % 2 == 0:
                        pe.wait_ge(gate_w_loaded[m // 2], 16 * e + 16)
                    columns(m % 2, gate_w_sb, m, xe_t, None, 0).then_inc(gate_ready, 1)
                    if m % 2 == 0:
                        pe.wait_ge(up_w_loaded[m // 2], 16 * e + 16)
                    columns(2 + m % 2, up_w_sb, m, xe_t, None, 0).then_inc(up_ready, 1)
                for m in range(KC):
                    pe.wait_ge(y_scaled, KC * e + m + 1)
                    if m % 2 == 0:
                        pe.wait_ge(down_w_loaded[m // 2], 16 * e + 16)
                    columns(4 + m % 2, down_w_sb, m, hid, hid_ready if m == 0 else None, KC * e + 2).then_inc(down_ready, 1)
                    if more:
                        if m == 0:
                            pe.wait_ge(gathered, 32 * e + 64)
                        if m >= 2:
                            pe.wait_ge(x_scaled, KC * e + KC + m - 1)
                        turn_token(e + 1, m)
                    if m:
                        turn_y(e, m - 1)
                turn_y(e, KC - 1)

            pe.wait_ge(gathered, 32)
            pe.wait_ge(top_ready, 4)
            for k in range(KC):
                if k >= 2:
                    pe.wait_ge(x_scaled, k - 1)
                turn_token(0, k)
            with pe.Fori(0, NE - 1) as e:
                expert(e, True)
            expert(NE - 1, False)

        @block.vector
        def _(dve):
            dve.wait_ge(cols_turned, 1)
            dve.tensor_copy(cols[:, :], bank(0)[:, 0:ROWS]).then_inc(cols_ready, 1)
            dve.tensor_copy(taps[:, :, :], bank(0)[:, 128:128 + CC * TAPS].rearrange("p (c t) -> p c t", c=CC)).then_inc(cols_ready, 1)
            dve.wait_ge(gains_loaded, 64)
            dve.tensor_scalar(gains[:, 0, :], gains[:, 0, :], HD ** -0.5, None, ALU.mult).then_inc(gains_scaled, 1)
            dve.wait_ge(gains_scaled, 1)
            dve.tensor_scalar(ngains[:, :, :], gains[:, :, :], -1.0, None, ALU.mult).then_inc(gains_scaled, 1)
            dve.wait_ge(gains_scaled, 2)
            for g in range(2):
                gain = gains[:, g, :].rearrange("p (i b) -> p i b", b=2)
                ngain = ngains[:, g, :].rearrange("p (i b) -> p i b", b=2)
                out_c = rope_c[:, :, g, :].rearrange("p t (i b) -> p t i b", b=2)
                out_s = rope_s[:, :, g, :].rearrange("p t (i b) -> p t i b", b=2)

                def over_tiles(v):
                    return v.unsqueeze(1).to_broadcast([P, 8, HD // 2])
                for b in range(2):
                    dve.tensor_tensor(out_c[:, :, :, b], cos_sb[:, :, :], over_tiles(gain[:, :, b]), ALU.mult).then_inc(tables_ready, 1)
                dve.tensor_tensor(out_s[:, :, :, 0], sin_sb[:, :, :], over_tiles(ngain[:, :, 1]), ALU.mult).then_inc(tables_ready, 1)
                dve.tensor_tensor(out_s[:, :, :, 1], sin_sb[:, :, :], over_tiles(gain[:, :, 0]), ALU.mult).then_inc(tables_ready, 1)

            def norm_x(p):
                dve.wait_ge(x_root, p + 1)
                dve.reciprocal(rs_x[:, :], rt_x[:, :]).then_inc(x_recip, 1)
                dve.wait_ge(x_recip, p + 1)
                for a in range(2):
                    dve.tensor_scalar(x_in[:, a, :], x_in[:, a, :], rs_x[:, a:a + 1], None, ALU.mult).then_inc(x_normed, 1)

            norm_x(0)
            dve.wait_ge(rows_turned, ADA_FIRST)
            dve.wait_ge(cols_ready, 2)

            def mod_cols(c0, c1, turned=7):
                bias = cols[:, ROW_AB + c0:ROW_AB + c1].unsqueeze(2).to_broadcast([P, c1 - c0, 2])
                dve.tensor_tensor(mod[:, c0:c1, :], bank(turned)[:, 2 * c0:2 * c1].rearrange("p (c g) -> p c g", g=2), bias,
                                  ALU.add).then_inc(mod_ready, 1)

            mod_cols(0, GATE1)
            dve.wait_ge(mod_ready, 1)

            def scale_of(out, norm_row, scale_col):
                gain = cols[:, norm_row:norm_row + KC].unsqueeze(2).to_broadcast([P, KC, 2])
                dve.scalar_tensor_tensor(out=out[:, :, :], in0=mod[:, scale_col:scale_col + KC, :], scalar=1.0, in1=gain,
                                         op0=ALU.add, op1=ALU.mult).then_inc(scale_ready, 1)

            scale_of(a1, ROW_NMIX, SCALE1)
            dve.wait_ge(scale_ready, 1)

            def x_out(p, i):
                g = group(p)
                n = turn_at["x", p] + i
                dve.wait_ge(t_ready[n % 2], n // 2 + 1)
                for c in range(2):
                    k = 2 * i + c
                    last = dve.tensor_scalar(h_t[:, (p + 1) % 2, k, :], bank(n % 2)[:, 256 * c:256 * (c + 1)], a1[:, k, g:g + 1],
                                             mod[:, SHIFT1 + k, g:g + 1], ALU.mult, ALU.add)
                last.then_inc(t_free[n % 2], 1)

            def low_out(p, a, i):
                t = 2 * p + a
                n = turn_at["q", p, a] + i
                dve.wait_ge(high_ready, 3 * t + i + 1)
                if i < 2:
                    src = bank(n % 2)[0:HD, :].rearrange("d (h q) -> d h q", h=4)
                    last = dve.tensor_tensor(q_st[HD:P, t, 4 * i:4 * i + 4, :], src,
                                             q_st[0:HD, t, 4 * i:4 * i + 4, :].bitcast(F32), ALU.subtract)
                else:
                    src = bank(n % 2)[0:HD, 0:NKV * P].rearrange("d (j q) -> d j q", j=NKV)
                    for lo in (0, HD):
                        last = dve.tensor_tensor(k_lo[lo:lo + HD, :, P * t:P * (t + 1)], src,
                                                 k_hi[0:HD, :, P * t:P * (t + 1)].bitcast(F32), ALU.subtract)
                last.then_inc(t_free[n % 2], 1)

            def qk_norm(q):
                a = q % 2
                dve.wait_ge(sq_ready, q + 1)
                dve.tensor_reduce(ss_q[:, a, :], sq[:, :, :], AX.X, ALU.add).then_inc(sq_summed, 1)
                dve.wait_ge(q_root, q + 1)
                dve.reciprocal(rs_q[:, a, :], rt_q[:, a, :]).then_inc(q_recip, 1)
                dve.wait_ge(q_recip, q + 1)
                dve.tensor_tensor(qk[a][:, :, :], qk[a][:, :, :], rs_q[:, a, :].unsqueeze(2).to_broadcast([P, 10, HD]),
                                  ALU.mult).then_inc(q_normed, 1)
                dve.wait_ge(q_normed, q + 1)
                for g, h0, nh in ((0, 0, NH), (1, NH, NKV)):
                    tab = rope_c[:, q % 8, g:g + 1, :].to_broadcast([P, nh, HD])
                    dve.tensor_tensor(rot1[:, h0:h0 + nh, :], qk[a][:, h0:h0 + nh, :], tab, ALU.mult).then_inc(rot1_ready, 1)
                dve.wait_ge(rot1_ready, 2 * q + 2)
                dve.wait_ge(rot2_ready, q + 1)
                dve.tensor_tensor(qk[a][:, :, :], rot1[:, :, :], rot2[:, :, :], ALU.add).then_inc(rotated, 1)

            def gate_u(p, i):
                n = CC * p + i
                dve.wait_ge(sig_ready, n + 1)
                dve.tensor_tensor(a_t[:, i, a_cols(p):a_cols(p) + 2 * P], bank(2 + n % 2)[:, 0:256], sig[:, n % 2, :],
                                  ALU.mult).then_inc(u_gated, 1)

            def tap(s, c, k):
                o, n = SPANS[s]
                if isinstance(k, int) and k == 0:
                    dve.tensor_scalar(c_t[s][:, c, :], a_t[:, c, o:o + n], taps[:, c, 0:1], cols[:, ROW_CB + c:ROW_CB + c + 1],
                                      ALU.mult, ALU.add).then_inc(conv_done[s][c], 1)
                else:
                    dve.wait_ge(conv_done[s][c], k)
                    dve.scalar_tensor_tensor(out=c_t[s][:, c, :], in0=a_t[:, c, bass.ds(k + o, n)], scalar=taps[:, c, bass.ds(k, 1)],
                                             in1=c_t[s][:, c, :], op0=ALU.mult, op1=ALU.add).then_inc(conv_done[s][c], 1)

            def some_taps(s, first, last):
                for i in range(first, last):
                    tap(s, i % CC, i // CC)

            BESIDE = 40

            def beside(p, first, last):
                if p >= NPAIR - 2:
                    o = BESIDE * (p - NPAIR + 2)
                    some_taps(0, o + first, o + last)

            x_out(0, 1)
            x_out(0, 3)
            for p in range(NPAIR):
                if p + 1 < NPAIR:
                    norm_x(p + 1)
                if p == NPAIR - 2:
                    dve.wait_ge(x_squared, NT)
                    dve.wait_ge(fills_made, 6)
                gate_u(p, 0)
                beside(p, 0, 4)
                if p:
                    low_out(p - 1, 0, 0)
                    low_out(p - 1, 0, 1)
                beside(p, 4, 6)
                gate_u(p, 1)
                if p:
                    low_out(p - 1, 0, 2)
                beside(p, 6, 10)
                if p:
                    low_out(p - 1, 1, 0)
                    low_out(p - 1, 1, 1)
                beside(p, 10, 12)
                gate_u(p, 2)
                if p:
                    low_out(p - 1, 1, 2)
                beside(p, 12, 16)
                if p + 1 < NPAIR:
                    x_out(p + 1, 1)
                beside(p, 16, 20)
                gate_u(p, 3)
                if p + 1 < NPAIR:
                    x_out(p + 1, 3)
                beside(p, 20, 35)
                qk_norm(2 * p)
                beside(p, 35, BESIDE)
                qk_norm(2 * p + 1)
            for a in range(2):
                for i in range(3):
                    low_out(NPAIR - 1, a, i)

            def centre(s):
                dve.wait_ge(mean_ready, s + 1)
                for c in range(CC):
                    dve.scalar_tensor_tensor(out=c_t[s][:, c, :], in0=bank(MEAN_BANK[s])[:, 0:SPANS[s][1]], scalar=-1.0 / DC,
                                             in1=c_t[s][:, c, :], op0=ALU.mult, op1=ALU.add).then_inc(centred, 1)

            def scale_span(s):
                n = SPANS[s][1]
                dve.wait_ge(root_ready, s + 1)
                if s == 2:
                    dve.wait_ge(scaled, CC * s)
                rs = rs_c[min(s, 1)]
                dve.reciprocal(rs[:, 0:n], rt_c[s][:, :]).then_inc(inv_ready, 1)
                dve.wait_ge(inv_ready, s + 1)
                dve.wait_ge(squared, CC * (s + 1))
                for c in range(CC):
                    dve.tensor_tensor(c_t[s][:, c, :], c_t[s][:, c, :], rs[:, 0:n], ALU.mult).then_inc(scaled, 1)

            dve.wait_ge(u_gated, CC * NPAIR)
            dve.wait_ge(rotated, NT)
            n = n_turns[0] - 1
            dve.wait_ge(t_ready[n % 2], n // 2 + 1)
            def gate_diag(n):
                for i in range(4):
                    k = GATE1 + 4 * (n % 2) + i
                    dve.tensor_scalar(diag[n // 2][:, n % 2, i, :], ident[:, :], mod[:, k, n // 2:n // 2 + 1], None, ALU.mult).then_inc(diag_ready, 1)

            some_taps(0, 2 * BESIDE, 100)
            dve.wait_ge(rows_turned, ADA_FIRST + 2)
            mod_cols(GATE1, SHIFT2)
            dve.wait_ge(mod_ready, 2)
            for n in range(4):
                gate_diag(n)
            some_taps(0, 100, CC * TAPS)
            centre(0)
            dve.wait_ge(gate_rows_ready, 4)
            dve.wait_ge(rows_turned, ADA_LATE)
            mod_cols(SHIFT2, GATE2)
            dve.wait_ge(mod_ready, 3)
            scale_of(a2, ROW_NFFN, SCALE2)

            def maximum(n, h, nk):
                dve.wait_ge(scores_ready, n + 1)
                dve.tensor_reduce(negmax[:, h:h + 1], two[h % 2][:, :, :].rearrange("p b n -> p (b n)")[:, 0:P * nk], AX.X,
                                  ALU.max, negate=True).then_inc(max_ready, 1)

            def low_weights(k):
                dve.wait_ge(w_hi_ready, k + 1)
                dve.tensor_tensor(w_lo[:, k, :], w_out_sb[:, k, :], w_hi[:, k, :].bitcast(F32), ALU.subtract).then_inc(w_lo_ready, 1)

            def tile_low(q):
                dve.wait_ge(s_hi_ready, q + 1)
                attn, conv = tile_parts(mix_t, c_t, q)
                attn_lo, conv_lo = tile_parts(mix_lo, c_lo, q)
                dve.tensor_tensor(attn_lo, attn, s_hi[:, q % 2, 0:CC, :].bitcast(F32), ALU.subtract)
                dve.tensor_tensor(conv_lo, conv, s_hi[:, q % 2, CC:KC, :].bitcast(F32), ALU.subtract).then_inc(s_lo_ready, 1)

            def divide(step):
                dve.wait_ge(weighed, step * QPK + 2 * QPK)
                o = bank(6)[:, 0:QPK * (HD + 1)].rearrange("q (h d) -> q h d", h=QPK)
                dve.reciprocal(rsum[:, :, :], o[:, :, HD:HD + 1]).then_inc(sums_inverted, 1)
                dve.wait_ge(sums_inverted, step + 1)
                dve.tensor_tensor(out_rows[:, :, :], o[:, :, 0:HD], rsum[:, :, :].to_broadcast([P, QPK, HD]), ALU.mult).then_inc(out_divided, 1)

            maximum(0, 0, phases[0][2])
            maximum(1, 1, phases[0][2])
            scale_span(0)
            for i, (j, t0, nt, s0) in enumerate(phases):
                def between(l, first, last):
                    n = (l + s0) * QPK
                    nxt_nk = nt if not last else phases[i + 1][2] if i + 1 < len(phases) else None

                    def chunks(s, k):
                        for c in range(CC):
                            tap(s, c, k)

                    def step_taps(m):
                        if t0:
                            return
                        k = STEP_TAPS * l + STEP_TAPS * PROMPT_TILES * j
                        full = not (last and j == NKV - 1)
                        if m == 0:
                            chunks(1, k)
                        elif m == 1:
                            chunks(2, k)
                            if full:
                                chunks(2, k + 1)
                        elif full:
                            chunks(1, k + 1)
                    maximum(n + 2, 2, nt)
                    if not (first and i == 0):
                        divide(l + (s0 - 1))
                    step_taps(0)
                    maximum(n + 3, 3, nt)
                    step_taps(1)
                    if nxt_nk is not None:
                        maximum(n + 4, 0, nxt_nk)
                    step_taps(2)
                    if nxt_nk is not None:
                        maximum(n + 5, 1, nxt_nk)
                if t0 == 0:
                    steps_of(dve, nt, between)
                elif j == 0:
                    between(0, True, False)
                    for k in range(3):
                        low_weights(k)
                    centre(1)
                    between(1, False, True)
                    for k in range(3, 6):
                        low_weights(k)
                    centre(2)
                else:
                    between(0, True, False)
                    low_weights(6)
                    low_weights(7)
                    between(1, False, True)
            divide(STEPS - 1)
            tile_low(0)
            tile_low(1)

            def gate_mix(q):
                a = q % 2
                dve.wait_ge(mix_ready, q + 1)
                if q >= 2:
                    dve.wait_ge(y_stored[a], 16 * (q // 2))
                    dve.wait_ge(xn2_ready, q - 1)
                g = group(q // 2)
                dve.tensor_tensor(x1[:, a, :], two[a][:, :, :].rearrange("p b n -> p (b n)"), gate1_row[:, g, :], ALU.mult).then_inc(mix_gated, 1)

            def norm_x1(q):
                a = q % 2
                dve.wait_ge(x1_root, q + 1)
                dve.reciprocal(rs_x[:, 0:1], rt_x[:, 0:1]).then_inc(x1_recip, 1)
                dve.wait_ge(x1_recip, q + 1)
                dve.tensor_scalar(xn2[:, a, :], x1[:, a, :], rs_x[:, 0:1], None, ALU.mult).then_inc(xn2_ready, 1)

            def h2_out(p):
                g = group(p)
                if p:
                    dve.wait_ge(logits_ready, p)
                for i in range(1, 4, 2):
                    n = 4 * p + i
                    dve.wait_ge(t2_ready[n % 2], n // 2 + 1)
                    for c in range(2):
                        k = 2 * i + c
                        last = dve.tensor_scalar(h2_t[:, k, :], bank(4 + n % 2)[:, 256 * c:256 * (c + 1)], a2[:, k, g:g + 1],
                                                 mod[:, SHIFT2 + k, g:g + 1], ALU.mult, ALU.add)
                    last.then_inc(t2_free[n % 2], 1)

            scale_span(1)
            scale_span(2)
            dve.wait_ge(gate_rows_copied, 4)
            dve.wait_ge(scale_ready, 2)
            gate_mix(0)
            tile_low(2)
            norm_x1(0)
            gate_mix(1)
            tile_low(3)
            norm_x1(1)
            for p in range(1, NPAIR - 1):
                gate_mix(2 * p)
                h2_out(p - 1)
                tile_low(2 * p + 2)
                norm_x1(2 * p)
                gate_mix(2 * p + 1)
                tile_low(2 * p + 3)
                norm_x1(2 * p + 1)
            h2_out(NPAIR - 2)

            def shift_logits(g, lg, v, m):
                dve.wait_ge(logits_turned, g + 1)
                dve.tensor_reduce(m, lg, AX.X, ALU.max).then_inc(router_max, 1)
                dve.wait_ge(router_max, g + 1)
                dve.tensor_tensor(v, lg, m.unsqueeze(len(m.shape)).to_broadcast(list(v.shape)), ALU.subtract).then_inc(router_shifted, 1)

            def affinities(g, v, m, inv):
                dve.wait_ge(router_exp, g + 1)
                dve.tensor_reduce(m, v, AX.X, ALU.add).then_inc(router_sum, 1)
                dve.wait_ge(router_sum, g + 1)
                dve.reciprocal(inv, m).then_inc(router_inv, 1)
                dve.wait_ge(router_inv, g + 1)
                dve.tensor_tensor(v, v, inv.unsqueeze(len(inv.shape)).to_broadcast(list(v.shape)), ALU.mult).then_inc(aff_ready, 1)

            def top_eight(vals, top, idx, r, step):
                if r:
                    dve.wait_ge(step, 3 * r)
                dve.max(top[:, 0, 8 * r:8 * r + 8], vals[:, :]).then_inc(step, 1)
                dve.wait_ge(step, 3 * r + 1)
                dve.max_index(idx[:, 8 * r:8 * r + 8], top[:, 0, 8 * r:8 * r + 8], vals[:, :]).then_inc(step, 1)
                dve.wait_ge(step, 3 * r + 2)
                dve.match_replace(vals[:, :], top[:, 0, 8 * r:8 * r + 8], vals[:, :], LOWEST).then_inc(step, 1)

            TP = SP_TOK // P
            prompt_rows = [smx[:, i, 0:TP].rearrange("p (s h) -> p s h", h=2) for i in range(3)]
            sample_rows = [smx[:, i, TP:NT] for i in range(3)]
            prompt_aff, sample_aff = aff_h[:, :, 0:3:2, :], aff_r[:, :, :]
            shift_logits(0, bank(7)[:, 0:NE * TP].rearrange("p (s h e) -> p s h e", h=2, e=NE), prompt_aff, prompt_rows[0])
            affinities(0, prompt_aff, prompt_rows[1], prompt_rows[2])
            dve.wait_ge(aff_turned, 1)
            dve.tensor_copy(aff_p[:, :], bank(4)[0:RANKED, :]).then_inc(aff_copied, 1)
            dve.wait_ge(aff_copied, 1)
            for r in range(CAP_P // 8):
                top_eight(aff_p, top_p, idx_p, r, top_p_step)
                if r == 3:
                    gate_mix(2 * NPAIR - 2)
                if r == 5:
                    norm_x1(2 * NPAIR - 2)
                if r == 6:
                    gate_mix(2 * NPAIR - 1)
                if r == 8:
                    norm_x1(2 * NPAIR - 1)
                if r == 10:
                    h2_out(NPAIR - 1)
                if r == 12:
                    shift_logits(1, bank(7)[:, NE * TP:NE * NT].rearrange("p (t e) -> p t e", e=NE), sample_aff, sample_rows[0])
                if r == 13:
                    affinities(1, sample_aff, sample_rows[1], sample_rows[2])
                if r == 14:
                    dve.wait_ge(aff_turned, 2)
                    dve.tensor_copy(aff_s[:, :], bank(7)[0:NE, 256:256 + SS_TOK]).then_inc(aff_copied, 1)
                    dve.wait_ge(aff_copied, 2)
                    top_eight(aff_s, top_s, idx_s, 0, top_s_step)
                if r == 15:
                    top_eight(aff_s, top_s, idx_s, 1, top_s_step)
            for r in range(2, CAP_S // 8):
                top_eight(aff_s, top_s, idx_s, r, top_s_step)
            dve.wait_ge(rows_turned, ADA_BLOCKS)
            mod_cols(GATE2, 6 * KC, 1)
            dve.wait_ge(top_p_step, 3 * CAP_P // 8)
            dve.wait_ge(top_s_step, 3 * CAP_S // 8)
            dve.tensor_copy(top_p[:, 1, :], idx_p[:, :]).then_inc(top_float, 2)
            dve.tensor_copy(top_s[:, 1, :], idx_s[:, :]).then_inc(top_float, 2)
            dve.wait_ge(top_turned, 1)
            dve.tensor_copy(top_sb[:, :, :], bank(0)[:, 0:2 * RANKED].rearrange("p (i e) -> p i e", i=2)).then_inc(top_copied, 1)
            dve.tensor_copy(g_top_s[0:CAP_S, 0:NE], bank(0)[0:CAP_S, 2 * RANKED:2 * RANKED + NE]).then_inc(top_ready, 1)
            dve.tensor_copy(i_top_s[0:CAP_S, 0:NE], bank(0)[0:CAP_S, 2 * RANKED + NE:2 * RANKED + 2 * NE]).then_inc(top_ready, 1)
            dve.wait_ge(top_copied, 1)
            dve.wait_ge(top_flipped, 1)
            second = bank(4)[:, 0:2 * NE].rearrange("p (i e) -> p i e", i=2)
            dve.tensor_tensor(from_low[:, :], top_sb[:, 0, 0:NE], second[:, 0, :], ALU.is_ge).then_inc(idx_chosen, 1)
            dve.scalar_tensor_tensor(out=idx_step[:, :], in0=top_sb[:, 1, 0:NE], scalar=float(-HALF), in1=second[:, 1, :],
                                     op0=ALU.add, op1=ALU.subtract).then_inc(idx_chosen, 1)
            dve.tensor_tensor(g_top_p[:, 0:NE], top_sb[:, 0, 0:NE], second[:, 0, :], ALU.max).then_inc(top_ready, 1)
            dve.wait_ge(idx_chosen, 2)
            dve.tensor_tensor(idx_step[:, :], idx_step[:, :], from_low[:, :], ALU.mult).then_inc(idx_chosen, 1)
            dve.wait_ge(idx_chosen, 3)
            dve.scalar_tensor_tensor(out=i_top_p[:, 0:NE], in0=second[:, 1, :], scalar=float(HALF), in1=idx_step[:, :],
                                     op0=ALU.add, op1=ALU.add).then_inc(top_ready, 1)

            def token_out(e, k):
                dve.wait_ge(x_turned, KC * e + k + 1)
                b = bank(k % 2)
                dve.tensor_scalar(xe_t[:, k, 0:CAP_P], b[:, 0:CAP_P], a2[:, k, 0:1], mod[:, SHIFT2 + k, 0:1], ALU.mult, ALU.add)
                dve.tensor_scalar(xe_t[:, k, CAP_P:CAP], b[:, CAP_P:CAP], a2[:, k, 1:2], mod[:, SHIFT2 + k, 1:2],
                                  ALU.mult, ALU.add).then_inc(x_scaled, 1)

            def expert(e, more):
                for m in range(KC):
                    dve.wait_ge(silu_done, KC * e + m + 1)
                    dve.wait_ge(up_ready, KC * e + m + 1)
                    dve.tensor_tensor(hid[:, m, :], sil[:, m % 2, :], bank(2 + m % 2)[:, 0:CAP], ALU.mult).then_inc(hid_ready, 1)
                for m in range(KC):
                    dve.wait_ge(down_ready, KC * e + m + 1)
                    b = bank(4 + m % 2)
                    dve.tensor_scalar(y_t[:, m, 0:CAP_P], b[:, 0:CAP_P], mod[:, GATE2 + m, 0:1], None, ALU.mult)
                    dve.tensor_scalar(y_t[:, m, CAP_P:CAP], b[:, CAP_P:CAP], mod[:, GATE2 + m, 1:2], None, ALU.mult).then_inc(y_scaled, 1)
                    if more:
                        token_out(e + 1, m)

            dve.sem_inc(hid_ready, 2)
            dve.sem_inc(y_scaled, 2)
            for k in range(KC):
                token_out(0, k)
            with dve.Fori(0, NE - 1) as e:
                expert(e, True)
            expert(NE - 1, False)


def rope_tables():
    pos = np.arange(SP_TOK)
    inv = (10000.0 ** (-np.arange(0, HD // 2, 2, dtype=np.float32) / np.float32(HD // 2))).astype(np.float32)
    row = (pos // 64).astype(np.float32)
    col = (pos % 64).astype(np.float32)
    ang = np.concatenate([row[:, None] * inv, col[:, None] * inv], axis=-1)
    return np.cos(ang).astype(np.float32), np.sin(ang).astype(np.float32)


_INS = ["x_prompt", "x_sample", "c_prompt", "c_sample", "ada_w", "ada_b", "norm_mix", "w_in", "q_norm", "k_norm",
        "conv_w", "conv_b", "conv_ln_g", "conv_ln_b", "w_out", "norm_ffn", "w_router", "w_gate", "w_up", "w_down"]


def kernel(**inputs):
    import concourse.bacc as bacc
    from concourse.bass_utils import run_bass_kernel_spmd

    nc = bacc.Bacc("TRN2", target_bir_lowering=False, num_devices=1)
    arrays, args = {}, []
    for name in _INS:
        arrays[f"in_{name}"] = np.ascontiguousarray(inputs[name])
    arrays["in_rope_cos"], arrays["in_rope_sin"] = rope_tables()
    for name, a in arrays.items():
        args.append(nc.dram_tensor(name, a.shape, mybir.dt.from_np(a.dtype), kind="ExternalInput").ap())
    for name, shape in (("out_prompt", (1, SP_TOK, D)), ("out_sample", (1, SS_TOK, D))):
        args.append(nc.dram_tensor(name, shape, F32, kind="ExternalOutput").ap())
    encoder_layer(nc, *args)
    r = run_bass_kernel_spmd(nc, [arrays], core_ids=[0])
    return r.results[0]["out_prompt"], r.results[0]["out_sample"]
```
